# Optimizing a Trainium2 kernel written in Bass

```python
import math
import jax, jax.numpy as jnp
from jax import lax
import numpy as np

D_MODEL = 1024
BATCH = 1
SEQ = 256
DEPTH = 1

BLOCK = 128
A_GROUPS = 4
A_GROUP_DIM = 128
A_WIDTH = A_GROUPS * A_GROUP_DIM
B_HEADS = 4
B_QK_DIM = 64
B_V_DIM = 2 * B_QK_DIM
B_QK_WIDTH = B_HEADS * 2 * B_QK_DIM
B_WIDTH = B_HEADS * B_V_DIM
C_HEADS = 8
C_HEAD_DIM = 64
C_WIDTH = C_HEADS * C_HEAD_DIM
N_BRANCHES = 3
GATE_WIDTH = N_BRANCHES * D_MODEL
IN_SPLITS = (A_WIDTH, A_WIDTH, B_QK_WIDTH, B_QK_WIDTH, B_WIDTH, C_WIDTH, C_WIDTH, C_WIDTH, GATE_WIDTH)
IN_WIDTH = 2 * A_WIDTH + 2 * B_QK_WIDTH + B_WIDTH + 3 * C_WIDTH + GATE_WIDTH
N_EXPERTS = 16
N_GROUPS = 4
EXPERTS_PER_GROUP = N_EXPERTS // N_GROUPS
TOP_K = 2
D_FF_EXPERT = 512
EPS = 1e-6

kernel_name = "hybrid_gated_gmlp_diffattn_stickbreak_groupmoe"

def rms_norm(x, g):
    xf = x.astype(jnp.float32)
    y = xf * lax.rsqrt(jnp.mean(xf * xf, axis=-1, keepdims=True) + EPS)
    return (y * g.astype(jnp.float32)).astype(x.dtype)

def alibi_slopes(n):
    start = 2.0 ** (-8.0 / n)
    return jnp.asarray([start ** (i + 1) for i in range(n)], dtype=jnp.float32)

def chunked_spatial_gating(u, v, w_s, b_s, g_v):
    bsz, seq, _ = u.shape
    u = jax.nn.gelu(u)
    v = rms_norm(jax.nn.gelu(v), g_v)
    vc = v.reshape(bsz, seq // BLOCK, BLOCK, A_GROUPS, A_GROUP_DIM)
    causal = jnp.tril(jnp.ones((BLOCK, BLOCK), dtype=bool))
    w = jnp.where(causal[None], w_s, 0).astype(v.dtype)
    mixed = jnp.einsum('gts,bcsgd->bctgd', w, vc) + b_s.T.astype(v.dtype)[None, None, :, :, None]
    return u * mixed.reshape(bsz, seq, A_WIDTH)

def diff_attention(q, k, v, lam, slopes):
    bsz, seq = q.shape[:2]
    nb = seq // BLOCK
    scale = B_QK_DIM ** -0.5
    qb = jnp.moveaxis(q.reshape(bsz, nb, BLOCK, B_HEADS, 2, B_QK_DIM), 1, 0)
    key_pos = jnp.arange(seq)

    def one_block(args):
        qblk, i = args
        q_pos = i * BLOCK + jnp.arange(BLOCK)
        dist = (q_pos[:, None] - key_pos[None, :]).astype(jnp.float32)
        s = jnp.einsum('bqhmd,bkhmd->bhmqk', qblk, k).astype(jnp.float32) * scale
        s = s - slopes[None, :, None, None, None] * dist
        s = jnp.where(dist >= 0, s, -jnp.inf)
        p = jax.nn.softmax(s, axis=-1)
        a = p[:, :, 0] - lam * p[:, :, 1]
        return jnp.einsum('bhqk,bkhe->bqhe', a.astype(v.dtype), v)

    out = lax.map(one_block, (qb, jnp.arange(nb)))
    return jnp.moveaxis(out, 0, 1).reshape(bsz, seq, B_HEADS, B_V_DIM)

def stick_breaking_attention(q, k, v):
    bsz, seq = q.shape[:2]
    nb = seq // BLOCK
    scale = C_HEAD_DIM ** -0.5
    qb = jnp.moveaxis(q.reshape(bsz, nb, BLOCK, C_HEADS, C_HEAD_DIM), 1, 0)
    key_pos = jnp.arange(seq)

    def one_block(args):
        qblk, i = args
        q_pos = i * BLOCK + jnp.arange(BLOCK)
        strict = q_pos[:, None] > key_pos[None, :]
        z = jnp.einsum('bqhd,bkhd->bhqk', qblk, k).astype(jnp.float32) * scale
        log_beta = jax.nn.log_sigmoid(z)
        log_keep = jnp.where(strict, log_beta - z, 0.0)
        after = lax.cumsum(log_keep, axis=3, reverse=True) - log_keep
        a = jnp.where(strict, jnp.exp(log_beta + after), 0.0)
        return jnp.einsum('bhqk,bkhd->bqhd', a.astype(v.dtype), v)

    out = lax.map(one_block, (qb, jnp.arange(nb)))
    return jnp.moveaxis(out, 0, 1).reshape(bsz, seq, C_WIDTH)

def hybrid_mixer(xn, w_in, w_s, b_s, g_v, diff_lambda, subln_g, w_up_a, w_up_b, w_up_c, w_out, lambda_init):
    bsz, seq, _ = xn.shape
    proj = xn @ w_in
    points, acc = [], 0
    for width in IN_SPLITS[:-1]:
        acc += width
        points.append(acc)
    ua, va, qb, kb, vb, qc, kc, vc, gl = jnp.split(proj, points, axis=-1)

    y_a = chunked_spatial_gating(ua, va, w_s, b_s, g_v)

    lamp = diff_lambda.astype(jnp.float32)
    lam = jnp.exp(jnp.sum(lamp[0] * lamp[1])) - jnp.exp(jnp.sum(lamp[2] * lamp[3])) + lambda_init
    o_b = diff_attention(qb.reshape(bsz, seq, B_HEADS, 2, B_QK_DIM),
                         kb.reshape(bsz, seq, B_HEADS, 2, B_QK_DIM),
                         vb.reshape(bsz, seq, B_HEADS, B_V_DIM),
                         lam, alibi_slopes(B_HEADS))
    y_b = (rms_norm(o_b, subln_g) * (1.0 - lambda_init)).reshape(bsz, seq, B_WIDTH)

    y_c = stick_breaking_attention(qc.reshape(bsz, seq, C_HEADS, C_HEAD_DIM),
                                   kc.reshape(bsz, seq, C_HEADS, C_HEAD_DIM),
                                   vc.reshape(bsz, seq, C_HEADS, C_HEAD_DIM))

    g = jax.nn.sigmoid(gl.reshape(bsz, seq, N_BRANCHES, D_MODEL))
    merged = g[:, :, 0] * (y_a @ w_up_a) + g[:, :, 1] * (y_b @ w_up_b) + g[:, :, 2] * (y_c @ w_up_c)
    return merged @ w_out

def grouped_moe(xn, router_w, router_bias, w1, w3, w2):
    bsz, seq, d = xn.shape
    xt = xn.reshape(-1, d)
    aff = jax.nn.sigmoid((xt @ router_w).astype(jnp.float32))
    sel = aff + router_bias.astype(jnp.float32)
    grouped = sel.reshape(-1, N_GROUPS, EXPERTS_PER_GROUP)
    group_score = lax.top_k(grouped, TOP_K)[0].sum(-1)
    best = jnp.argmax(group_score, axis=-1)
    cand = jnp.take_along_axis(grouped, best[:, None, None], axis=1)[:, 0]
    _, local = lax.top_k(cand, TOP_K)
    idx = best[:, None] * EXPERTS_PER_GROUP + local
    w = jnp.take_along_axis(aff, idx, axis=1)
    w = w / jnp.sum(w, axis=-1, keepdims=True)
    gate = jnp.sum(jax.nn.one_hot(idx, N_EXPERTS, dtype=jnp.float32) * w[..., None], axis=1)
    h = jax.nn.silu(jnp.einsum('td,edf->tef', xt, w1)) * jnp.einsum('td,edf->tef', xt, w3)
    h = h * gate[:, :, None].astype(h.dtype)
    y = jnp.einsum('tef,efd->td', h, w2)
    return y.reshape(bsz, seq, d)

def setup_inputs(seed: int = 0) -> dict:
    key = jax.random.key(seed)
    ks = jax.random.split(key, 20)
    f32 = jnp.float32
    resid = (2 * DEPTH) ** -0.5
    nrm = lambda k, shape, s: jax.random.normal(k, shape, dtype=f32) * s
    return {
        "x": nrm(ks[0], (BATCH, SEQ, D_MODEL), 1.0),
        "norm_mix_gain": 1.0 + nrm(ks[1], (DEPTH, D_MODEL), 0.02),
        "w_in": nrm(ks[2], (DEPTH, D_MODEL, IN_WIDTH), D_MODEL ** -0.5),
        "gmlp_w_s": nrm(ks[3], (DEPTH, A_GROUPS, BLOCK, BLOCK), BLOCK ** -0.5),
        "gmlp_b_s": 1.0 + nrm(ks[4], (DEPTH, A_GROUPS, BLOCK), 0.02),
        "gmlp_v_gain": 1.0 + nrm(ks[5], (DEPTH, A_WIDTH), 0.02),
        "diff_lambda": nrm(ks[6], (DEPTH, 4, B_QK_DIM), 0.1),
        "diff_subln_gain": 1.0 + nrm(ks[7], (DEPTH, B_V_DIM), 0.02),
        "w_up_a": nrm(ks[8], (DEPTH, A_WIDTH, D_MODEL), A_WIDTH ** -0.5),
        "w_up_b": nrm(ks[9], (DEPTH, B_WIDTH, D_MODEL), B_WIDTH ** -0.5),
        "w_up_c": nrm(ks[10], (DEPTH, C_WIDTH, D_MODEL), C_WIDTH ** -0.5),
        "w_out": nrm(ks[11], (DEPTH, D_MODEL, D_MODEL), D_MODEL ** -0.5 * resid),
        "norm_ffn_gain": 1.0 + nrm(ks[12], (DEPTH, D_MODEL), 0.02),
        "router_w": nrm(ks[13], (D_MODEL, N_EXPERTS), D_MODEL ** -0.5),
        "router_bias": nrm(ks[14], (N_EXPERTS,), 0.01),
        "moe_w1": nrm(ks[15], (DEPTH, N_EXPERTS, D_MODEL, D_FF_EXPERT), D_MODEL ** -0.5),
        "moe_w3": nrm(ks[16], (DEPTH, N_EXPERTS, D_MODEL, D_FF_EXPERT), D_MODEL ** -0.5),
        "moe_w2": nrm(ks[17], (DEPTH, N_EXPERTS, D_FF_EXPERT, D_MODEL), D_FF_EXPERT ** -0.5 * resid),
        "final_gain": 1.0 + nrm(ks[18], (D_MODEL,), 0.02),
    }

def reference(x, norm_mix_gain, w_in, gmlp_w_s, gmlp_b_s, gmlp_v_gain, diff_lambda, diff_subln_gain,
              w_up_a, w_up_b, w_up_c, w_out, norm_ffn_gain, router_w, router_bias,
              moe_w1, moe_w3, moe_w2, final_gain):
    for l in range(DEPTH):
        lambda_init = 0.8 - 0.6 * math.exp(-0.3 * l)
        h = x + hybrid_mixer(rms_norm(x, norm_mix_gain[l]), w_in[l], gmlp_w_s[l], gmlp_b_s[l], gmlp_v_gain[l],
                             diff_lambda[l], diff_subln_gain[l], w_up_a[l], w_up_b[l], w_up_c[l], w_out[l],
                             lambda_init)
        x = h + grouped_moe(rms_norm(h, norm_ffn_gain[l]), router_w, router_bias,
                            moe_w1[l], moe_w3[l], moe_w2[l])
    return rms_norm(x, final_gain)


_drawn_inputs = setup_inputs


def setup_inputs(seed=0):
    import zlib

    import numpy as np

    out = dict(_drawn_inputs(seed))
    spreads = {}
    factors = {'norm_mix_gain': 2.781,
     'gmlp_b_s': 19.294,
     'gmlp_v_gain': 27.903,
     'final_gain': 24.51,
     'diff_lambda': 5.671,
     'diff_subln_gain': 64.0,
     'norm_ffn_gain': 8.0,
     'router_bias': 4.012}
    for name, (base, spread) in spreads.items():
        noise = np.random.default_rng([zlib.crc32(name.encode()), seed]).standard_normal(out[name].shape)
        drawn = base * np.exp(spread * noise) if base else spread * noise
        out[name] = __import__('jax').numpy.asarray(drawn.astype(out[name].dtype))
    for name, factor in factors.items():
        out[name] = (out[name] * factor).astype(out[name].dtype)
    return out
```

```python
from contextlib import ExitStack

import concourse.bass as bass
import concourse.mybir as mybir

F32 = mybir.dt.float32
BF16 = mybir.dt.bfloat16
I32 = mybir.dt.int32
ALU = mybir.AluOpType
ACT = mybir.ActivationFunctionType
AX = mybir.AxisListType

P = 128
EPS = 1e-6
LAMBDA_INIT = 0.8 - 0.6
MASKED = -1e30


def trunk(nc, x, norm_mix_gain, w_in, gmlp_w_s, gmlp_b_s, gmlp_v_gain, diff_lambda, diff_subln_gain,
          w_up_a, w_up_b, w_up_c, w_out, norm_ffn_gain, router_w, router_bias,
          moe_w1, moe_w3, moe_w2, final_gain, out):
    T, D = x.shape[1], x.shape[2]
    TT, KD = T // P, D // P
    NG = gmlp_w_s.shape[1]
    AW = NG * P
    BH, BQ = 4, 64
    CH, CD = 8, 64
    E = router_w.shape[1]
    EG = 4
    NGR = E // EG
    F = moe_w1.shape[3]
    KF = F // P
    PAIRS = E // 2
    J = 64
    W3 = 3 * P
    B_SCALE, C_SCALE = BQ ** -0.5, CD ** -0.5
    SLOPES = [(2.0 ** (-8.0 / BH)) ** (i + 1) for i in range(BH)]

    RING = 6
    CW = 512
    UA, VA, QB, KB, VB, QC, KC, VC = range(8)
    PROJ = [QB, KB, VB, QC, KC, VC, VA, UA]
    BRANCHES = [("B", 10, w_up_b), ("C", 12, w_up_c), ("A", 8, w_up_a)]
    w_in_v = w_in[0].rearrange("(k p) n -> p k n", p=P)
    w_out_v = w_out[0].rearrange("(k p) n -> p k n", p=P)
    chunks = [w_in_v[:, :, c * CW:(c + 1) * CW] for c in PROJ]
    gate_chunk, up_chunk = {}, {}
    for name, c0, up in BRANCHES:
        gate_chunk[name] = (len(chunks), len(chunks) + 2)
        up_chunk[name] = len(chunks) + 1
        chunks += [w_in_v[:, :, c0 * CW:(c0 + 1) * CW], up[0].rearrange("(k p) n -> p k n", p=P),
                   w_in_v[:, :, (c0 + 1) * CW:(c0 + 2) * CW]]
    out_chunk = len(chunks)
    chunks += [w_out_v[:, :, n * CW:(n + 1) * CW] for n in range(D // CW)]
    NC = len(chunks)
    assert RING == 6 and D // CW == 2 and F == CW

    TIMELINE = [("proj", (0, 0)), ("proj", (0, 1)), ("proj", (1, 0)), ("proj", (1, 1)), ("b_scores", 0),
                ("proj", (2, 0)), ("b_combine", 0), ("proj", (2, 1))]
    for h in range(BH - 1):
        TIMELINE += [("b_turn", h), ("b_scores", h + 1), ("proj", (3 + h, 0)), ("b_values", h),
                     ("b_combine", h + 1), ("proj", (3 + h, 1))]
    TIMELINE += [("b_turn", BH - 1), ("c_scores", 0), ("c_scores", 1), ("proj", (6, 0)), ("b_values", BH - 1),
                 ("b_norm", 0), ("c_keep", 0), ("c_keep", 1), ("c_sums", 0), ("c_sums", 1),
                 ("c_scores", 2), ("c_scores", 3), ("proj", (6, 1)), ("b_done", 0)]
    for q in range(3):
        TIMELINE += [("c_logits", 2 * q), ("c_logits", 2 * q + 1), ("c_keep", 2 * q + 2), ("c_keep", 2 * q + 3),
                     ("c_values", 2 * q), ("c_values", 2 * q + 1), ("c_sums", 2 * q + 2), ("c_sums", 2 * q + 3)]
        if q < 2:
            TIMELINE += [("c_scores", 2 * q + 4), ("c_scores", 2 * q + 5), ("proj", (7, q))]
    TIMELINE += [("c_logits", 6), ("c_logits", 7), ("a_gelu", 0), ("gate", (0, 0)), ("c_values", 6), ("c_values", 7),
                 ("gate", (0, 1)), ("gate", (0, 2)), ("a_mix", 0)]
    TIMELINE += [("gate", (0, d)) for d in range(3, KD)]
    TIMELINE += [("gate", (b, d)) for b in (1, 2) for d in range(KD)]

    with ExitStack() as ctx:
        def sb(name, shape, dt=F32):
            return ctx.enter_context(nc.sbuf_tensor(name, shape, dt))

        def sem(name):
            return ctx.enter_context(nc.semaphore(name))

        ring = sb("ring", [P, RING, 4096])
        h_sb = sb("h_sb", [P, TT, D])
        xn = sb("xn", [P, TT, D])
        mergedT = xn[:, :, :].rearrange("p a (b t) -> p (a b) t", t=T)
        xnT = sb("xnT", [P, KD, T])
        work = sb("work", [P, 8192])
        qbT = work[:, 0:1024].rearrange("p (h t) -> p h t", t=T)
        kbT = work[:, 1024:2048].rearrange("p (h t) -> p h t", t=T)
        vb = work[:, 2048:3072].rearrange("p (a n) -> p a n", a=TT)
        qcT = work[:, 3072:4096].rearrange("p (h t) -> p h t", t=T)
        kcT = work[:, 4096:5120].rearrange("p (h t) -> p h t", t=T)
        vc = work[:, 5120:6144].rearrange("p (a n) -> p a n", a=TT)
        va = work[:, 6144:7168].rearrange("p (a n) -> p a n", a=TT)
        uT = work[:, 7168:8192].rearrange("p (g t) -> p g t", t=T)
        yT = {"A": uT, "B": qbT, "C": qcT}
        xgT = work[:, 0:1024].rearrange("p (k j) -> p k j", j=2 * J)
        yeT = work[:, 1024:2048].rearrange("p (k j) -> p k j", j=2 * J)
        ye = work[:, 2048:3072]
        silu = work[:, 3072:3584].rearrange("p (e n) -> p e n", e=2)
        heT = work[:, 3584:4096].rearrange("p (e n) -> p e n", e=2)
        sel = work[:, 4096:4352]
        gated = work[:, 4352:4608]
        gatedT = work[:, 4608:4864]
        scratch = work[:, 6144:7168]

        mix_gain = sb("mix_gain", [P, D])
        ffn_gain = sb("ffn_gain", [P, D])
        v_gain = sb("v_gain", [P, AW])
        sub_gain = sb("sub_gain", [P, 1])
        lam_in = sb("lam_in", [P, 4, BQ])
        b_row = sb("b_row", [1, NG * P])
        rw = sb("rw", [P, KD, E])
        rbias = sb("rbias", [P, E])
        ws = sb("ws", [P, NG, P])
        wsT = sb("wsT", [P, NG, P])
        ident = sb("ident", [P, P])
        ones = sb("ones", [P, P])
        from_here = sb("from_here", [P, P])
        before = sb("before", [P, P])
        zeros = sb("zeros", [P, 512], BF16)
        dist_i = sb("dist_i", [P, W3], I32)
        dist = dist_i[:, :].bitcast(F32)
        b_bias = sb("b_bias", [P, BH, W3])
        c_mask = sb("c_mask", [P, W3])
        iota_i = sb("iota_i", [P, T], I32)
        iota = sb("iota", [P, T])
        prob = sb("prob", [P, 4, W3])
        diff = sb("diff", [P, 2, W3])
        diffT = sb("diffT", [P, 2, W3])
        o_b = sb("o_b", [P, TT, BH, P])
        gate = sb("gate", [P, 2, T])
        gated_up = sb("gated_up", [P, 2, T])
        st = sb("st", [P, 128])
        rt = sb("rt", [P, 24, TT * E])
        tab = sb("tab", [P, 64])
        tab_i = sb("tab_i", [1, 2, PAIRS], I32)

        bank = ctx.enter_context(nc.psum_tensor("bank", [P, 8, 512], F32))
        PJ, UP, SC, TR, OV = 0, 2, 4, 6, 7

        slot_full = [sem(f"slot_full{s}") for s in range(RING)]
        ld_x, ld_gain, ld_small, ld_ws, ld_final = (sem(n) for n in
                                                    ("ld_x", "ld_gain", "ld_small", "ld_ws", "ld_final"))
        consts_pool, consts_dve = sem("consts_pool"), sem("consts_dve")
        pool_step = sem("pool_step")
        ws_masked = sem("ws_masked")
        bias_scaled, bias_masked = sem("bias_scaled"), sem("bias_masked")
        act_stat, dve_stat = sem("act_stat"), sem("dve_stat")
        xn_ready = sem("xn_ready")
        turned = sem("turned")
        turn_taken_a, turn_taken_d = sem("turn_taken_a"), sem("turn_taken_d")
        ws_turned, wsT_ready = sem("ws_turned"), sem("wsT_ready")
        proj_done = sem("proj_done")
        pj_taken = [sem("pj_taken0"), sem("pj_taken1")]
        b_scored, b_max, b_exp, b_comb, b_diff, b_turned, b_turn_taken = (
            sem(n) for n in ("b_scored", "b_max", "b_exp", "b_comb", "b_diff", "b_turned", "b_turn_taken"))
        b_ov, b_ov_a, b_ov_d, b_normed, b_nturned, b_ready = (
            sem(n) for n in ("b_ov", "b_ov_a", "b_ov_d", "b_normed", "b_nturned", "b_ready"))
        c_scored, c_z, c_ln, c_sp, c_summed, c_lo, c_prob, c_ov, c_ready = (
            sem(n) for n in ("c_scored", "c_z", "c_ln", "c_sp", "c_summed", "c_lo", "c_prob", "c_ov", "c_ready"))
        c_abs = sem("c_abs")
        a_gelu, a_vn, a_mixed, a_ready = (sem(n) for n in ("a_gelu", "a_vn", "a_mixed", "a_ready"))
        up_done, gate_sig, up_taken, merged = (sem(n) for n in ("up_done", "gate_sig", "up_taken", "merged"))
        out_done, h_ready = sem("out_done"), sem("h_ready")
        xn2_ready, turned2, turn2_a, turn2_d = (sem(n) for n in ("xn2_ready", "turned2", "turn2_a", "turn2_d"))
        routed, aff_exp, masked, chosen_ready, pos_done, table = (
            sem(n) for n in ("routed", "aff_exp", "masked", "chosen_ready", "pos_done", "table"))
        stored = sem("stored")
        fences = sem("fences")

        NAMES = ("sel", "gathered", "xg_a", "xg_d", "h_done", "silu", "he", "gt_turned", "gt", "y_done",
                 "y_a", "y_d", "ye_turned", "ye_a", "ye_d", "scattered")
        main = {n: sem("m_" + n) for n in NAMES}
        more = {n: sem("o_" + n) for n in NAMES}

        def full_at(i):
            return slot_full[i % RING], 16 * (i // RING + 1)

        def read_at(i):
            if i < len(PROJ):
                return proj_done, 2 * i + 2
            if i >= out_chunk:
                return out_done, TT * (i - out_chunk + 1)
            b, j = divmod(i - len(PROJ), 3)
            if j == 1:
                return up_done, KD * (b + 1)
            return proj_done, 2 * len(PROJ) + KD * b + (4 if j == 0 else KD)

        def slot(i, k):
            return ring[:, i % RING, :].rearrange("p (k n) -> p k n", k=k)

        SS, MS, RS = 0, 8, 16
        LAMP, LAME, NLAM = 24, 26, 28
        NMAX, SUM, COEF = 32, 40, 48
        SSB, MSB, RSB = 56, 64, 72
        SSV, MSV, RSV = 80, 82, 84

        def col(c, n=1):
            return st[:, c:c + n]

        mix_scratch = o_b[:, :, :, :].rearrange("p a h n -> p (a h n)")[:, 0:AW]
        sub_gain_scaled = st[:, 90:91]

        def proj_dst(c, half):
            dst = {UA: uT, VA: va, QB: qbT, KB: kbT, VB: vb, QC: qcT, KC: kcT, VC: vc}[PROJ[c]]
            if PROJ[c] in (VA, VB, VC):
                return dst[:, half, :]
            return dst[:, 2 * half:2 * half + 2, :]

        def bank_view(c, half):
            if PROJ[c] in (VA, VB, VC):
                return bank[:, PJ + half, :]
            return bank[:, PJ + half, :].rearrange("p (h t) -> p h t", t=T)

        def run_pairs(eng, expert_pass):
            eng.wait_ge(table, 1)
            with eng.Fori(0, PAIRS) as p:
                expert_pass(main, p, p, None)
                again = eng.value_load(tab_i[0:1, 0, bass.ds(p, 1)], min_val=0, max_val=3)
                with eng.If(again > 0):
                    base = eng.value_load(tab_i[0:1, 1, bass.ds(p, 1)], min_val=0, max_val=3 * PAIRS)
                    eng.wait_ge(main["scattered"], p + 1 + 1)
                    eng.sem_inc(fences, 1)
                    with eng.Fori(0, again) as i:
                        expert_pass(more, base + i, p, i)
                    eng.wait_ge(more["scattered"], base + again + 1)
                    eng.sem_inc(fences, 1)
                with eng.Else():
                    eng.nop()

        block = ctx.enter_context(nc.Block())

        @block.sync
        def _(sp):
            sp.dma_start(h_sb[:, :, :], x[0].rearrange("(a p) d -> p a d", p=P)).then_inc(ld_x, 16)
            for n in NAMES:
                sp.sem_inc(main[n], 1)
                sp.sem_inc(more[n], 1)
            for i in range(NC):
                if i >= RING:
                    sp.wait_ge(*read_at(i - RING))
                sp.dma_start(ring[:, i % RING, :].rearrange("p (k n) -> p k n", n=chunks[i].shape[2]),
                             chunks[i]).then_inc(slot_full[i % RING], 16)

            def expert_chunk(j, e):
                s = (NC + j) % RING
                src = (moe_w1, moe_w3)[j % 2] if j < 4 else moe_w2
                idx = (e, e, e + 1, e + 1, e, e + 1)[j]
                sp.dma_start(ring[:, s, :].rearrange("p (k n) -> p k n", n=src.shape[3]),
                             src[0, idx].rearrange("(k p) n -> p k n", p=P)).then_inc(slot_full[s], 16)

            for j in range(RING):
                sp.wait_ge(*read_at(NC + j - RING))
                expert_chunk(j, 0)
            sp.wait_ge(table, 1)
            with sp.Fori(0, PAIRS - 1) as p:
                again = sp.value_load(tab_i[0:1, 0, bass.ds(p, 1)], min_val=0, max_val=3)
                with sp.If(again > 0):
                    base = sp.value_load(tab_i[0:1, 1, bass.ds(p, 1)], min_val=0, max_val=3 * PAIRS)
                    sp.wait_ge(more["scattered"], base + again + 1)
                    sp.sem_inc(fences, 1)
                with sp.Else():
                    sp.nop()
                for j in range(RING):
                    done = main["h_done"] if j < 4 else main["y_done"]
                    sp.wait_ge(done, 2 * p + 2 + (j // 2 if j < 4 else j - 4))
                    expert_chunk(j, 2 * p + 2)
            for a in range(TT):
                sp.wait_ge(h_ready, 2 * TT + a + 1)
                sp.dma_start(out[0, a * P:(a + 1) * P, :], xn[:, a, :]).then_inc(stored, 16)
            sp.wait_ge(stored, 16 * TT)

        @block.gpsimd
        def _(pool):
            def rows(ap):
                return ap.partition_broadcast(P)

            pool.dma_start(mix_gain[:, :], rows(norm_mix_gain[0])).then_inc(ld_gain, 16)
            pool.dma_start(ws[:, :, :], gmlp_w_s[0].rearrange("g t s -> t g s")).then_inc(ld_ws, 16)
            small = [(lam_in[:, :, :], rows(diff_lambda[0])), (v_gain[:, :], rows(gmlp_v_gain[0])),
                     (sub_gain[:, :], diff_subln_gain[0].rearrange("(p a) -> p a", a=1)),
                     (b_row[:, :], gmlp_b_s[0:1].rearrange("a g t -> a (g t)")),
                     (rw[:, :, :], router_w.rearrange("(k p) e -> p k e", p=P)),
                     (rbias[:, :], rows(router_bias)), (ffn_gain[:, :], rows(norm_ffn_gain[0]))]
            for dst, src in small:
                pool.dma_start(dst, src).then_inc(ld_small, 16)
            pool.memset(ident[:, :], 0.0).then_inc(pool_step, 1)
            pool.memset(ones[:, :], 1.0).then_inc(pool_step, 1)
            pool.memset(c_mask[:, :], 0.0).then_inc(pool_step, 1)
            pool.memset(zeros[:, :], 0.0).then_inc(pool_step, 1)
            pool.iota(dist_i[:, 0:P], pattern=[[-1, P]], base=0, channel_multiplier=1).then_inc(pool_step, 1)
            pool.iota(dist_i[:, P:W3], pattern=[[-1, 2 * P]], base=P, channel_multiplier=1).then_inc(pool_step, 1)
            pool.iota(iota_i[:, :], pattern=[[1, T]], base=0, channel_multiplier=0).then_inc(pool_step, 1)
            pool.wait_ge(pool_step, 7)
            pool.affine_select(out=ident[:, :], in_=ident[:, :], compare_op=ALU.not_equal, fill=1.0, base=0,
                               pattern=[[-1, P]], channel_multiplier=1).then_inc(consts_pool, 1)
            pool.affine_select(out=from_here[:, :], in_=ones[:, :], compare_op=ALU.is_ge, fill=0.0, base=0,
                               pattern=[[-1, P]], channel_multiplier=1).then_inc(consts_pool, 1)
            pool.affine_select(out=before[:, :], in_=ones[:, :], compare_op=ALU.is_gt, fill=0.0, base=0,
                               pattern=[[1, P]], channel_multiplier=-1).then_inc(consts_pool, 1)
            for c in (0, 2):
                pool.affine_select(out=c_mask[:, c * P:(c + 1) * P], in_=c_mask[:, c * P:(c + 1) * P],
                                   compare_op=ALU.is_gt, fill=MASKED, base=0, pattern=[[1, P]],
                                   channel_multiplier=-1).then_inc(consts_pool, 1)
            pool.wait_ge(ld_ws, 16)
            pool.affine_select(out=ws[:, :, :], in_=ws[:, :, :], compare_op=ALU.is_ge, fill=0.0, base=0,
                               pattern=[[0, NG], [-1, P]], channel_multiplier=1).then_inc(ws_masked, 1)
            pool.wait_ge(bias_scaled, BH)
            pool.affine_select(out=b_bias[:, :, 0:P], in_=b_bias[:, :, 0:P], compare_op=ALU.is_ge, fill=MASKED,
                               base=0, pattern=[[0, BH], [-1, P]], channel_multiplier=1).then_inc(bias_masked, 1)
            pool.affine_select(out=b_bias[:, :, P:W3], in_=b_bias[:, :, P:W3], compare_op=ALU.is_ge, fill=MASKED,
                               base=P, pattern=[[0, BH], [-1, 2 * P]], channel_multiplier=1).then_inc(bias_masked, 1)
            pool.wait_ge(xn_ready, TT)
            pool.dma_start(mix_gain[:, :], rows(final_gain)).then_inc(ld_final, 16)

        @block.scalar
        def _(act):
            def square_sum(src, dst, width):
                act.activation(scratch_of(width), src, ACT.Square, accum_out=dst).then_inc(act_stat, 1)

            def scratch_of(width):
                return scratch[:, 0:width]

            def sqrt(dst, src, need):
                act.wait_ge(dve_stat, need)
                act.activation(dst, src, ACT.Sqrt).then_inc(act_stat, 1)

            act.wait_ge(ld_x, 16)
            for a in range(TT):
                if a:
                    act.wait_ge(act_stat, a)
                square_sum(h_sb[:, a, :], col(SS + a), D)
            sqrt(col(RS, TT), col(MS, TT), 2)
            act.wait_ge(dve_stat, 4)
            act.activation(col(LAME, 2), col(LAMP, 2), ACT.Exp).then_inc(act_stat, 1)
            for g in range(2):
                act.wait_ge(turned, g + 1)
                act.activation(xnT[:, 2 * g:2 * g + 2, :], bank[:, SC + g, :].rearrange("p (k t) -> p k t", t=T),
                               ACT.Copy).then_inc(turn_taken_a, 1)

            def proj(c, half):
                if half or PROJ[c] in (UA, VA):
                    return
                act.wait_ge(proj_done, 2 * c + 1)
                act.activation(proj_dst(c, half), bank_view(c, half), ACT.Copy).then_inc(pj_taken[0], 1)

            def b_scores(h):
                q = h % 2
                act.wait_ge(b_max, h + 1)
                for m in range(2):
                    for blk, (lo, hi) in enumerate(((0, P), (P, W3))):
                        act.activation(prob[:, 2 * q + m, lo:hi], prob[:, 2 * q + m, lo:hi], ACT.Exp,
                                       bias=col(NMAX + 4 * q + 2 * blk + m),
                                       accum_out=col(SUM + 4 * q + 2 * blk + m)).then_inc(b_exp, 1)

            def b_turn(h):
                act.wait_ge(b_turned, h + 1)
                if h >= 2:
                    act.wait_ge(b_ov, h - 1)
                act.activation(diffT[:, h % 2, :], bank[:, TR, 0:W3], ACT.Copy).then_inc(b_turn_taken, 1)

            def b_values(h):
                act.wait_ge(b_ov_d, h + 1)
                for a in range(TT):
                    if h or a:
                        act.wait_ge(b_ov_a, TT * h + a)
                    act.activation(gate[:, 0, 0:P], o_b[:, a, h, :], ACT.Square,
                                   accum_out=col(SSB + BH * a + h)).then_inc(b_ov_a, 1)

            def b_norm(_):
                sqrt(col(RSB, TT * BH), col(MSB, TT * BH), 6)

            def b_done(_):
                act.wait_ge(consts_dve, 4)
                act.wait_ge(b_nturned, 1)
                act.activation(yT["B"][:, 0:2, :], bank[:, TR, :].rearrange("p (h t) -> p h t", t=T), ACT.Copy,
                               scale=sub_gain_scaled).then_inc(b_ready, 1)

            def c_keep(h):
                act.wait_ge(c_z, h + 1)
                w = diff[:, h % 2, :]
                if h >= 2:
                    act.wait_ge(c_summed, h - 1)
                act.activation(w, prob[:, h % 4, :], ACT.Abs).then_inc(c_abs, 1)
                act.wait_ge(c_abs, 3 * h + 1)
                act.activation(w, w, ACT.Exp, scale=-1.0).then_inc(c_abs, 1)
                act.wait_ge(c_abs, 3 * h + 2)
                act.activation(w, w, ACT.Ln, bias=1.0).then_inc(c_abs, 1)

            def c_logits(h):
                act.wait_ge(c_lo, h + 1)
                act.activation(prob[:, h % 4, :], prob[:, h % 4, :], ACT.Exp).then_inc(c_prob, 1)

            def c_values(h):
                if h % 2:
                    act.wait_ge(c_ov, h + 1)
                    t = h // 2
                    act.activation(yT["C"][:, t, :], bank[:, OV, (t % 2) * T:(t % 2 + 1) * T],
                                   ACT.Copy).then_inc(c_ready, 1)

            def a_gelu_(_):
                act.wait_ge(pj_taken[0], 8)
                act.wait_ge(pj_taken[1], 8)
                for a in range(TT):
                    act.activation(va[:, a, :], va[:, a, :], ACT.Gelu_apprx_tanh).then_inc(a_gelu, 1)
                act.activation(uT[:, :, :], uT[:, :, :], ACT.Gelu_apprx_tanh).then_inc(a_gelu, 1)
                act.wait_ge(a_gelu, TT)
                for a in range(TT):
                    if a:
                        act.wait_ge(act_stat, 6)
                    act.activation(mix_scratch, va[:, a, :], ACT.Square,
                                   accum_out=col(SSV + a)).then_inc(act_stat, 1)
                sqrt(col(RSV, TT), col(MSV, TT), 8)

            def gate_(b, d):
                n = KD * b + d
                act.wait_ge(proj_done, 16 + n + 1)
                if n >= 2:
                    act.wait_ge(up_taken, n - 1)
                act.activation(gate[:, n % 2, :], bank[:, PJ + n % 2, 0:T], ACT.Sigmoid)\
                   .then_inc(pj_taken[n % 2], 1)

            STEPS = {"proj": lambda i: proj(*i), "b_scores": b_scores, "b_turn": b_turn, "b_values": b_values,
                     "b_norm": b_norm, "b_done": b_done, "c_keep": c_keep, "c_logits": c_logits,
                     "c_values": c_values, "a_gelu": a_gelu_, "gate": lambda i: gate_(*i)}
            for step, i in TIMELINE:
                if step in STEPS:
                    STEPS[step](i)

            act.wait_ge(merged, 2 * KD)
            for a in range(TT):
                act.wait_ge(h_ready, a + 1)
                act.wait_ge(act_stat, 8 + a)
                square_sum(h_sb[:, a, :], col(SS + a), D)
            sqrt(col(RS, TT), col(MS, TT), 10)
            for g in range(2):
                act.wait_ge(turned2, g + 1)
                act.activation(xnT[:, 2 * g:2 * g + 2, :], bank[:, SC + g, :].rearrange("p (k t) -> p k t", t=T),
                               ACT.Copy).then_inc(turn2_a, 1)
            act.wait_ge(routed, 1)
            act.activation(rt[:, 0, :], bank[:, SC, 0:TT * E], ACT.Exp, scale=-1.0).then_inc(aff_exp, 1)

            def expert_pass(s, n, p, i):
                act.wait_ge(s["gathered"], 2 * n + 1 + 1)
                act.wait_ge(s["h_done"], 2 * n + 1)
                act.activation(xgT[:, 0:4, :], bank[:, 4, :].rearrange("p (k j) -> p k j", j=2 * J),
                               ACT.Copy).then_inc(s["xg_a"], 1)
                for e in range(2):
                    act.wait_ge(s["h_done"], 2 * n + e + 1 + 1)
                    act.wait_ge(s["he"], 2 * n + e + 1)
                    act.activation(silu[:, e, :], bank[:, 6 + e, 0:KF * J], ACT.Silu).then_inc(s["silu"], 1)
                act.wait_ge(s["gt_turned"], n + 1 + 1)
                act.wait_ge(s["scattered"], n + 1)
                act.activation(gatedT, bank[:, 4, 0:T], ACT.Copy).then_inc(s["gt"], 1)
                act.wait_ge(s["y_done"], 2 * n + 1 + 1)
                act.wait_ge(s["ye_turned"], 2 * n + 1)
                act.activation(yeT[:, :, 0:J], bank[:, 6, :].rearrange("p (k j) -> p k j", j=J),
                               ACT.Copy).then_inc(s["y_a"], 1)
                act.wait_ge(s["ye_turned"], 2 * n + 1 + 1)
                act.wait_ge(s["scattered"], n + 1)
                act.activation(ye[:, 0:512], bank[:, 4, :], ACT.Copy).then_inc(s["ye_a"], 1)

            run_pairs(act, expert_pass)
            for a in range(TT):
                act.wait_ge(h_ready, TT + a + 1)
                act.wait_ge(act_stat, 11 + a)
                square_sum(h_sb[:, a, :], col(SS + a), D)
            sqrt(col(RS, TT), col(MS, TT), 12)

        @block.vector
        def _(dve):
            n_stat = [0]

            def stat(ins):
                n_stat[0] += 1
                ins.then_inc(dve_stat, 1)
                dve.wait_ge(dve_stat, n_stat[0])

            def mean_inverse(dst, src, width):
                stat(dve.tensor_scalar(dst, src, 1.0 / width, EPS, ALU.mult, ALU.add))
                stat(dve.reciprocal(dst, dst))

            dve.wait_ge(act_stat, 2)
            mean_inverse(col(MS, TT), col(SS, TT), D)
            dve.wait_ge(ld_small, 16 * 7)
            lam4 = lam_in[:, :, :].rearrange("p (a b) q -> p a b q", b=2)
            stat(dve.tensor_tensor(gated_up[:, 0, 0:2 * BQ].rearrange("p (a q) -> p a q", q=BQ),
                                   lam4[:, :, 0, :], lam4[:, :, 1, :], ALU.mult))
            stat(dve.tensor_reduce(col(LAMP, 2), gated_up[:, 0, 0:2 * BQ].rearrange("p (a q) -> p a q", q=BQ),
                                   AX.X, ALU.add))
            dve.wait_ge(act_stat, 3)
            dve.wait_ge(ld_gain, 16)
            for a in range(TT):
                dve.scalar_tensor_tensor(out=xn[:, a, :], in0=h_sb[:, a, :], scalar=col(RS + a),
                                         in1=mix_gain[:, :], op0=ALU.mult, op1=ALU.mult).then_inc(xn_ready, 1)
            dve.wait_ge(pool_step, 7)
            dve.tensor_copy(dist, dist_i[:, :]).then_inc(consts_dve, 1)
            dve.tensor_copy(iota[:, :], iota_i[:, :]).then_inc(consts_dve, 1)
            dve.wait_ge(consts_dve, 2)
            for h in range(BH):
                dve.tensor_scalar(b_bias[:, h, :], dist, -SLOPES[h], None, ALU.mult).then_inc(bias_scaled, 1)
            for g in range(2):
                dve.wait_ge(turned, 2 + g + 1)
                dve.tensor_copy(xnT[:, 4 + 2 * g:6 + 2 * g, :],
                                bank[:, TR + g, :].rearrange("p (k t) -> p k t", t=T)).then_inc(turn_taken_d, 1)
            dve.wait_ge(act_stat, 4)
            dve.scalar_tensor_tensor(out=col(NLAM), in0=col(LAME + 1), scalar=-LAMBDA_INIT, in1=col(LAME),
                                     op0=ALU.add, op1=ALU.subtract).then_inc(consts_dve, 1)
            dve.tensor_scalar(sub_gain_scaled, sub_gain[:, :], 1.0 - LAMBDA_INIT, None, ALU.mult)\
               .then_inc(consts_dve, 1)
            dve.wait_ge(consts_dve, 4)
            dve.wait_ge(ws_turned, 1)
            dve.tensor_copy(wsT[:, :, :], bank[:, SC, :].rearrange("p (g t) -> p g t", t=P)).then_inc(wsT_ready, 1)

            def proj(c, half):
                if not half and PROJ[c] not in (UA, VA):
                    return
                dve.wait_ge(proj_done, 2 * c + half + 1)
                dve.tensor_copy(proj_dst(c, half), bank_view(c, half)).then_inc(pj_taken[half], 1)

            def b_scores(h):
                q = h % 2
                if h == 0:
                    dve.wait_ge(bias_masked, 2)
                dve.wait_ge(b_scored, h + 1)
                p2 = prob[:, 2 * q:2 * q + 2, :]
                for m in range(2):
                    dve.scalar_tensor_tensor(out=prob[:, 2 * q + m, :], in0=bank[:, SC + m, 0:W3], scalar=B_SCALE,
                                             in1=b_bias[:, h, :], op0=ALU.mult, op1=ALU.add).then_inc(b_comb, 1)
                dve.wait_ge(b_comb, 7 * h + 2)
                for blk, (lo, hi) in enumerate(((0, P), (P, W3))):
                    dve.tensor_reduce(col(NMAX + 4 * q + 2 * blk, 2), p2[:, :, lo:hi], AX.X, ALU.max)\
                       .then_inc(b_comb, 1)
                dve.wait_ge(b_comb, 7 * h + 4)
                dve.tensor_scalar(col(NMAX + 4 * q, 4), col(NMAX + 4 * q, 4), -1.0, None, ALU.mult)\
                   .then_inc(b_max, 1)

            def b_combine(h):
                q = h % 2
                dve.wait_ge(b_exp, 4 * (h + 1))
                dve.reciprocal(col(COEF + 4 * q, 4), col(SUM + 4 * q, 4)).then_inc(b_comb, 1)
                dve.wait_ge(b_comb, 7 * h + 5)
                lam_cols = st[:, COEF + 4 * q + 1:COEF + 4 * q + 4:2]
                dve.tensor_scalar(lam_cols, lam_cols, col(NLAM), None, ALU.mult).then_inc(b_comb, 1)
                dve.wait_ge(b_comb, 7 * h + 6)
                if h >= 2:
                    dve.wait_ge(b_turned, h - 1)
                for blk, (lo, hi) in enumerate(((0, P), (P, W3))):
                    ins = dve.tensor_scalar(prob[:, 2 * q + 1, lo:hi], prob[:, 2 * q + 1, lo:hi],
                                            col(COEF + 4 * q + 2 * blk + 1), None, ALU.mult)
                ins.then_inc(b_comb, 1)
                dve.wait_ge(b_comb, 7 * h + 7)
                for blk, (lo, hi) in enumerate(((0, P), (P, W3))):
                    ins = dve.scalar_tensor_tensor(out=diff[:, q, lo:hi], in0=prob[:, 2 * q, lo:hi],
                                                   scalar=col(COEF + 4 * q + 2 * blk), in1=prob[:, 2 * q + 1, lo:hi],
                                                   op0=ALU.mult, op1=ALU.add)
                ins.then_inc(b_diff, 1)

            def b_values(h):
                dve.wait_ge(b_ov, h + 1)
                dve.tensor_copy(o_b[:, :, h, :], bank[:, OV, (h % 2) * T:(h % 2 + 1) * T]
                                .rearrange("p (a n) -> p a n", a=TT)).then_inc(b_ov_d, 1)

            def b_norm(_):
                dve.wait_ge(b_ov_a, TT * BH)
                mean_inverse(col(MSB, TT * BH), col(SSB, TT * BH), P)
                dve.wait_ge(act_stat, 5)
                dve.wait_ge(b_ov_d, BH)
                o8 = o_b[:, :, :, :].rearrange("p a h n -> p (a h) n")
                dve.tensor_tensor(o8, o8, col(RSB, TT * BH).unsqueeze(2).to_broadcast([P, TT * BH, P]), ALU.mult)\
                   .then_inc(b_normed, 1)

            def b_done(_):
                dve.wait_ge(b_nturned, 2)
                dve.tensor_scalar(yT["B"][:, 2:4, :], bank[:, OV, :].rearrange("p (h t) -> p h t", t=T),
                                  sub_gain_scaled, None, ALU.mult).then_inc(b_ready, 1)

            def c_scores(h):
                dve.wait_ge(c_scored, h + 1)
                if h == 0:
                    dve.wait_ge(consts_pool, 5)
                if h >= 4:
                    dve.wait_ge(c_ov, h - 3)
                dve.scalar_tensor_tensor(out=prob[:, h % 4, :], in0=bank[:, SC + h % 2, 0:W3], scalar=C_SCALE,
                                         in1=c_mask[:, :], op0=ALU.mult, op1=ALU.add).then_inc(c_z, 1)

            def c_keep(h):
                dve.wait_ge(c_abs, 3 * h + 3)
                w = diff[:, h % 2, :]
                dve.scalar_tensor_tensor(out=w, in0=prob[:, h % 4, :], scalar=0.0, in1=w,
                                         op0=ALU.max, op1=ALU.add).then_inc(c_sp, 1)

            def c_logits(h):
                dve.wait_ge(c_summed, h + 1)
                dve.tensor_tensor(prob[:, h % 4, :], prob[:, h % 4, :], bank[:, UP + h % 2, 0:W3],
                                  ALU.subtract).then_inc(c_lo, 1)

            def a_gelu_(_):
                dve.wait_ge(act_stat, 7)
                mean_inverse(col(MSV, TT), col(SSV, TT), AW)
                dve.wait_ge(act_stat, 8)
                for a in range(TT):
                    dve.scalar_tensor_tensor(out=va[:, a, :], in0=va[:, a, :], scalar=col(RSV + a),
                                             in1=v_gain[:, :], op0=ALU.mult, op1=ALU.mult).then_inc(a_vn, 1)

            def a_mix(_):
                dve.wait_ge(a_gelu, TT + 1)
                for a in range(TT):
                    dve.wait_ge(a_mixed, a + 1)
                    dve.tensor_tensor(uT[:, :, a * P:(a + 1) * P], uT[:, :, a * P:(a + 1) * P],
                                      bank[:, SC + a, :].rearrange("p (g t) -> p g t", t=P), ALU.mult)\
                       .then_inc(a_ready, 1)

            def gate_(b, d):
                n = KD * b + d
                dve.wait_ge(pj_taken[n % 2], 8 + n // 2 + 1)
                dve.wait_ge(up_done, n + 1)
                if b == 0:
                    dve.tensor_tensor(mergedT[:, d, :], gate[:, n % 2, :], bank[:, UP + n % 2, 0:T], ALU.mult)\
                       .then_inc(up_taken, 1)
                else:
                    dve.tensor_tensor(gated_up[:, n % 2, :], gate[:, n % 2, :], bank[:, UP + n % 2, 0:T], ALU.mult)\
                       .then_inc(up_taken, 1)
                    dve.wait_ge(up_taken, n + 1)
                    if b == 2:
                        dve.wait_ge(merged, d + 1)
                    dve.tensor_tensor(mergedT[:, d, :], mergedT[:, d, :], gated_up[:, n % 2, :], ALU.add)\
                       .then_inc(merged, 1)

            STEPS = {"proj": lambda i: proj(*i), "b_scores": b_scores, "b_combine": b_combine, "b_values": b_values,
                     "b_norm": b_norm, "b_done": b_done, "c_scores": c_scores, "c_keep": c_keep,
                     "c_logits": c_logits, "a_gelu": a_gelu_, "a_mix": a_mix, "gate": lambda i: gate_(*i)}
            for step, i in TIMELINE:
                if step in STEPS:
                    STEPS[step](i)

            for a in range(TT):
                for n in range(2):
                    dve.wait_ge(out_done, 2 * n + a + 1)
                    ins = dve.tensor_tensor(h_sb[:, a, n * CW:(n + 1) * CW], h_sb[:, a, n * CW:(n + 1) * CW],
                                            bank[:, 2 * n + a, :], ALU.add)
                ins.then_inc(h_ready, 1)
            dve.wait_ge(act_stat, 10)
            mean_inverse(col(MS, TT), col(SS, TT), D)
            dve.wait_ge(act_stat, 11)
            for a in range(TT):
                dve.scalar_tensor_tensor(out=xn[:, a, :], in0=h_sb[:, a, :], scalar=col(RS + a),
                                         in1=ffn_gain[:, :], op0=ALU.mult, op1=ALU.mult).then_inc(xn2_ready, 1)
            for g in range(2):
                dve.wait_ge(turned2, 2 + g + 1)
                dve.tensor_copy(xnT[:, 4 + 2 * g:6 + 2 * g, :],
                                bank[:, TR + g, :].rearrange("p (k t) -> p k t", t=T)).then_inc(turn2_d, 1)

            n_step = [0]

            def step(ins):
                n_step[0] += 1
                ins.then_inc(masked, 1)
                dve.wait_ge(masked, n_step[0])

            def r(i):
                return rt[:, i, :]

            def by_expert(ap):
                return ap.rearrange("p (a e) -> p a e", e=E)

            def by_group(ap):
                return ap.rearrange("p (g e) -> p g e", e=EG)

            def small(i, n):
                return rt[:, i, 0:n]

            def tt(o, a, b, op):
                step(dve.tensor_tensor(o, a, b, op))

            def ts(o, a, s1, s2, op0, op1=ALU.bypass):
                step(dve.tensor_scalar(o, a, s1, s2, op0, op1))

            NGT = TT * NGR
            bias2 = rbias[:, :].unsqueeze(1).to_broadcast([P, TT, E])
            ts(tab[:, 0:E], iota[:, 0:E], -1.0, float(E), ALU.mult, ALU.add)
            dve.wait_ge(aff_exp, 1)
            ts(r(0), r(0), 1.0, None, ALU.add)
            step(dve.reciprocal(r(1), r(0)))
            tt(by_expert(r(2)), by_expert(r(1)), bias2, ALU.add)
            s4 = by_group(r(2))
            tt(small(3, NGT), s4[:, :, 0], s4[:, :, 1], ALU.max)
            tt(small(4, NGT), s4[:, :, 2], s4[:, :, 3], ALU.max)
            tt(small(5, NGT), s4[:, :, 0], s4[:, :, 1], ALU.min)
            tt(small(6, NGT), s4[:, :, 2], s4[:, :, 3], ALU.min)
            tt(small(7, NGT), small(3, NGT), small(4, NGT), ALU.max)
            tt(small(8, NGT), small(3, NGT), small(4, NGT), ALU.min)
            tt(small(9, NGT), small(5, NGT), small(6, NGT), ALU.max)
            tt(small(8, NGT), small(8, NGT), small(9, NGT), ALU.max)
            tt(small(9, NGT), small(7, NGT), small(8, NGT), ALU.add)

            def first_of_max(oh, v, n, w, m):
                def view(ap):
                    return ap.rearrange("p (a e) -> p a e", e=n)

                def wide(ap):
                    return ap.unsqueeze(2).to_broadcast([P, TT, n])
                step(dve.tensor_reduce(m, view(v), AX.X, ALU.max))
                tt(view(w), view(v), wide(m), ALU.is_equal)
                tt(view(w), view(w), tab[:, 0:n].unsqueeze(1).to_broadcast([P, TT, n]), ALU.mult)
                step(dve.tensor_reduce(m, view(w), AX.X, ALU.max))
                tt(view(oh), view(w), wide(m), ALU.is_equal)

            first_of_max(small(10, NGT), small(9, NGT), NGR, small(11, NGT), small(12, TT))
            in_group = small(10, NGT).unsqueeze(2).to_broadcast([P, NGT, EG])
            ts(small(11, NGT), small(10, NGT), -MASKED, MASKED, ALU.mult, ALU.add)
            tt(by_group(r(2)), by_group(r(2)), in_group, ALU.mult)
            tt(by_group(r(2)), by_group(r(2)), small(11, NGT).unsqueeze(2).to_broadcast([P, NGT, EG]), ALU.add)
            first_of_max(r(13), r(2), E, r(14), small(12, TT))
            step(dve.scalar_tensor_tensor(out=r(2), in0=r(13), scalar=2 * MASKED, in1=r(2),
                                          op0=ALU.mult, op1=ALU.add))
            first_of_max(r(15), r(2), E, r(14), small(12, TT))
            tt(r(13), r(13), r(15), ALU.add)
            dve.tensor_tensor(r(14), r(13), r(1), ALU.mult).then_inc(chosen_ready, 1)
            dve.wait_ge(chosen_ready, 1)
            step(dve.tensor_reduce(small(12, TT), by_expert(r(14)), AX.X, ALU.add))
            step(dve.reciprocal(small(16, TT), small(12, TT)))
            pair_order = "p (a q e) -> p a q e"
            dst17 = rt[:, 17, :].rearrange("p (q a e) -> p a q e", a=TT, e=2)
            dst18 = rt[:, 18, :].rearrange("p (q a e) -> p a q e", a=TT, e=2)
            for a in range(TT):
                ts(dst17[:, a], r(14).rearrange(pair_order, a=TT, e=2)[:, a], rt[:, 16, a:a + 1], None, ALU.mult)
            dve.wait_ge(pos_done, 1)
            tt(r(19), bank[:, SC, 0:TT * E], r(13), ALU.mult)
            for a in range(TT):
                step(dve.scalar_tensor_tensor(out=dst18[:, a], in0=r(19).rearrange(pair_order, a=TT, e=2)[:, a],
                                              scalar=-1.0, in1=r(13).rearrange(pair_order, a=TT, e=2)[:, a],
                                              op0=ALU.add, op1=ALU.add))
            step(dve.tensor_copy(tab[:, 16:16 + E], bank[:, SC + 1, 0:E]))
            tt(tab[:, 32:32 + PAIRS], tab[:, 16:16 + E:2], tab[:, 17:16 + E:2], ALU.max)
            ts(tab[:, 40:40 + PAIRS], tab[:, 32:32 + PAIRS], float(J), None, ALU.is_gt)
            for c in (2, 3):
                step(dve.scalar_tensor_tensor(out=tab[:, 40:40 + PAIRS], in0=tab[:, 32:32 + PAIRS],
                                              scalar=float(c * J), in1=tab[:, 40:40 + PAIRS],
                                              op0=ALU.is_gt, op1=ALU.add))
            step(dve.memset(tab[:, 48:49], 0.0))
            for q in range(1, PAIRS):
                tt(tab[:, 48 + q:49 + q], tab[:, 47 + q:48 + q], tab[:, 39 + q:40 + q], ALU.add)
            step(dve.tensor_copy(tab_i[0:1, 0, :], tab[0:1, 40:40 + PAIRS]))
            dve.tensor_copy(tab_i[0:1, 1, :], tab[0:1, 48:48 + PAIRS]).then_inc(table, 1)

            def expert_pass(s, n, p, i):
                dve.wait_ge(s["gathered"], 2 * n + 1)
                wide = [P, 4, J]
                cols = iota[:, 0:J] if i is None else iota[:, bass.ds(i * J + J, J)]
                pos4 = rt[:, 18, bass.ds(p * 4, 4)].unsqueeze(2).to_broadcast(wide)
                gate4 = rt[:, 17, bass.ds(p * 4, 4)].unsqueeze(2).to_broadcast(wide)
                sel4 = sel.rearrange("p (a j) -> p a j", j=J)
                gated4 = gated.rearrange("p (a j) -> p a j", j=J)
                dve.tensor_tensor(sel4, cols.unsqueeze(1).to_broadcast(wide), pos4, ALU.is_equal)\
                   .then_inc(s["sel"], 1)
                dve.wait_ge(s["sel"], 2 * n + 1 + 1)
                dve.wait_ge(s["gt_turned"], n + 1)
                dve.tensor_tensor(gated4, sel4, gate4, ALU.mult).then_inc(s["sel"], 1)
                dve.wait_ge(s["gathered"], 2 * n + 2 + 1)
                dve.wait_ge(s["h_done"], 2 * n + 1)
                dve.tensor_copy(xgT[:, 4:8, :], bank[:, 5, :].rearrange("p (k j) -> p k j", j=2 * J))\
                   .then_inc(s["xg_d"], 1)
                for e in range(2):
                    dve.wait_ge(s["silu"], 2 * n + e + 1 + 1)
                    dve.wait_ge(s["y_done"], 2 * n + 1)
                    dve.tensor_tensor(heT[:, e, :], silu[:, e, :], bank[:, 6 + e, KF * J:2 * KF * J], ALU.mult)\
                       .then_inc(s["he"], 1)
                dve.wait_ge(s["y_done"], 2 * n + 2 + 1)
                dve.wait_ge(s["ye_turned"], 2 * n + 1)
                dve.tensor_copy(yeT[:, :, J:2 * J], bank[:, 7, :].rearrange("p (k j) -> p k j", j=J))\
                   .then_inc(s["y_d"], 1)
                dve.wait_ge(s["ye_turned"], 2 * n + 2 + 1)
                dve.wait_ge(s["scattered"], n + 1)
                dve.tensor_copy(ye[:, 512:1024], bank[:, 5, :]).then_inc(s["ye_d"], 1)

            run_pairs(dve, expert_pass)

            dve.wait_ge(main["scattered"], PAIRS + 1)
            for a in range(TT):
                for n in range(2):
                    ins = dve.tensor_tensor(h_sb[:, a, n * CW:(n + 1) * CW], h_sb[:, a, n * CW:(n + 1) * CW],
                                            bank[:, 2 * n + a, :], ALU.add)
                ins.then_inc(h_ready, 1)
            dve.wait_ge(act_stat, 13)
            mean_inverse(col(MS, TT), col(SS, TT), D)
            dve.wait_ge(act_stat, 14)
            dve.wait_ge(ld_final, 16)
            for a in range(TT):
                dve.scalar_tensor_tensor(out=xn[:, a, :], in0=h_sb[:, a, :], scalar=col(RS + a),
                                         in1=mix_gain[:, :], op0=ALU.mult, op1=ALU.mult).then_inc(h_ready, 1)

        @block.tensor
        def _(pe):
            def turn_rows(done):
                for g in range(4):
                    for i in range(4):
                        k, a = 2 * g + i // 2, i % 2
                        ins = pe.transpose(bank[:, SC + g, i * P:(i + 1) * P], xn[:, a, k * P:(k + 1) * P], ident[:, :])
                    ins.then_inc(done, 1)

            pe.wait_ge(xn_ready, TT)
            pe.wait_ge(consts_pool, 5)
            turn_rows(turned)
            pe.wait_ge(turn_taken_a, 1)
            pe.wait_ge(ws_masked, 1)
            for g in range(NG):
                ins = pe.transpose(bank[:, SC, g * P:(g + 1) * P], ws[:, g, :], ident[:, :])
            ins.then_inc(ws_turned, 1)
            pe.wait_ge(turn_taken_a, 2)
            pe.wait_ge(turn_taken_d, 2)

            def proj(c, half):
                w = slot(c, KD)
                if half == 0:
                    pe.wait_ge(*full_at(c))
                if c:
                    pe.wait_ge(pj_taken[half], c)
                if PROJ[c] in (VA, VB, VC):
                    for k in range(KD):
                        ins = pe.matmul(bank[:, PJ + half, :], xnT[:, k, half * P:(half + 1) * P], w[:, k, :],
                                        start=(k == 0), stop=(k == KD - 1))
                else:
                    for i in range(2):
                        m = 2 * half + i
                        for k in range(KD):
                            ins = pe.matmul(bank[:, PJ + half, i * T:(i + 1) * T], w[:, k, m * P:(m + 1) * P],
                                            xnT[:, k, :], start=(k == 0), stop=(k == KD - 1))
                ins.then_inc(proj_done, 1)

            def b_scores(h):
                if h == 0:
                    pe.wait_ge(pj_taken[0], 2)
                    pe.wait_ge(pj_taken[1], 2)
                    pe.wait_ge(wsT_ready, 1)
                else:
                    pe.wait_ge(b_max, h)
                for m in range(2):
                    rows = slice(m * BQ, (m + 1) * BQ)
                    pe.matmul(bank[:, SC + m, 0:P], qbT[rows, h, 0:P], kbT[rows, h, 0:P], start=True, stop=True)
                    ins = pe.matmul(bank[:, SC + m, P:W3], qbT[rows, h, P:T], kbT[rows, h, :], start=True, stop=True)
                ins.then_inc(b_scored, 1)

            def b_turn(h):
                pe.wait_ge(b_diff, h + 1)
                if h >= 1:
                    pe.wait_ge(b_turn_taken, h)
                for i in range(3):
                    ins = pe.transpose(bank[:, TR, i * P:(i + 1) * P], diff[:, h % 2, i * P:(i + 1) * P], ident[:, :])
                ins.then_inc(b_turned, 1)

            def b_values(h):
                pe.wait_ge(b_turn_taken, h + 1)
                if h == 0:
                    pe.wait_ge(pj_taken[0], 3)
                    pe.wait_ge(pj_taken[1], 3)
                if h >= 1:
                    pe.wait_ge(b_ov_d, h)
                o, e = (h % 2) * T, slice(h * P, (h + 1) * P)
                pe.matmul(bank[:, OV, o:o + P], diffT[:, h % 2, 0:P], vb[:, 0, e], start=True, stop=True)
                pe.matmul(bank[:, OV, o + P:o + T], diffT[:, h % 2, P:2 * P], vb[:, 0, e], start=True, stop=False)
                pe.matmul(bank[:, OV, o + P:o + T], diffT[:, h % 2, 2 * P:W3], vb[:, 1, e], start=False, stop=True)\
                  .then_inc(b_ov, 1)

            def b_done(_):
                pe.wait_ge(b_normed, 1)
                pe.wait_ge(b_turn_taken, BH)
                for b, first in enumerate((0, 2)):
                    for i in range(4):
                        h, a = first + i // 2, i % 2
                        ins = pe.transpose(bank[:, TR + b, i * P:(i + 1) * P], o_b[:, a, h, :], ident[:, :])
                    ins.then_inc(b_nturned, 1)

            def c_scores(h):
                if h == 0:
                    pe.wait_ge(pj_taken[0], 5)
                    pe.wait_ge(pj_taken[1], 5)
                    pe.wait_ge(b_max, BH)
                if h >= 2:
                    pe.wait_ge(c_z, h - 1)
                rows, t = slice((h % 2) * CD, (h % 2 + 1) * CD), h // 2
                pe.matmul(bank[:, SC + h % 2, 0:T], kcT[rows, t, 0:P], qcT[rows, t, :], start=True, stop=True)
                pe.matmul(bank[:, SC + h % 2, T:W3], kcT[rows, t, P:T], qcT[rows, t, P:T], start=True, stop=True)\
                  .then_inc(c_scored, 1)

            def c_sums(h):
                pe.wait_ge(c_sp, h + 1)
                if h >= 2:
                    pe.wait_ge(c_lo, h - 1)
                w, b = diff[:, h % 2, :], bank[:, UP + h % 2, :]
                pe.matmul(b[:, 0:W3], from_here[:, :], w, start=True, stop=False, skip_group_check=True)
                pe.matmul(b[:, P:T], ones[:, :], w[:, T:W3], start=False, stop=True, skip_group_check=True)\
                  .then_inc(c_summed, 1)

            def c_values(h):
                pe.wait_ge(c_prob, h + 1)
                if h == 0:
                    pe.wait_ge(pj_taken[0], 6)
                    pe.wait_ge(pj_taken[1], 6)
                    pe.wait_ge(b_ready, 2)
                if h >= 2 and h % 2 == 0:
                    pe.wait_ge(c_ready, h // 2)
                rows, t = slice((h % 2) * CD, (h % 2 + 1) * CD), h // 2
                o = (t % 2) * T
                a, v = prob[:, h % 4, :], slice(h * CD, (h + 1) * CD)
                pe.matmul(bank[rows, OV, o:o + T], vc[:, 0, v], a[:, 0:T], start=True, stop=False,
                          skip_group_check=True)
                pe.matmul(bank[rows, OV, o + P:o + T], vc[:, 1, v], a[:, T:W3], start=False, stop=True,
                          skip_group_check=True).then_inc(c_ov, 1)

            def a_mix(_):
                pe.wait_ge(a_vn, TT)
                pe.wait_ge(c_z, CH)
                for a in range(TT):
                    for g in range(NG):
                        dst = bank[:, SC + a, g * P:(g + 1) * P]
                        pe.matmul(dst, va[:, a, g * P:(g + 1) * P], wsT[:, g, :], start=True, stop=False)
                        ins = pe.matmul(dst, ones[0:1, :], b_row[0:1, g * P:(g + 1) * P], start=False, stop=True)
                    ins.then_inc(a_mixed, 1)

            def gate_(b, d):
                name = BRANCHES[b][0]
                n = KD * b + d
                gc, uc = gate_chunk[name][d // 4], up_chunk[name]
                if d % 4 == 0:
                    pe.wait_ge(*full_at(gc))
                pe.wait_ge(pj_taken[n % 2], 8 + n // 2)
                w = slot(gc, KD)
                for k in range(KD):
                    ins = pe.matmul(bank[:, PJ + n % 2, 0:T], w[:, k, (d % 4) * P:(d % 4 + 1) * P], xnT[:, k, :],
                                    start=(k == 0), stop=(k == KD - 1))
                ins.then_inc(proj_done, 1)
                if d == 0:
                    pe.wait_ge(*full_at(uc))
                    pe.wait_ge(*{"A": (a_ready, TT), "B": (b_ready, 2), "C": (c_ready, CH // 2)}[name])
                if n < 2:
                    pe.wait_ge(c_lo, CH - 1 + n)
                else:
                    pe.wait_ge(up_taken, n - 1)
                w = slot(uc, 4)
                for k in range(4):
                    ins = pe.matmul(bank[:, UP + n % 2, 0:T], w[:, k, d * P:(d + 1) * P], yT[name][:, k, :],
                                    start=(k == 0), stop=(k == 3))
                ins.then_inc(up_done, 1)

            STEPS = {"proj": lambda i: proj(*i), "b_scores": b_scores, "b_turn": b_turn, "b_values": b_values,
                     "b_done": b_done, "c_scores": c_scores, "c_sums": c_sums, "c_values": c_values,
                     "a_mix": a_mix, "gate": lambda i: gate_(*i)}
            for step, i in TIMELINE:
                if step in STEPS:
                    STEPS[step](i)

            pe.wait_ge(merged, 2 * KD)
            for n in range(2):
                pe.wait_ge(*full_at(out_chunk + n))
                if n == 1:
                    pe.wait_ge(up_taken, 3 * KD)
                w = slot(out_chunk + n, KD)
                for a in range(TT):
                    for k in range(KD):
                        ins = pe.matmul(bank[:, 2 * n + a, :], mergedT[:, k, a * P:(a + 1) * P], w[:, k, :],
                                        start=(k == 0), stop=(k == KD - 1))
                    ins.then_inc(out_done, 1)
            pe.wait_ge(xn2_ready, TT)
            pe.wait_ge(a_ready, TT)
            turn_rows(turned2)
            pe.wait_ge(h_ready, TT)
            for b in range(4):
                pe.matmul(bank[:, b, :], zeros[:, 0:P], zeros[:, :], start=True, stop=True)
            pe.wait_ge(turn2_a, 2)
            pe.wait_ge(turn2_d, 2)
            for a in range(TT):
                for k in range(KD):
                    ins = pe.matmul(bank[:, SC, a * E:(a + 1) * E], xnT[:, k, a * P:(a + 1) * P], rw[:, k, :],
                                    start=(k == 0), stop=(k == KD - 1))
            ins.then_inc(routed, 1)
            pe.wait_ge(chosen_ready, 1)
            chosen = rt[:, 13, :]
            pe.matmul(bank[:, SC, 0:E], before[:, :], chosen[:, 0:E], start=True, stop=True)
            pe.matmul(bank[:, SC, E:2 * E], before[:, :], chosen[:, E:2 * E], start=True, stop=False)
            pe.matmul(bank[:, SC, E:2 * E], ones[:, :], chosen[:, 0:E], start=False, stop=True)
            pe.matmul(bank[:, SC + 1, 0:E], ones[:, :], chosen[:, 0:E], start=True, stop=False)
            pe.matmul(bank[:, SC + 1, 0:E], ones[:, :], chosen[:, E:2 * E], start=False, stop=True)\
              .then_inc(pos_done, 1)

            def expert_pass(s, n, p, i):
                def landed(j):
                    c = NC + j
                    if i is None:
                        pe.wait_ge(slot_full[c % RING], 16 * p + 16 * (c // RING + 1))
                    return c

                pe.wait_ge(s["sel"], 2 * n + 1 + 1)
                for b in range(2):
                    pe.wait_ge(s["ye_d" if b else "ye_a"], n + 1)
                    for k in range(4):
                        for a in range(TT):
                            ins = pe.matmul(bank[:, 4 + b, k * P:(k + 1) * P],
                                            xn[:, a, (4 * b + k) * P:(4 * b + k + 1) * P],
                                            sel[:, a * 2 * J:(a + 1) * 2 * J], start=(a == 0), stop=(a == TT - 1))
                    ins.then_inc(s["gathered"], 1)
                for e in range(2):
                    if e == 0:
                        pe.wait_ge(s["xg_a"], n + 1 + 1)
                        pe.wait_ge(s["xg_d"], n + 1 + 1)
                    pe.wait_ge(s["y_d" if e else "y_a"], n + 1)
                    for m in range(2):
                        w = slot(landed(2 * e + m), KD)
                        for f in range(KF):
                            for k in range(KD):
                                ins = pe.matmul(bank[:, 6 + e, (KF * m + f) * J:(KF * m + f + 1) * J],
                                                w[:, k, f * P:(f + 1) * P], xgT[:, k, e * J:(e + 1) * J],
                                                start=(m == 0 and f == 0 and k == 0),
                                                stop=(k == KD - 1), skip_group_check=True)
                    ins.then_inc(s["h_done"], 1)
                pe.wait_ge(s["sel"], 2 * n + 2 + 1)
                for a in range(TT):
                    ins = pe.transpose(bank[:, 4, a * P:(a + 1) * P], gated[:, a * 2 * J:(a + 1) * 2 * J], ident[:, :])
                ins.then_inc(s["gt_turned"], 1)
                for e in range(2):
                    w = slot(landed(4 + e), KF)
                    pe.wait_ge(s["he"], 2 * n + e + 1 + 1)
                    for d in range(KD):
                        for f in range(KF):
                            ins = pe.matmul(bank[:, 6 + e, d * J:(d + 1) * J], w[:, f, d * P:(d + 1) * P],
                                            heT[:, e, f * J:(f + 1) * J], start=(d == 0 and f == 0),
                                            stop=(f == KF - 1), skip_group_check=True)
                    ins.then_inc(s["y_done"], 1)
                pe.wait_ge(s["gt"], n + 1 + 1)
                pe.wait_ge(s["y_a"], n + 1 + 1)
                pe.wait_ge(s["y_d"], n + 1 + 1)
                for b in range(2):
                    for k in range(4):
                        ins = pe.transpose(bank[:, 4 + b, k * P:(k + 1) * P], yeT[:, 4 * b + k, :], ident[:, :])
                    ins.then_inc(s["ye_turned"], 1)
                for b in range(2):
                    pe.wait_ge(s["ye_d" if b else "ye_a"], n + 1 + 1)
                    for a in range(TT):
                        ins = pe.matmul(bank[:, 2 * b + a, :], gatedT[:, a * P:(a + 1) * P],
                                        ye[:, b * 512:(b + 1) * 512], start=False, stop=False, skip_group_check=True)
                ins.then_inc(s["scattered"], 1)

            run_pairs(pe, expert_pass)


_INS = ["x", "norm_mix_gain", "w_in", "gmlp_w_s", "gmlp_b_s", "gmlp_v_gain", "diff_lambda", "diff_subln_gain",
        "w_up_a", "w_up_b", "w_up_c", "w_out", "norm_ffn_gain", "router_w", "router_bias",
        "moe_w1", "moe_w3", "moe_w2", "final_gain"]


def kernel(**inputs):
    import numpy as np
    import concourse.bacc as bacc
    from concourse.bass_utils import run_bass_kernel_spmd as run

    nc = bacc.Bacc("TRN2", target_bir_lowering=False, num_devices=1)
    arrays, args = {}, []
    for name in _INS:
        a = np.ascontiguousarray(inputs[name])
        arrays["in_" + name] = a
        args.append(nc.dram_tensor("in_" + name, a.shape, mybir.dt.from_np(a.dtype), kind="ExternalInput").ap())
    args.append(nc.dram_tensor("out_0", inputs["x"].shape, F32, kind="ExternalOutput").ap())
    trunk(nc, *args)
    r = run(nc, [arrays], core_ids=[0])
    return r.results[0]["out_0"]
```

```python
from contextlib import ExitStack

import concourse.bass as bass
import concourse.mybir as mybir

F32 = mybir.dt.float32
F32R = mybir.dt.float32r
BF16 = mybir.dt.bfloat16
I32 = mybir.dt.int32
ALU = mybir.AluOpType
ACT = mybir.ActivationFunctionType
AX = mybir.AxisListType

P = 128
EPS = 1e-6
LAMBDA_INIT = 0.8 - 0.6
MASKED = -1e30


def trunk(nc, x, norm_mix_gain, w_in, gmlp_w_s, gmlp_b_s, gmlp_v_gain, diff_lambda, diff_subln_gain,
          w_up_a, w_up_b, w_up_c, w_out, norm_ffn_gain, router_w, router_bias,
          moe_w1, moe_w3, moe_w2, final_gain, out):
    T, D = x.shape[1], x.shape[2]
    TT, KD = T // P, D // P
    NG = gmlp_w_s.shape[1]
    AW = NG * P
    BH, BQ = 4, 64
    CH, CD = 8, 64
    E = router_w.shape[1]
    EG = 4
    NGR = E // EG
    F = moe_w1.shape[3]
    KF = F // P
    PAIRS = E // 2
    J = 64
    W3 = 3 * P
    B_SCALE, C_SCALE = BQ ** -0.5, CD ** -0.5
    SLOPES = [(2.0 ** (-8.0 / BH)) ** (i + 1) for i in range(BH)]

    RING, MIX_RING = 6, 4
    CW = 512
    UA, VA, QB, KB, VB, QC, KC, VC = range(8)
    PROJ = [QB, KB, VB, QC, KC, VC, VA, UA]
    BRANCHES = [("B", 10, w_up_b), ("C", 12, w_up_c), ("A", 8, w_up_a)]
    w_in_v = w_in[0].rearrange("(k p) n -> p k n", p=P)
    w_out_v = w_out[0].rearrange("(k p) n -> p k n", p=P)
    chunks = [w_in_v[:, :, c * CW:(c + 1) * CW] for c in PROJ]
    gate_chunk, up_chunk = {}, {}
    for name, c0, up in BRANCHES:
        gate_chunk[name] = (len(chunks), len(chunks) + 2)
        up_chunk[name] = len(chunks) + 1
        chunks += [w_in_v[:, :, c0 * CW:(c0 + 1) * CW], up[0].rearrange("(k p) n -> p k n", p=P),
                   w_in_v[:, :, (c0 + 1) * CW:(c0 + 2) * CW]]
    out_chunk = len(chunks)
    chunks += [w_out_v[:, :, n * CW:(n + 1) * CW] for n in range(D // CW)]
    NC = len(chunks)
    w_in_order = [i for i in range(out_chunk) if i not in up_chunk.values()]
    HALF = CW // 2
    NH = 2 * len(w_in_order)
    assert RING == 6 and D // CW == 2 and F == CW

    TIMELINE = [("proj", (0, 0)), ("proj", (0, 1)), ("proj", (1, 0)), ("proj", (1, 1)), ("b_scores", 0),
                ("proj", (2, 0)), ("b_combine", 0), ("proj", (2, 1))]
    for h in range(BH - 1):
        TIMELINE += [("b_turn", h), ("b_scores", h + 1), ("proj", (3 + h, 0)), ("b_values", h),
                     ("b_combine", h + 1), ("proj", (3 + h, 1))]
    TIMELINE += [("b_turn", BH - 1), ("c_scores", 0), ("c_scores", 1), ("c_keep", 0), ("c_keep", 1),
                 ("proj", (6, 0)), ("b_values", BH - 1)]
    for q in range(3):
        TIMELINE += [("c_sums", 2 * q), ("c_sums", 2 * q + 1), ("c_scores", 2 * q + 2), ("c_scores", 2 * q + 3),
                     ("c_logits", 2 * q), ("c_logits", 2 * q + 1), ("c_keep", 2 * q + 2), ("c_keep", 2 * q + 3)]
        if q == 0:
            TIMELINE += [("b_norm", 0), ("proj", (6, 1)), ("b_done", 0)]
        else:
            TIMELINE += [("proj", (7, q - 1))]
        TIMELINE += [("c_values", 2 * q), ("c_values", 2 * q + 1)]
    TIMELINE += [("c_sums", 6), ("c_sums", 7), ("c_logits", 6), ("c_logits", 7), ("a_gelu", 0), ("gate", (0, 0)),
                 ("c_values", 6), ("c_values", 7), ("gate", (0, 1)), ("gate", (0, 2)), ("a_mix", 0)]
    TIMELINE += [("gate", (0, d)) for d in range(3, KD)]
    TIMELINE += [("gate", (b, d)) for b in (1, 2) for d in range(KD)]

    with ExitStack() as ctx:
        def sb(name, shape, dt=F32):
            return ctx.enter_context(nc.sbuf_tensor(name, shape, dt))

        def sem(name):
            return ctx.enter_context(nc.semaphore(name))

        base = (nc.sbuf_base + 31) // 32 * 32
        ring_slab = sb("ring_slab", [P, (MIX_RING + 2) * 4096 + 2 * 2048])
        SLOT = 4096 * 4

        def at(name, shape, offset, dt=F32R):
            return nc.alloc_sbuf_tensor_at(name, shape, dt, offset=base + offset)

        ring = at("ring", [P, RING, 4096], 0, F32)
        shared = MIX_RING * SLOT
        w_hi = [at(f"w_hi{b}", [P, KD, HALF], shared + b * SLOT // 2) for b in range(2)]
        w_lo = [at(f"w_lo{b}", [P, KD, HALF], shared + SLOT + b * SLOT // 2) for b in range(2)]
        x_hi = at("x_hi", [P, KD, T], shared + 2 * SLOT)
        x_lo = at("x_lo", [P, KD, T], shared + 2 * SLOT + SLOT // 2)
        xnT = at("xnT", [P, KD, T], shared + 2 * SLOT, F32)
        h_sb = sb("h_sb", [P, TT, D])
        xn = sb("xn", [P, TT, D])
        mergedT = xn[:, :, :].rearrange("p a (b t) -> p (a b) t", t=T)
        work = sb("work", [P, 8192])
        qbT = work[:, 0:1024].rearrange("p (h t) -> p h t", t=T)
        kbT = work[:, 1024:2048].rearrange("p (h t) -> p h t", t=T)
        vb = work[:, 2048:3072].rearrange("p (a n) -> p a n", a=TT)
        qcT = work[:, 3072:4096].rearrange("p (h t) -> p h t", t=T)
        kcT = work[:, 4096:5120].rearrange("p (h t) -> p h t", t=T)
        vc = work[:, 5120:6144].rearrange("p (a n) -> p a n", a=TT)
        va = work[:, 6144:7168].rearrange("p (a n) -> p a n", a=TT)
        uT = work[:, 7168:8192].rearrange("p (g t) -> p g t", t=T)
        yT = {"A": uT, "B": qbT, "C": qcT}
        xgT = work[:, 0:1024].rearrange("p (k j) -> p k j", j=2 * J)
        silu = work[:, 1024:1024 + F]
        he = work[:, 1536:1536 + F]
        ye = work[:, 2048:3072]
        heT = work[:, 3072:3584].rearrange("p (f j) -> p f j", j=2 * J)
        sel = work[:, 4096:4352]
        gated = work[:, 4352:4608]
        gatedT = work[:, 4608:4864]
        scratch = work[:, 6144:7168]

        gain = sb("gain", [P, D])
        v_gain = sb("v_gain", [P, AW])
        sub_gain = sb("sub_gain", [P, 1])
        lam_in = sb("lam_in", [P, 4, BQ])
        b_row = sb("b_row", [1, NG * P])
        rw = sb("rw", [P, KD, E])
        rbias = sb("rbias", [P, E])
        wsT = sb("wsT", [P, NG, P])
        ident = sb("ident", [P, P])
        ones = sb("ones", [P, P])
        from_here = sb("from_here", [P, P])
        before = sb("before", [P, P])
        zeros = sb("zeros", [P, 512], BF16)
        b_bias = sb("b_bias", [P, BH, W3])
        c_mask = sb("c_mask", [P, W3])
        iota_i = sb("iota_i", [P, T], I32)
        iota = sb("iota", [P, T])
        prob = sb("prob", [P, 4, W3])
        diff = sb("diff", [P, 2, W3])
        diffT = sb("diffT", [P, 2, W3])
        dist = diffT[:, 0, :]
        dist_i = diffT[:, 1, :].bitcast(I32)
        o_b = sb("o_b", [P, TT, BH, P])
        ws = o_b[:, 0, :, :]
        gate = sb("gate", [P, 2, T])
        gated_up = sb("gated_up", [P, 2, T])
        st = sb("st", [P, 128])
        rt = work[:, 4864:4864 + 20 * TT * E].rearrange("p (r n) -> p r n", n=TT * E)
        tab = sb("tab", [P, 64])
        tab_i = sb("tab_i", [1, 2, PAIRS], I32)

        bank = ctx.enter_context(nc.psum_tensor("bank", [P, 8, 512], F32))
        PJ, UP, SC, TR, OV = 0, 2, 4, 6, 7

        slot_full = [sem(f"slot_full{s}") for s in range(RING)]
        ld_x, ld_gain, ld_small, ld_ws, ld_final = (sem(n) for n in
                                                    ("ld_x", "ld_gain", "ld_small", "ld_ws", "ld_final"))
        consts_pool, consts_dve = sem("consts_pool"), sem("consts_dve")
        pool_step = sem("pool_step")
        ws_masked = sem("ws_masked")
        bias_scaled, bias_masked = sem("bias_scaled"), sem("bias_masked")
        act_stat, dve_stat = sem("act_stat"), sem("dve_stat")
        xn_ready = sem("xn_ready")
        turned = sem("turned")
        turn_taken_a, turn_taken_d = sem("turn_taken_a"), sem("turn_taken_d")
        ws_turned, wsT_ready = sem("ws_turned"), sem("wsT_ready")
        w_hi_ready, w_lo_ready = sem("w_hi_ready"), sem("w_lo_ready")
        proj_done = sem("proj_done")
        pj_taken = [sem("pj_taken0"), sem("pj_taken1")]
        b_scored, b_max, b_exp, b_comb, b_diff, b_turned, b_turn_taken = (
            sem(n) for n in ("b_scored", "b_max", "b_exp", "b_comb", "b_diff", "b_turned", "b_turn_taken"))
        b_ov, b_ov_a, b_ov_d, b_normed, b_nturned, b_ready = (
            sem(n) for n in ("b_ov", "b_ov_a", "b_ov_d", "b_normed", "b_nturned", "b_ready"))
        c_scored, c_z, c_ln, c_sp, c_summed, c_lo, c_prob, c_ov, c_ready = (
            sem(n) for n in ("c_scored", "c_z", "c_ln", "c_sp", "c_summed", "c_lo", "c_prob", "c_ov", "c_ready"))
        c_abs = sem("c_abs")
        a_gelu, a_vn, a_mixed, a_ready = (sem(n) for n in ("a_gelu", "a_vn", "a_mixed", "a_ready"))
        up_done, gate_sig, up_taken, merged = (sem(n) for n in ("up_done", "gate_sig", "up_taken", "merged"))
        out_done, h_ready = sem("out_done"), sem("h_ready")
        xn2_ready, turned2, turn2_a, turn2_d = (sem(n) for n in ("xn2_ready", "turned2", "turn2_a", "turn2_d"))
        routed, aff_exp, masked, chosen_ready, pos_done, table = (
            sem(n) for n in ("routed", "aff_exp", "masked", "chosen_ready", "pos_done", "table"))
        stored = sem("stored")
        fences = sem("fences")

        NAMES = ("sel", "gathered", "xg", "h_done", "silu", "he", "gt_turned", "gt", "he_turned", "heT",
                 "y_done", "ye_a", "ye_d", "scattered")
        main = {n: sem("m_" + n) for n in NAMES}
        more = {n: sem("o_" + n) for n in NAMES}

        def full_at(i):
            return slot_full[i % MIX_RING], 16 * (i // MIX_RING + 1)

        def half_read(q):
            n = q - 2 * len(PROJ)
            return proj_done, q + 1 if n < 0 else 2 * len(PROJ) + 2 * (n + 1)

        def w_half(q):
            return slot(w_in_order[q // 2], KD)[:, :, (q % 2) * HALF:(q % 2 + 1) * HALF]

        def read_at(i):
            if i >= out_chunk:
                return out_done, TT * (i - out_chunk + 1)
            if i in w_in_order:
                return w_lo_ready, 2 * w_in_order.index(i) + 2
            return up_done, KD * ((i - len(PROJ)) // 3 + 1)

        def slot(i, k):
            return ring[:, i % MIX_RING, :].rearrange("p (k n) -> p k n", k=k)

        def e_slot(j, k):
            return ring[:, j, :].rearrange("p (k n) -> p k n", k=k)

        SS, MS, RS = 0, 8, 16
        LAMP, LAME, NLAM = 24, 26, 28
        NMAX, SUM, COEF = 32, 40, 48
        SSB, MSB, RSB = 56, 64, 72
        SSV, MSV, RSV = 80, 82, 84

        def col(c, n=1):
            return st[:, c:c + n]

        mix_scratch = o_b[:, :, :, :].rearrange("p a h n -> p (a h n)")[:, 0:AW]
        sub_gain_scaled = st[:, 90:91]

        def proj_dst(c, half):
            dst = {UA: uT, VA: va, QB: qbT, KB: kbT, VB: vb, QC: qcT, KC: kcT, VC: vc}[PROJ[c]]
            if PROJ[c] in (VA, VB, VC):
                return dst[:, :, half * HALF:(half + 1) * HALF]
            return dst[:, 2 * half:2 * half + 2, :]

        def bank_view(c, half):
            return bank[:, PJ + half, :].rearrange("p (h t) -> p h t", t=T)

        def run_pairs(eng, expert_pass):
            with eng.Fori(0, PAIRS) as p:
                expert_pass(main, p, p, None)
                eng.wait_ge(table, 1)
                again = eng.value_load(tab_i[0:1, 0, bass.ds(p, 1)], min_val=0, max_val=3)
                with eng.If(again > 0):
                    base = eng.value_load(tab_i[0:1, 1, bass.ds(p, 1)], min_val=0, max_val=3 * PAIRS)
                    eng.wait_ge(main["scattered"], p + 2)
                    eng.sem_inc(fences, 1)
                    with eng.Fori(0, again) as i:
                        expert_pass(more, base + i, p, i)
                    eng.wait_ge(more["scattered"], base + again + 1)
                    eng.sem_inc(fences, 1)
                with eng.Else():
                    eng.nop()

        block = ctx.enter_context(nc.Block())

        @block.sync
        def _(sp):
            sp.dma_start(h_sb[:, :, :], x[0].rearrange("(a p) d -> p a d", p=P)).then_inc(ld_x, 16)
            for n in NAMES:
                sp.sem_inc(main[n], 1)
                sp.sem_inc(more[n], 1)
            for i in range(NC):
                if i >= MIX_RING:
                    sp.wait_ge(*read_at(i - MIX_RING))
                sp.dma_start(ring[:, i % MIX_RING, :].rearrange("p (k n) -> p k n", n=chunks[i].shape[2]),
                             chunks[i]).then_inc(slot_full[i % MIX_RING], 16)

            def expert_chunk(j, e):
                s = j
                src = (moe_w1, moe_w3, moe_w2)[j // 2]
                idx = e + j % 2
                sp.dma_start(ring[:, s, :].rearrange("p (k n) -> p k n", n=src.shape[3]),
                             src[0, idx].rearrange("(k p) n -> p k n", p=P)).then_inc(slot_full[s], 16)

            for j in range(RING):
                if j < MIX_RING:
                    sp.wait_ge(*read_at(max(i for i in range(NC) if i % MIX_RING == j)))
                else:
                    sp.wait_ge(*half_read(NH - 1))
                expert_chunk(j, 0)
            sp.wait_ge(table, 1)
            with sp.Fori(0, PAIRS - 1) as p:
                again = sp.value_load(tab_i[0:1, 0, bass.ds(p, 1)], min_val=0, max_val=3)

                def next_pair(s, passes):
                    for j in range(RING):
                        if j % 2 == 0:
                            sp.wait_ge(s["y_done"] if j == 4 else s["h_done"], 2 * passes + (0 if j == 0 else 1))
                        expert_chunk(j, 2 * p + 2)

                with sp.If(again > 0):
                    base = sp.value_load(tab_i[0:1, 1, bass.ds(p, 1)], min_val=0, max_val=3 * PAIRS)
                    next_pair(more, base + again)
                with sp.Else():
                    next_pair(main, p + 1)
                sp.nop()
            for a in range(TT):
                sp.wait_ge(h_ready, 2 * TT + a + 1)
                sp.dma_start(out[0, a * P:(a + 1) * P, :], xn[:, a, :]).then_inc(stored, 16)
            sp.wait_ge(stored, 16 * TT)

        @block.gpsimd
        def _(pool):
            def rows(ap):
                return ap.partition_broadcast(P)

            pool.dma_start(gain[:, :], rows(norm_mix_gain[0])).then_inc(ld_gain, 16)
            pool.dma_start(ws, gmlp_w_s[0].rearrange("g t s -> t g s")).then_inc(ld_ws, 16)
            small = [(lam_in[:, :, :], rows(diff_lambda[0])), (v_gain[:, :], rows(gmlp_v_gain[0])),
                     (sub_gain[:, :], diff_subln_gain[0].rearrange("(p a) -> p a", a=1)),
                     (b_row[:, :], gmlp_b_s[0:1].rearrange("a g t -> a (g t)")),
                     (rw[:, :, :], router_w.rearrange("(k p) e -> p k e", p=P)),
                     (rbias[:, :], rows(router_bias))]
            for dst, src in small:
                pool.dma_start(dst, src).then_inc(ld_small, 16)
            pool.memset(ident[:, :], 0.0).then_inc(pool_step, 1)
            pool.memset(ones[:, :], 1.0).then_inc(pool_step, 1)
            pool.memset(c_mask[:, :], 0.0).then_inc(pool_step, 1)
            pool.memset(zeros[:, :], 0.0).then_inc(pool_step, 1)
            pool.iota(dist_i[:, 0:P], pattern=[[-1, P]], base=0, channel_multiplier=1).then_inc(pool_step, 1)
            pool.iota(dist_i[:, P:W3], pattern=[[-1, 2 * P]], base=P, channel_multiplier=1).then_inc(pool_step, 1)
            pool.iota(iota_i[:, :], pattern=[[1, T]], base=0, channel_multiplier=0).then_inc(pool_step, 1)
            pool.wait_ge(pool_step, 7)
            pool.affine_select(out=ident[:, :], in_=ident[:, :], compare_op=ALU.not_equal, fill=1.0, base=0,
                               pattern=[[-1, P]], channel_multiplier=1).then_inc(consts_pool, 1)
            pool.affine_select(out=from_here[:, :], in_=ones[:, :], compare_op=ALU.is_ge, fill=0.0, base=0,
                               pattern=[[-1, P]], channel_multiplier=1).then_inc(consts_pool, 1)
            pool.affine_select(out=before[:, :], in_=ones[:, :], compare_op=ALU.is_gt, fill=0.0, base=0,
                               pattern=[[1, P]], channel_multiplier=-1).then_inc(consts_pool, 1)
            for c in (0, 2):
                pool.affine_select(out=c_mask[:, c * P:(c + 1) * P], in_=c_mask[:, c * P:(c + 1) * P],
                                   compare_op=ALU.is_gt, fill=MASKED, base=0, pattern=[[1, P]],
                                   channel_multiplier=-1).then_inc(consts_pool, 1)
            pool.wait_ge(ld_ws, 16)
            pool.affine_select(out=ws, in_=ws, compare_op=ALU.is_ge, fill=0.0, base=0,
                               pattern=[[0, NG], [-1, P]], channel_multiplier=1).then_inc(ws_masked, 1)
            pool.wait_ge(bias_scaled, BH)
            pool.affine_select(out=b_bias[:, :, 0:P], in_=b_bias[:, :, 0:P], compare_op=ALU.is_ge, fill=MASKED,
                               base=0, pattern=[[0, BH], [-1, P]], channel_multiplier=1).then_inc(bias_masked, 1)
            pool.affine_select(out=b_bias[:, :, P:W3], in_=b_bias[:, :, P:W3], compare_op=ALU.is_ge, fill=MASKED,
                               base=P, pattern=[[0, BH], [-1, 2 * P]], channel_multiplier=1).then_inc(bias_masked, 1)
            pool.wait_ge(xn_ready, TT)
            pool.dma_start(gain[:, :], rows(norm_ffn_gain[0])).then_inc(ld_gain, 16)
            for q in range(NH):
                i = w_in_order[q // 2]
                pool.wait_ge(*full_at(i))
                pool.wait_ge(w_hi_ready, q + 1)
                if q >= 2:
                    pool.wait_ge(*half_read(q - 2))
                pool.tensor_tensor(w_lo[q % 2][:, :, :], w_half(q), w_hi[q % 2][:, :, :].bitcast(F32),
                                   ALU.subtract).then_inc(w_lo_ready, 1)
            pool.wait_ge(xn2_ready, TT)
            pool.dma_start(gain[:, :], rows(final_gain)).then_inc(ld_final, 16)

        @block.scalar
        def _(act):
            def square_sum(src, dst, width):
                act.activation(scratch_of(width), src, ACT.Square, accum_out=dst).then_inc(act_stat, 1)

            def scratch_of(width):
                return scratch[:, 0:width]

            def sqrt(dst, src, need):
                act.wait_ge(dve_stat, need)
                act.activation(dst, src, ACT.Sqrt).then_inc(act_stat, 1)

            act.wait_ge(ld_x, 16)
            for a in range(TT):
                if a:
                    act.wait_ge(act_stat, a)
                square_sum(h_sb[:, a, :], col(SS + a), D)
            sqrt(col(RS, TT), col(MS, TT), 2)
            for g in range(4):
                act.wait_ge(turned, g + 1)
                act.activation(x_hi[:, 2 * g:2 * g + 2, :], bank[:, SC + g, :].rearrange("p (k t) -> p k t", t=T),
                               ACT.Copy).then_inc(turn_taken_a, 1)

            act.preload_act_table_set("natural_log_exp_and_others")

            def proj(c, half):
                if half or PROJ[c] in (UA, VA):
                    return
                act.wait_ge(proj_done, 2 * c + 1)
                act.activation(proj_dst(c, half), bank_view(c, half), ACT.Copy).then_inc(pj_taken[0], 1)

            def b_scores(h):
                q = h % 2
                act.wait_ge(b_max, h + 1)
                for m in range(2):
                    for blk, (lo, hi) in enumerate(((0, P), (P, W3))):
                        act.activation(prob[:, 2 * q + m, lo:hi], prob[:, 2 * q + m, lo:hi], ACT.Exp,
                                       bias=col(NMAX + 4 * q + 2 * blk + m),
                                       accum_out=col(SUM + 4 * q + 2 * blk + m)).then_inc(b_exp, 1)
                if h == 0:
                    act.wait_ge(dve_stat, 4)
                    act.activation(col(LAME, 2), col(LAMP, 2), ACT.Exp).then_inc(act_stat, 1)

            def b_turn(h):
                act.wait_ge(b_turned, h + 1)
                if h >= 2:
                    act.wait_ge(b_ov, h - 1)
                act.activation(diffT[:, h % 2, :], bank[:, TR, 0:W3], ACT.Copy).then_inc(b_turn_taken, 1)

            def b_values(h):
                act.wait_ge(b_ov_d, h + 1)
                for a in range(TT):
                    if h or a:
                        act.wait_ge(b_ov_a, TT * h + a)
                    act.activation(gate[:, 0, 0:P], o_b[:, a, h, :], ACT.Square,
                                   accum_out=col(SSB + BH * a + h)).then_inc(b_ov_a, 1)

            def b_norm(_):
                sqrt(col(RSB, TT * BH), col(MSB, TT * BH), 6)

            def b_done(_):
                act.preload_act_table_set("natural_log_exp_and_others")
                act.wait_ge(consts_dve, 4)
                act.wait_ge(b_nturned, 1)
                act.activation(yT["B"][:, 0:2, :], bank[:, TR, :].rearrange("p (h t) -> p h t", t=T), ACT.Copy,
                               scale=sub_gain_scaled).then_inc(b_ready, 1)

            def c_keep(h):
                act.wait_ge(c_z, h + 1)
                w = diff[:, h % 2, :]
                if h >= 2:
                    act.wait_ge(c_summed, h - 1)
                act.activation(w, prob[:, h % 4, :], ACT.Abs).then_inc(c_abs, 1)
                act.wait_ge(c_abs, 3 * h + 1)
                act.activation(w, w, ACT.Exp, scale=-1.0).then_inc(c_abs, 1)
                act.wait_ge(c_abs, 3 * h + 2)
                act.activation(w, w, ACT.Ln, bias=1.0).then_inc(c_abs, 1)

            def c_logits(h):
                act.wait_ge(c_lo, h + 1)
                act.activation(prob[:, h % 4, :], prob[:, h % 4, :], ACT.Exp).then_inc(c_prob, 1)

            def c_values(h):
                if h % 2:
                    act.wait_ge(c_ov, h + 1)
                    t = h // 2
                    act.activation(yT["C"][:, t, :], bank[:, OV, (t % 2) * T:(t % 2 + 1) * T],
                                   ACT.Copy).then_inc(c_ready, 1)

            def a_gelu_(_):
                act.wait_ge(pj_taken[0], 8)
                act.wait_ge(pj_taken[1], 8)
                for a in range(TT):
                    act.activation(va[:, a, :], va[:, a, :], ACT.Gelu_apprx_tanh).then_inc(a_gelu, 1)
                act.activation(uT[:, :, :], uT[:, :, :], ACT.Gelu_apprx_tanh).then_inc(a_gelu, 1)
                act.wait_ge(a_gelu, TT)
                for a in range(TT):
                    if a:
                        act.wait_ge(act_stat, 6)
                    act.activation(mix_scratch, va[:, a, :], ACT.Square,
                                   accum_out=col(SSV + a)).then_inc(act_stat, 1)
                sqrt(col(RSV, TT), col(MSV, TT), 8)

            def gate_(b, d):
                n = KD * b + d
                act.wait_ge(proj_done, 16 + n + 1)
                if n >= 2:
                    act.wait_ge(up_taken, n - 1)
                act.activation(gate[:, n % 2, :], bank[:, PJ + n % 2, 0:T], ACT.Sigmoid)\
                   .then_inc(pj_taken[n % 2], 1)

            STEPS = {"proj": lambda i: proj(*i), "b_scores": b_scores, "b_turn": b_turn, "b_values": b_values,
                     "b_norm": b_norm, "b_done": b_done, "c_keep": c_keep, "c_logits": c_logits,
                     "c_values": c_values, "a_gelu": a_gelu_, "gate": lambda i: gate_(*i)}
            for step, i in TIMELINE:
                if step in STEPS:
                    STEPS[step](i)

            act.wait_ge(merged, 2 * KD)
            for a in range(TT):
                act.wait_ge(h_ready, a + 1)
                act.wait_ge(act_stat, 8 + a)
                square_sum(h_sb[:, a, :], col(SS + a), D)
            sqrt(col(RS, TT), col(MS, TT), 10)
            for g in range(2):
                act.wait_ge(turned2, g + 1)
                act.activation(xnT[:, 2 * g:2 * g + 2, :], bank[:, SC + g, :].rearrange("p (k t) -> p k t", t=T),
                               ACT.Copy).then_inc(turn2_a, 1)
            act.wait_ge(routed, 1)
            act.activation(rt[:, 0, :], bank[:, SC, 0:TT * E], ACT.Exp, scale=-1.0).then_inc(aff_exp, 1)

            def expert_pass(s, n, p, i):
                act.wait_ge(s["h_done"], 2 * n + 2)
                act.wait_ge(s["he"], n + 1)
                act.activation(silu, bank[:, 6, :], ACT.Silu).then_inc(s["silu"], 1)
                act.wait_ge(s["gt_turned"], n + 2)
                act.wait_ge(s["scattered"], n + 1)
                act.activation(gatedT, bank[:, 5, 0:T], ACT.Copy).then_inc(s["gt"], 1)
                act.wait_ge(s["he_turned"], n + 2)
                act.wait_ge(s["y_done"], 2 * n + 1)
                act.activation(heT[:, :, :], bank[:, 4, :].rearrange("p (f j) -> p f j", j=2 * J),
                               ACT.Copy).then_inc(s["heT"], 1)
                act.wait_ge(s["y_done"], 2 * n + 2)
                act.activation(ye[:, 0:512], bank[:, 6, :], ACT.Copy).then_inc(s["ye_a"], 1)

            act.preload_act_table_set("silu_and_others")
            run_pairs(act, expert_pass)
            for a in range(TT):
                act.wait_ge(h_ready, TT + a + 1)
                act.wait_ge(act_stat, 11 + a)
                square_sum(h_sb[:, a, :], col(SS + a), D)
            sqrt(col(RS, TT), col(MS, TT), 12)

        @block.vector
        def _(dve):
            n_stat = [0]

            def stat(ins):
                n_stat[0] += 1
                ins.then_inc(dve_stat, 1)
                dve.wait_ge(dve_stat, n_stat[0])

            def mean_inverse(dst, src, width):
                stat(dve.tensor_scalar(dst, src, 1.0 / width, EPS, ALU.mult, ALU.add))
                stat(dve.reciprocal(dst, dst))

            def split(q):
                if q >= NH:
                    return
                dve.wait_ge(*full_at(w_in_order[q // 2]))
                if q >= 2:
                    dve.wait_ge(*half_read(q - 2))
                dve.tensor_copy(w_hi[q % 2][:, :, :], w_half(q)).then_inc(w_hi_ready, 1)

            dve.wait_ge(act_stat, 2)
            mean_inverse(col(MS, TT), col(SS, TT), D)
            dve.wait_ge(act_stat, 3)
            dve.wait_ge(ld_gain, 16)
            for a in range(TT):
                dve.scalar_tensor_tensor(out=xn[:, a, :], in0=h_sb[:, a, :], scalar=col(RS + a),
                                         in1=gain[:, :], op0=ALU.mult, op1=ALU.mult).then_inc(xn_ready, 1)
            dve.wait_ge(pool_step, 7)
            dve.tensor_copy(dist, dist_i).then_inc(consts_dve, 1)
            dve.tensor_copy(iota[:, :], iota_i[:, :]).then_inc(consts_dve, 1)
            dve.wait_ge(consts_dve, 2)
            for h in range(BH):
                dve.tensor_scalar(b_bias[:, h, :], dist, -SLOPES[h], None, ALU.mult).then_inc(bias_scaled, 1)
            for g in range(4):
                dve.wait_ge(turn_taken_a, g + 1)
                dve.tensor_tensor(x_lo[:, 2 * g:2 * g + 2, :],
                                  bank[:, SC + g, :].rearrange("p (k t) -> p k t", t=T),
                                  x_hi[:, 2 * g:2 * g + 2, :].bitcast(F32), ALU.subtract).then_inc(turn_taken_d, 1)
                if g == 1:
                    split(0)
            split(1)
            dve.wait_ge(ws_turned, 1)
            dve.tensor_copy(wsT[:, :, :], bank[:, SC, :].rearrange("p (g t) -> p g t", t=P)).then_inc(wsT_ready, 1)

            def proj(c, half):
                split(2 * c + half + 2)
                if not half and PROJ[c] not in (UA, VA):
                    return
                dve.wait_ge(proj_done, 2 * c + half + 1)
                dve.tensor_copy(proj_dst(c, half), bank_view(c, half)).then_inc(pj_taken[half], 1)

            def b_scores(h):
                q = h % 2
                if h == 0:
                    dve.wait_ge(bias_masked, 2)
                dve.wait_ge(b_scored, h + 1)
                p2 = prob[:, 2 * q:2 * q + 2, :]
                for m in range(2):
                    dve.scalar_tensor_tensor(out=prob[:, 2 * q + m, :], in0=bank[:, SC + m, 0:W3], scalar=B_SCALE,
                                             in1=b_bias[:, h, :], op0=ALU.mult, op1=ALU.add).then_inc(b_comb, 1)
                dve.wait_ge(b_comb, 7 * h + 2)
                for blk, (lo, hi) in enumerate(((0, P), (P, W3))):
                    dve.tensor_reduce(col(NMAX + 4 * q + 2 * blk, 2), p2[:, :, lo:hi], AX.X, ALU.max)\
                       .then_inc(b_comb, 1)
                dve.wait_ge(b_comb, 7 * h + 4)
                dve.tensor_scalar(col(NMAX + 4 * q, 4), col(NMAX + 4 * q, 4), -1.0, None, ALU.mult)\
                   .then_inc(b_max, 1)

            def b_combine(h):
                q = h % 2
                if h == 0:
                    dve.wait_ge(ld_small, 16 * 6)
                    lam4 = lam_in[:, :, :].rearrange("p (a b) q -> p a b q", b=2)
                    stat(dve.tensor_tensor(gated_up[:, 0, 0:2 * BQ].rearrange("p (a q) -> p a q", q=BQ),
                                           lam4[:, :, 0, :], lam4[:, :, 1, :], ALU.mult))
                    stat(dve.tensor_reduce(col(LAMP, 2), gated_up[:, 0, 0:2 * BQ].rearrange("p (a q) -> p a q", q=BQ),
                                           AX.X, ALU.add))
                    dve.wait_ge(act_stat, 4)
                    dve.scalar_tensor_tensor(out=col(NLAM), in0=col(LAME + 1), scalar=-LAMBDA_INIT, in1=col(LAME),
                                             op0=ALU.add, op1=ALU.subtract).then_inc(consts_dve, 1)
                    dve.tensor_scalar(sub_gain_scaled, sub_gain[:, :], 1.0 - LAMBDA_INIT, None, ALU.mult)\
                       .then_inc(consts_dve, 1)
                    dve.wait_ge(consts_dve, 4)
                dve.wait_ge(b_exp, 4 * (h + 1))
                dve.reciprocal(col(COEF + 4 * q, 4), col(SUM + 4 * q, 4)).then_inc(b_comb, 1)
                dve.wait_ge(b_comb, 7 * h + 5)
                lam_cols = st[:, COEF + 4 * q + 1:COEF + 4 * q + 4:2]
                dve.tensor_scalar(lam_cols, lam_cols, col(NLAM), None, ALU.mult).then_inc(b_comb, 1)
                dve.wait_ge(b_comb, 7 * h + 6)
                if h >= 2:
                    dve.wait_ge(b_turned, h - 1)
                for blk, (lo, hi) in enumerate(((0, P), (P, W3))):
                    ins = dve.tensor_scalar(prob[:, 2 * q + 1, lo:hi], prob[:, 2 * q + 1, lo:hi],
                                            col(COEF + 4 * q + 2 * blk + 1), None, ALU.mult)
                ins.then_inc(b_comb, 1)
                dve.wait_ge(b_comb, 7 * h + 7)
                for blk, (lo, hi) in enumerate(((0, P), (P, W3))):
                    ins = dve.scalar_tensor_tensor(out=diff[:, q, lo:hi], in0=prob[:, 2 * q, lo:hi],
                                                   scalar=col(COEF + 4 * q + 2 * blk), in1=prob[:, 2 * q + 1, lo:hi],
                                                   op0=ALU.mult, op1=ALU.add)
                ins.then_inc(b_diff, 1)

            def b_values(h):
                dve.wait_ge(b_ov, h + 1)
                dve.tensor_copy(o_b[:, :, h, :], bank[:, OV, (h % 2) * T:(h % 2 + 1) * T]
                                .rearrange("p (a n) -> p a n", a=TT)).then_inc(b_ov_d, 1)

            def b_norm(_):
                dve.wait_ge(b_ov_a, TT * BH)
                mean_inverse(col(MSB, TT * BH), col(SSB, TT * BH), P)
                dve.wait_ge(act_stat, 5)
                dve.wait_ge(b_ov_d, BH)
                o8 = o_b[:, :, :, :].rearrange("p a h n -> p (a h) n")
                dve.tensor_tensor(o8, o8, col(RSB, TT * BH).unsqueeze(2).to_broadcast([P, TT * BH, P]), ALU.mult)\
                   .then_inc(b_normed, 1)

            def b_done(_):
                dve.wait_ge(b_nturned, 2)
                dve.tensor_scalar(yT["B"][:, 2:4, :], bank[:, OV, :].rearrange("p (h t) -> p h t", t=T),
                                  sub_gain_scaled, None, ALU.mult).then_inc(b_ready, 1)

            def c_scores(h):
                dve.wait_ge(c_scored, h + 1)
                if h == 0:
                    dve.wait_ge(consts_pool, 5)
                if h >= 4:
                    dve.wait_ge(c_ov, h - 3)
                dve.scalar_tensor_tensor(out=prob[:, h % 4, :], in0=bank[:, SC + h % 2, 0:W3], scalar=C_SCALE,
                                         in1=c_mask[:, :], op0=ALU.mult, op1=ALU.add).then_inc(c_z, 1)

            def c_keep(h):
                dve.wait_ge(c_abs, 3 * h + 3)
                w = diff[:, h % 2, :]
                dve.scalar_tensor_tensor(out=w, in0=prob[:, h % 4, :], scalar=0.0, in1=w,
                                         op0=ALU.max, op1=ALU.add).then_inc(c_sp, 1)

            def c_logits(h):
                dve.wait_ge(c_summed, h + 1)
                dve.tensor_tensor(prob[:, h % 4, :], prob[:, h % 4, :], bank[:, UP + h % 2, 0:W3],
                                  ALU.subtract).then_inc(c_lo, 1)

            def a_gelu_(_):
                dve.wait_ge(act_stat, 7)
                mean_inverse(col(MSV, TT), col(SSV, TT), AW)
                dve.wait_ge(act_stat, 8)
                for a in range(TT):
                    dve.scalar_tensor_tensor(out=va[:, a, :], in0=va[:, a, :], scalar=col(RSV + a),
                                             in1=v_gain[:, :], op0=ALU.mult, op1=ALU.mult).then_inc(a_vn, 1)

            def a_mix(_):
                dve.wait_ge(a_gelu, TT + 1)
                for a in range(TT):
                    dve.wait_ge(a_mixed, a + 1)
                    dve.tensor_tensor(uT[:, :, a * P:(a + 1) * P], uT[:, :, a * P:(a + 1) * P],
                                      bank[:, SC + a, :].rearrange("p (g t) -> p g t", t=P), ALU.mult)\
                       .then_inc(a_ready, 1)

            def gate_(b, d):
                n = KD * b + d
                if d % 2:
                    split(2 * len(PROJ) + 4 * b + d // 2 + 2)
                dve.wait_ge(pj_taken[n % 2], 8 + n // 2 + 1)
                dve.wait_ge(up_done, n + 1)
                if b == 0:
                    dve.tensor_tensor(mergedT[:, d, :], gate[:, n % 2, :], bank[:, UP + n % 2, 0:T], ALU.mult)\
                       .then_inc(up_taken, 1)
                else:
                    dve.tensor_tensor(gated_up[:, n % 2, :], gate[:, n % 2, :], bank[:, UP + n % 2, 0:T], ALU.mult)\
                       .then_inc(up_taken, 1)
                    dve.wait_ge(up_taken, n + 1)
                    if b == 2:
                        dve.wait_ge(merged, d + 1)
                    dve.tensor_tensor(mergedT[:, d, :], mergedT[:, d, :], gated_up[:, n % 2, :], ALU.add)\
                       .then_inc(merged, 1)

            STEPS = {"proj": lambda i: proj(*i), "b_scores": b_scores, "b_combine": b_combine, "b_values": b_values,
                     "b_norm": b_norm, "b_done": b_done, "c_scores": c_scores, "c_keep": c_keep,
                     "c_logits": c_logits, "a_gelu": a_gelu_, "a_mix": a_mix, "gate": lambda i: gate_(*i)}
            for step, i in TIMELINE:
                if step in STEPS:
                    STEPS[step](i)

            for a in range(TT):
                for n in range(2):
                    dve.wait_ge(out_done, 2 * n + a + 1)
                    ins = dve.tensor_tensor(h_sb[:, a, n * CW:(n + 1) * CW], h_sb[:, a, n * CW:(n + 1) * CW],
                                            bank[:, 2 * n + a, :], ALU.add)
                ins.then_inc(h_ready, 1)
            dve.wait_ge(act_stat, 10)
            mean_inverse(col(MS, TT), col(SS, TT), D)
            dve.wait_ge(act_stat, 11)
            dve.wait_ge(ld_gain, 32)
            for a in range(TT):
                dve.scalar_tensor_tensor(out=xn[:, a, :], in0=h_sb[:, a, :], scalar=col(RS + a),
                                         in1=gain[:, :], op0=ALU.mult, op1=ALU.mult).then_inc(xn2_ready, 1)
            for g in range(2):
                dve.wait_ge(turned2, 2 + g + 1)
                dve.tensor_copy(xnT[:, 4 + 2 * g:6 + 2 * g, :],
                                bank[:, TR + g, :].rearrange("p (k t) -> p k t", t=T)).then_inc(turn2_d, 1)

            n_step = [0]

            def step(ins):
                n_step[0] += 1
                ins.then_inc(masked, 1)
                dve.wait_ge(masked, n_step[0])

            def r(i):
                return rt[:, i, :]

            def by_expert(ap):
                return ap.rearrange("p (a e) -> p a e", e=E)

            def by_group(ap):
                return ap.rearrange("p (g e) -> p g e", e=EG)

            def small(i, n):
                return rt[:, i, 0:n]

            def tt(o, a, b, op):
                step(dve.tensor_tensor(o, a, b, op))

            def ts(o, a, s1, s2, op0, op1=ALU.bypass):
                step(dve.tensor_scalar(o, a, s1, s2, op0, op1))

            NGT = TT * NGR
            bias2 = rbias[:, :].unsqueeze(1).to_broadcast([P, TT, E])
            ts(tab[:, 0:E], iota[:, 0:E], -1.0, float(E), ALU.mult, ALU.add)
            dve.wait_ge(aff_exp, 1)
            ts(r(0), r(0), 1.0, None, ALU.add)
            step(dve.reciprocal(r(1), r(0)))
            tt(by_expert(r(2)), by_expert(r(1)), bias2, ALU.add)
            s4 = by_group(r(2))
            tt(small(3, NGT), s4[:, :, 0], s4[:, :, 1], ALU.max)
            tt(small(4, NGT), s4[:, :, 2], s4[:, :, 3], ALU.max)
            tt(small(5, NGT), s4[:, :, 0], s4[:, :, 1], ALU.min)
            tt(small(6, NGT), s4[:, :, 2], s4[:, :, 3], ALU.min)
            tt(small(7, NGT), small(3, NGT), small(4, NGT), ALU.max)
            tt(small(8, NGT), small(3, NGT), small(4, NGT), ALU.min)
            tt(small(9, NGT), small(5, NGT), small(6, NGT), ALU.max)
            tt(small(8, NGT), small(8, NGT), small(9, NGT), ALU.max)
            tt(small(9, NGT), small(7, NGT), small(8, NGT), ALU.add)

            def first_of_max(oh, v, n, w, m):
                def view(ap):
                    return ap.rearrange("p (a e) -> p a e", e=n)

                def wide(ap):
                    return ap.unsqueeze(2).to_broadcast([P, TT, n])
                step(dve.tensor_reduce(m, view(v), AX.X, ALU.max))
                tt(view(w), view(v), wide(m), ALU.is_equal)
                tt(view(w), view(w), tab[:, 0:n].unsqueeze(1).to_broadcast([P, TT, n]), ALU.mult)
                step(dve.tensor_reduce(m, view(w), AX.X, ALU.max))
                tt(view(oh), view(w), wide(m), ALU.is_equal)

            first_of_max(small(10, NGT), small(9, NGT), NGR, small(11, NGT), small(12, TT))
            in_group = small(10, NGT).unsqueeze(2).to_broadcast([P, NGT, EG])
            ts(small(11, NGT), small(10, NGT), -MASKED, MASKED, ALU.mult, ALU.add)
            tt(by_group(r(2)), by_group(r(2)), in_group, ALU.mult)
            tt(by_group(r(2)), by_group(r(2)), small(11, NGT).unsqueeze(2).to_broadcast([P, NGT, EG]), ALU.add)
            first_of_max(r(13), r(2), E, r(14), small(12, TT))
            step(dve.scalar_tensor_tensor(out=r(2), in0=r(13), scalar=2 * MASKED, in1=r(2),
                                          op0=ALU.mult, op1=ALU.add))
            first_of_max(r(15), r(2), E, r(14), small(12, TT))
            tt(r(13), r(13), r(15), ALU.add)
            dve.tensor_tensor(r(14), r(13), r(1), ALU.mult).then_inc(chosen_ready, 1)
            dve.wait_ge(chosen_ready, 1)
            step(dve.tensor_reduce(small(12, TT), by_expert(r(14)), AX.X, ALU.add))
            step(dve.reciprocal(small(16, TT), small(12, TT)))
            pair_order = "p (a q e) -> p a q e"
            dst17 = rt[:, 17, :].rearrange("p (q a e) -> p a q e", a=TT, e=2)
            dst18 = rt[:, 18, :].rearrange("p (q a e) -> p a q e", a=TT, e=2)
            for a in range(TT):
                ts(dst17[:, a], r(14).rearrange(pair_order, a=TT, e=2)[:, a], rt[:, 16, a:a + 1], None, ALU.mult)
            dve.wait_ge(pos_done, 1)
            tt(r(19), bank[:, SC, 0:TT * E], r(13), ALU.mult)
            for a in range(TT):
                step(dve.scalar_tensor_tensor(out=dst18[:, a], in0=r(19).rearrange(pair_order, a=TT, e=2)[:, a],
                                              scalar=-1.0, in1=r(13).rearrange(pair_order, a=TT, e=2)[:, a],
                                              op0=ALU.add, op1=ALU.add))
            step(dve.tensor_copy(tab[:, 16:16 + E], bank[:, SC + 1, 0:E]))
            tt(tab[:, 32:32 + PAIRS], tab[:, 16:16 + E:2], tab[:, 17:16 + E:2], ALU.max)
            ts(tab[:, 40:40 + PAIRS], tab[:, 32:32 + PAIRS], float(J), None, ALU.is_gt)
            for c in (2, 3):
                step(dve.scalar_tensor_tensor(out=tab[:, 40:40 + PAIRS], in0=tab[:, 32:32 + PAIRS],
                                              scalar=float(c * J), in1=tab[:, 40:40 + PAIRS],
                                              op0=ALU.is_gt, op1=ALU.add))
            step(dve.memset(tab[:, 48:49], 0.0))
            for q in range(1, PAIRS):
                tt(tab[:, 48 + q:49 + q], tab[:, 47 + q:48 + q], tab[:, 39 + q:40 + q], ALU.add)
            step(dve.tensor_copy(tab_i[0:1, 0, :], tab[0:1, 40:40 + PAIRS]))
            dve.tensor_copy(tab_i[0:1, 1, :], tab[0:1, 48:48 + PAIRS]).then_inc(table, 1)

            def expert_pass(s, n, p, i):
                dve.wait_ge(s["gathered"], 2 * n + 1)
                wide = [P, 4, J]
                cols = iota[:, 0:J] if i is None else iota[:, bass.ds(i * J + J, J)]
                pos4 = rt[:, 18, bass.ds(p * 4, 4)].unsqueeze(2).to_broadcast(wide)
                gate4 = rt[:, 17, bass.ds(p * 4, 4)].unsqueeze(2).to_broadcast(wide)
                sel4 = sel.rearrange("p (a j) -> p a j", j=J)
                gated4 = gated.rearrange("p (a j) -> p a j", j=J)
                dve.tensor_tensor(sel4, cols.unsqueeze(1).to_broadcast(wide), pos4, ALU.is_equal)\
                   .then_inc(s["sel"], 1)
                dve.wait_ge(s["sel"], 2 * n + 2)
                dve.wait_ge(s["gt_turned"], n + 1)
                dve.tensor_tensor(gated4, sel4, gate4, ALU.mult).then_inc(s["sel"], 1)
                dve.wait_ge(s["h_done"], 2 * n + 1)
                for b in range(2):
                    dve.wait_ge(s["gathered"], 2 * n + 2 + b)
                    dve.tensor_copy(xgT[:, 4 * b:4 * b + 4, :],
                                    bank[:, 4 + b, :].rearrange("p (k j) -> p k j", j=2 * J)).then_inc(s["xg"], 1)
                dve.wait_ge(s["silu"], n + 2)
                dve.wait_ge(s["h_done"], 2 * n + 3)
                dve.wait_ge(s["he_turned"], n + 1)
                dve.tensor_tensor(he, silu, bank[:, 7, :], ALU.mult).then_inc(s["he"], 1)
                dve.wait_ge(s["y_done"], 2 * n + 3)
                dve.wait_ge(s["scattered"], n + 1)
                dve.tensor_copy(ye[:, 512:1024], bank[:, 7, :]).then_inc(s["ye_d"], 1)

            run_pairs(dve, expert_pass)

            dve.wait_ge(main["scattered"], PAIRS + 1)
            for a in range(TT):
                for n in range(2):
                    ins = dve.tensor_tensor(h_sb[:, a, n * CW:(n + 1) * CW], h_sb[:, a, n * CW:(n + 1) * CW],
                                            bank[:, 2 * n + a, :], ALU.add)
                ins.then_inc(h_ready, 1)
            dve.wait_ge(act_stat, 13)
            mean_inverse(col(MS, TT), col(SS, TT), D)
            dve.wait_ge(act_stat, 14)
            dve.wait_ge(ld_final, 16)
            for a in range(TT):
                dve.scalar_tensor_tensor(out=xn[:, a, :], in0=h_sb[:, a, :], scalar=col(RS + a),
                                         in1=gain[:, :], op0=ALU.mult, op1=ALU.mult).then_inc(h_ready, 1)

        @block.tensor
        def _(pe):
            def turn_rows(done):
                for g in range(4):
                    for i in range(4):
                        k, a = 2 * g + i // 2, i % 2
                        ins = pe.transpose(bank[:, SC + g, i * P:(i + 1) * P], xn[:, a, k * P:(k + 1) * P], ident[:, :])
                    ins.then_inc(done, 1)

            pe.wait_ge(xn_ready, TT)
            pe.wait_ge(consts_pool, 5)
            turn_rows(turned)
            pe.wait_ge(turn_taken_d, 1)
            pe.wait_ge(ws_masked, 1)
            for g in range(NG):
                ins = pe.transpose(bank[:, SC, g * P:(g + 1) * P], ws[:, g, :], ident[:, :])
            ins.then_inc(ws_turned, 1)
            pe.wait_ge(turn_taken_d, 4)

            def products(dst, q, tiles, stationary_x):
                b = q % 2
                first = True
                for w, xs in ((w_hi[b], (x_hi, x_lo)), (w_lo[b], (x_hi,))):
                    if w is w_lo[b]:
                        pe.wait_ge(w_lo_ready, q + 1)
                    for i, m in enumerate(tiles):
                        for k in range(KD):
                            for xp in xs:
                                last = w is w_lo[b] and k == KD - 1
                                if stationary_x:
                                    ins = pe.matmul(dst[:, i * T:(i + 1) * T], xp[:, k, m * P:(m + 1) * P], w[:, k, :],
                                                    start=first, stop=last, skip_group_check=True)
                                else:
                                    ins = pe.matmul(dst[:, i * T:(i + 1) * T], w[:, k, m * P:(m + 1) * P], xp[:, k, :],
                                                    start=first, stop=last, skip_group_check=True)
                                first = False
                return ins

            def proj(c, half):
                q = 2 * c + half
                pe.wait_ge(w_hi_ready, q + 1)
                if c:
                    pe.wait_ge(pj_taken[half], c)
                products(bank[:, PJ + half, :], q, (0, 1), PROJ[c] in (VA, VB, VC)).then_inc(proj_done, 1)

            def b_scores(h):
                if h == 0:
                    pe.wait_ge(pj_taken[0], 2)
                    pe.wait_ge(pj_taken[1], 2)
                    pe.wait_ge(wsT_ready, 1)
                else:
                    pe.wait_ge(b_max, h)
                for m in range(2):
                    rows = slice(m * BQ, (m + 1) * BQ)
                    pe.matmul(bank[:, SC + m, 0:P], qbT[rows, h, 0:P], kbT[rows, h, 0:P], start=True, stop=True)
                    ins = pe.matmul(bank[:, SC + m, P:W3], qbT[rows, h, P:T], kbT[rows, h, :], start=True, stop=True)
                ins.then_inc(b_scored, 1)

            def b_turn(h):
                pe.wait_ge(b_diff, h + 1)
                if h >= 1:
                    pe.wait_ge(b_turn_taken, h)
                for i in range(3):
                    ins = pe.transpose(bank[:, TR, i * P:(i + 1) * P], diff[:, h % 2, i * P:(i + 1) * P], ident[:, :])
                ins.then_inc(b_turned, 1)

            def b_values(h):
                pe.wait_ge(b_turn_taken, h + 1)
                if h == 0:
                    pe.wait_ge(pj_taken[0], 3)
                    pe.wait_ge(pj_taken[1], 3)
                if h >= 1:
                    pe.wait_ge(b_ov_d, h)
                o, e = (h % 2) * T, slice(h * P, (h + 1) * P)
                pe.matmul(bank[:, OV, o:o + P], diffT[:, h % 2, 0:P], vb[:, 0, e], start=True, stop=True)
                pe.matmul(bank[:, OV, o + P:o + T], diffT[:, h % 2, P:2 * P], vb[:, 0, e], start=True, stop=False)
                pe.matmul(bank[:, OV, o + P:o + T], diffT[:, h % 2, 2 * P:W3], vb[:, 1, e], start=False, stop=True)\
                  .then_inc(b_ov, 1)

            def b_done(_):
                pe.wait_ge(b_normed, 1)
                pe.wait_ge(b_turn_taken, BH)
                for b, first in enumerate((0, 2)):
                    for i in range(4):
                        h, a = first + i // 2, i % 2
                        ins = pe.transpose(bank[:, TR + b, i * P:(i + 1) * P], o_b[:, a, h, :], ident[:, :])
                    ins.then_inc(b_nturned, 1)

            def c_scores(h):
                if h == 0:
                    pe.wait_ge(pj_taken[0], 5)
                    pe.wait_ge(pj_taken[1], 5)
                    pe.wait_ge(b_max, BH)
                if h >= 2:
                    pe.wait_ge(c_z, h - 1)
                rows, t = slice((h % 2) * CD, (h % 2 + 1) * CD), h // 2
                pe.matmul(bank[:, SC + h % 2, 0:T], kcT[rows, t, 0:P], qcT[rows, t, :], start=True, stop=True)
                pe.matmul(bank[:, SC + h % 2, T:W3], kcT[rows, t, P:T], qcT[rows, t, P:T], start=True, stop=True)\
                  .then_inc(c_scored, 1)

            def c_sums(h):
                pe.wait_ge(c_sp, h + 1)
                if h >= 2:
                    pe.wait_ge(c_lo, h - 1)
                w, b = diff[:, h % 2, :], bank[:, UP + h % 2, :]
                pe.matmul(b[:, 0:W3], from_here[:, :], w, start=True, stop=False, skip_group_check=True)
                pe.matmul(b[:, P:T], ones[:, :], w[:, T:W3], start=False, stop=True, skip_group_check=True)\
                  .then_inc(c_summed, 1)

            def c_values(h):
                pe.wait_ge(c_prob, h + 1)
                if h == 0:
                    pe.wait_ge(pj_taken[0], 6)
                    pe.wait_ge(pj_taken[1], 6)
                    pe.wait_ge(b_ready, 2)
                if h >= 2 and h % 2 == 0:
                    pe.wait_ge(c_ready, h // 2)
                rows, t = slice((h % 2) * CD, (h % 2 + 1) * CD), h // 2
                o = (t % 2) * T
                a, v = prob[:, h % 4, :], slice(h * CD, (h + 1) * CD)
                pe.matmul(bank[rows, OV, o:o + T], vc[:, 0, v], a[:, 0:T], start=True, stop=False,
                          skip_group_check=True)
                pe.matmul(bank[rows, OV, o + P:o + T], vc[:, 1, v], a[:, T:W3], start=False, stop=True,
                          skip_group_check=True).then_inc(c_ov, 1)

            def a_mix(_):
                pe.wait_ge(a_vn, TT)
                pe.wait_ge(c_z, CH)
                for a in range(TT):
                    for g in range(NG):
                        dst = bank[:, SC + a, g * P:(g + 1) * P]
                        pe.matmul(dst, va[:, a, g * P:(g + 1) * P], wsT[:, g, :], start=True, stop=False)
                        ins = pe.matmul(dst, ones[0:1, :], b_row[0:1, g * P:(g + 1) * P], start=False, stop=True)
                    ins.then_inc(a_mixed, 1)

            def gate_(b, d):
                name = BRANCHES[b][0]
                n = KD * b + d
                q, uc = 2 * len(PROJ) + 4 * b + d // 2, up_chunk[name]
                pe.wait_ge(w_hi_ready, q + 1)
                pe.wait_ge(pj_taken[n % 2], 8 + n // 2)
                products(bank[:, PJ + n % 2, 0:T], q, (d % 2,), False).then_inc(proj_done, 1)
                if d == 0:
                    pe.wait_ge(*full_at(uc))
                    pe.wait_ge(*{"A": (a_ready, TT), "B": (b_ready, 2), "C": (c_ready, CH // 2)}[name])
                if n < 2:
                    pe.wait_ge(c_lo, CH - 1 + n)
                else:
                    pe.wait_ge(up_taken, n - 1)
                w = slot(uc, 4)
                for k in range(4):
                    ins = pe.matmul(bank[:, UP + n % 2, 0:T], w[:, k, d * P:(d + 1) * P], yT[name][:, k, :],
                                    start=(k == 0), stop=(k == 3))
                ins.then_inc(up_done, 1)

            STEPS = {"proj": lambda i: proj(*i), "b_scores": b_scores, "b_turn": b_turn, "b_values": b_values,
                     "b_done": b_done, "c_scores": c_scores, "c_sums": c_sums, "c_values": c_values,
                     "a_mix": a_mix, "gate": lambda i: gate_(*i)}
            for step, i in TIMELINE:
                if step in STEPS:
                    STEPS[step](i)

            pe.wait_ge(merged, 2 * KD)
            for n in range(2):
                pe.wait_ge(*full_at(out_chunk + n))
                if n == 1:
                    pe.wait_ge(up_taken, 3 * KD)
                w = slot(out_chunk + n, KD)
                for a in range(TT):
                    for k in range(KD):
                        ins = pe.matmul(bank[:, 2 * n + a, :], mergedT[:, k, a * P:(a + 1) * P], w[:, k, :],
                                        start=(k == 0), stop=(k == KD - 1))
                    ins.then_inc(out_done, 1)
            pe.wait_ge(xn2_ready, TT)
            pe.wait_ge(a_ready, TT)
            turn_rows(turned2)
            pe.wait_ge(h_ready, TT)
            for b in range(4):
                pe.matmul(bank[:, b, :], zeros[:, 0:P], zeros[:, :], start=True, stop=True)
            pe.wait_ge(turn2_a, 2)
            pe.wait_ge(turn2_d, 2)
            for a in range(TT):
                for k in range(KD):
                    ins = pe.matmul(bank[:, SC, a * E:(a + 1) * E], xnT[:, k, a * P:(a + 1) * P], rw[:, k, :],
                                    start=(k == 0), stop=(k == KD - 1))
            ins.then_inc(routed, 1)
            pe.wait_ge(chosen_ready, 1)
            chosen = rt[:, 13, :]
            pe.matmul(bank[:, SC, 0:E], before[:, :], chosen[:, 0:E], start=True, stop=True)
            pe.matmul(bank[:, SC, E:2 * E], before[:, :], chosen[:, E:2 * E], start=True, stop=False)
            pe.matmul(bank[:, SC, E:2 * E], ones[:, :], chosen[:, 0:E], start=False, stop=True)
            pe.matmul(bank[:, SC + 1, 0:E], ones[:, :], chosen[:, 0:E], start=True, stop=False)
            pe.matmul(bank[:, SC + 1, 0:E], ones[:, :], chosen[:, E:2 * E], start=False, stop=True)\
              .then_inc(pos_done, 1)

            def expert_pass(s, n, p, i):
                def landed(j):
                    before_it = len([c for c in range(NC) if c % MIX_RING == j])
                    if i is None:
                        pe.wait_ge(slot_full[j], 16 * p + 16 * (before_it + 1))
                    return j

                pe.wait_ge(s["sel"], 2 * n + 2)
                for b in range(2):
                    for k in range(4):
                        for a in range(TT):
                            ins = pe.matmul(bank[:, 4 + b, k * P:(k + 1) * P],
                                            xn[:, a, (4 * b + k) * P:(4 * b + k + 1) * P],
                                            sel[:, a * 2 * J:(a + 1) * 2 * J], start=(a == 0), stop=(a == TT - 1))
                    ins.then_inc(s["gathered"], 1)

                def two_experts(dst, lhsT, rhs, tiles):
                    for k in range(tiles):
                        for e in range(2):
                            last = pe.matmul(bank[e * J:(e + 1) * J, dst, :], lhsT[:, k, e * J:(e + 1) * J],
                                             rhs[e][:, k, :], start=(k == 0), stop=(k == tiles - 1))
                    return last

                pe.wait_ge(s["xg"], 2 * n + 3)
                for m in range(2):
                    pe.wait_ge(s["ye_d" if m else "ye_a"], n + 1)
                    w = [e_slot(landed(2 * m + e), KD) for e in range(2)]
                    two_experts(6 + m, xgT, w, KD).then_inc(s["h_done"], 1)
                pe.wait_ge(s["sel"], 2 * n + 3)
                for a in range(TT):
                    ins = pe.transpose(bank[:, 5, a * P:(a + 1) * P], gated[:, a * 2 * J:(a + 1) * 2 * J], ident[:, :])
                ins.then_inc(s["gt_turned"], 1)
                pe.wait_ge(s["he"], n + 2)
                for f in range(KF):
                    ins = pe.transpose(bank[:, 4, f * P:(f + 1) * P], he[:, f * P:(f + 1) * P], ident[:, :])
                ins.then_inc(s["he_turned"], 1)
                pe.wait_ge(s["heT"], n + 2)
                w = [e_slot(landed(4 + e), KF) for e in range(2)]
                for b in range(2):
                    two_experts(6 + b, heT, [x[:, :, b * 512:(b + 1) * 512] for x in w], KF)\
                        .then_inc(s["y_done"], 1)
                pe.wait_ge(s["gt"], n + 2)
                for b in range(2):
                    pe.wait_ge(s["ye_d" if b else "ye_a"], n + 2)
                    for a in range(TT):
                        ins = pe.matmul(bank[:, 2 * b + a, :], gatedT[:, a * P:(a + 1) * P],
                                        ye[:, b * 512:(b + 1) * 512], start=False, stop=False, skip_group_check=True)
                ins.then_inc(s["scattered"], 1)

            run_pairs(pe, expert_pass)


_INS = ["x", "norm_mix_gain", "w_in", "gmlp_w_s", "gmlp_b_s", "gmlp_v_gain", "diff_lambda", "diff_subln_gain",
        "w_up_a", "w_up_b", "w_up_c", "w_out", "norm_ffn_gain", "router_w", "router_bias",
        "moe_w1", "moe_w3", "moe_w2", "final_gain"]


def kernel(**inputs):
    import numpy as np
    import concourse.bacc as bacc
    from concourse.bass_utils import run_bass_kernel_spmd as run

    nc = bacc.Bacc("TRN2", target_bir_lowering=False, num_devices=1)
    arrays, args = {}, []
    for name in _INS:
        a = np.ascontiguousarray(inputs[name])
        arrays["in_" + name] = a
        args.append(nc.dram_tensor("in_" + name, a.shape, mybir.dt.from_np(a.dtype), kind="ExternalInput").ap())
    args.append(nc.dram_tensor("out_0", inputs["x"].shape, F32, kind="ExternalOutput").ap())
    trunk(nc, *args)
    r = run(nc, [arrays], core_ids=[0])
    return r.results[0]["out_0"]
```

```python
from contextlib import ExitStack

import concourse.bass as bass
import concourse.mybir as mybir

F32 = mybir.dt.float32
F32R = mybir.dt.float32r
I32 = mybir.dt.int32
ALU = mybir.AluOpType
ACT = mybir.ActivationFunctionType
AX = mybir.AxisListType

P = 128
EPS = 1e-6
LAMBDA_INIT = 0.8 - 0.6
MASKED = -1e30


def trunk(nc, x, norm_mix_gain, w_in, gmlp_w_s, gmlp_b_s, gmlp_v_gain, diff_lambda, diff_subln_gain,
          w_up_a, w_up_b, w_up_c, w_out, norm_ffn_gain, router_w, router_bias,
          moe_w1, moe_w3, moe_w2, final_gain, out):
    T, D = x.shape[1], x.shape[2]
    TT, KD = T // P, D // P
    NG = gmlp_w_s.shape[1]
    AW = NG * P
    BH, BQ = 4, 64
    CH, CD = 8, 64
    E = router_w.shape[1]
    EG = 4
    NGR = E // EG
    F = moe_w1.shape[3]
    KF = F // P
    PAIRS = E // 2
    J = 64
    PASSES = PAIRS + 2 * T // J
    W3 = 3 * P
    B_SCALE, C_SCALE = BQ ** -0.5, CD ** -0.5
    SLOPES = [(2.0 ** (-8.0 / BH)) ** (i + 1) for i in range(BH)]

    RING, MIX_RING = 8, 4
    W1_SLOTS, W3_SLOTS, W2_SLOTS = ((4, 5), (1, 2)), (0, 3), (6, 7)
    CW = 512
    UA, VA, QB, KB, VB, QC, KC, VC = range(8)
    PROJ = [QB, KB, VB, QC, KC, VC, VA, UA]
    BRANCHES = [("B", 10, w_up_b), ("C", 12, w_up_c), ("A", 8, w_up_a)]
    w_in_v = w_in[0].rearrange("(k p) n -> p k n", p=P)
    w_out_v = w_out[0].rearrange("(k p) n -> p k n", p=P)
    chunks = [w_in_v[:, :, c * CW:(c + 1) * CW] for c in PROJ]
    up_chunk = {}
    for name, c0, up in BRANCHES:
        up_chunk[name] = len(chunks) + 1
        chunks += [w_in_v[:, :, c0 * CW:(c0 + 1) * CW], up[0].rearrange("(k p) n -> p k n", p=P),
                   w_in_v[:, :, (c0 + 1) * CW:(c0 + 2) * CW]]
    out_chunk = len(chunks)
    chunks += [w_out_v[:, :, n * CW:(n + 1) * CW] for n in range(D // CW)]
    NC = len(chunks)
    split_order = [i for i in range(NC) if i not in up_chunk.values()]
    NH_IN = 2 * len([i for i in split_order if i < out_chunk])
    MASKS_AT = 4
    HALF = CW // 2
    NH = 2 * len(split_order)
    assert D // CW == 2 and F == CW and PAIRS % 2 == 0

    TIMELINE = [("proj", (0, 0)), ("proj", (0, 1)), ("proj", (1, 0)), ("proj", (1, 1)), ("ws_turn", 0),
                ("b_scores", 0), ("proj", (2, 0)), ("b_combine", 0), ("proj", (2, 1))]
    for h in range(BH - 1):
        TIMELINE += [("b_turn", h), ("b_scores", h + 1), ("proj", (3 + h, 0)), ("b_values", h),
                     ("b_combine", h + 1), ("proj", (3 + h, 1))]
    TIMELINE += [("b_turn", BH - 1), ("c_scores", 0), ("c_scores", 1), ("c_keep", 0), ("c_keep", 1),
                 ("proj", (6, 0)), ("b_values", BH - 1), ("b_norm", 0)]
    for q in range(3):
        TIMELINE += [("c_sums", 2 * q), ("c_sums", 2 * q + 1), ("c_scores", 2 * q + 2), ("c_scores", 2 * q + 3),
                     ("c_logits", 2 * q), ("c_logits", 2 * q + 1), ("c_keep", 2 * q + 2), ("c_keep", 2 * q + 3)]
        if q == 2:
            TIMELINE += [("y_split", 0), ("a_gelu_v", 0)]
        if q == 0:
            TIMELINE += [("proj", (6, 1)), ("b_done", 0)]
        else:
            TIMELINE += [("proj", (7, q - 1))]
        TIMELINE += [("c_values", 2 * q), ("c_values", 2 * q + 1)]
    TIMELINE += [("c_sums", 6), ("c_sums", 7), ("c_logits", 6), ("c_logits", 7), ("gate", (0, 0)),
                 ("c_values", 6), ("c_values", 7), ("gate", (0, 1)), ("a_norm", 0), ("gate", (0, 2)),
                 ("a_gelu_u", 0), ("gate", (0, 3)), ("a_mix", 0),
                 ("y_split", 1), ("gate", (0, 4)), ("gate", (0, 5)), ("y_split", 2),
                 ("gate", (0, 6)), ("gate", (0, 7))]
    TIMELINE += [("gate", (b, d)) for b in (1, 2) for d in range(KD)]

    with ExitStack() as ctx:
        def sb(name, shape, dt=F32):
            return ctx.enter_context(nc.sbuf_tensor(name, shape, dt))

        def sem(name):
            return ctx.enter_context(nc.semaphore(name))

        base = (nc.sbuf_base + 31) // 32 * 32
        ring_slab = sb("ring_slab", [P, RING * 4096 + 8192])
        SLOT = 4096 * 4

        def at(name, shape, offset, dt=F32R):
            return nc.alloc_sbuf_tensor_at(name, shape, dt, offset=base + offset)

        ring = at("ring", [P, RING, 4096], 0, F32)
        shared = MIX_RING * SLOT
        w_hi = [at(f"w_hi{b}", [P, KD, HALF], shared + b * SLOT // 2) for b in range(2)]
        w_lo = [at(f"w_lo{b}", [P, KD, HALF], shared + SLOT + b * SLOT // 2) for b in range(2)]
        x_hi = at("x_hi", [P, KD, T], shared + 2 * SLOT)
        x_lo = at("x_lo", [P, KD, T], shared + 2 * SLOT + SLOT // 2)
        b_bias = at("b_bias", [P, BH, W3], shared + 3 * SLOT, F32)
        o_b = at("o_b", [P, TT, BH, P], shared + 3 * SLOT + 4 * BH * W3, F32)
        prob = at("prob", [P, 4, W3], shared + 3 * SLOT + 4 * (BH * W3 + TT * BH * P), F32)
        WORK = RING * SLOT
        u_hi = [at("u_hi0", [P, 4, HALF], WORK + 4 * 1024), at("u_hi1", [P, 4, HALF], shared + 3 * SLOT)]
        u_lo = [at("u_lo0", [P, 4, HALF], WORK + 4 * 2048),
                at("u_lo1", [P, 4, HALF], shared + 3 * SLOT + 4 * BH * W3)]
        y_hi = {name: at("y_hi_" + name, [P, 4, T], WORK + 4 * o)
                for name, o in (("B", 4096), ("C", 5120), ("A", 6144))}
        y_lo = {name: at("y_lo_" + name, [P, 4, T], WORK + 4 * o)
                for name, o in (("B", 0), ("C", 3072), ("A", 7168))}
        merged_hi_parts = [at("merged_hi0", [P, 4, T], WORK),
                           at("merged_hi1", [P, 4, T], shared + 3 * SLOT + 4 * (BH * W3 + TT * BH * P))]
        merged_lo = at("merged_lo", [P, KD, T], WORK + 4 * 4096)
        ye_hi = at("ye_hi", [P, D], WORK + 4 * 2048)
        ye_lo = at("ye_lo", [P, D], WORK + 4 * 6144)
        selT = at("selT", [P, T], WORK + 4 * 4608)
        h_sb = sb("h_sb", [P, TT, D])
        xn = sb("xn", [P, TT, D])
        mergedT = xn[:, :, :].rearrange("p a (b t) -> p (a b) t", t=T)
        work = at("work", [P, 8192], WORK, F32)
        qbT = work[:, 0:1024].rearrange("p (h t) -> p h t", t=T)
        kbT = work[:, 1024:2048].rearrange("p (h t) -> p h t", t=T)
        vb = work[:, 2048:3072].rearrange("p (a n) -> p a n", a=TT)
        qcT = work[:, 3072:4096].rearrange("p (h t) -> p h t", t=T)
        kcT = work[:, 4096:5120].rearrange("p (h t) -> p h t", t=T)
        vc = work[:, 5120:6144].rearrange("p (a n) -> p a n", a=TT)
        va = work[:, 6144:7168].rearrange("p (a n) -> p a n", a=TT)
        uT = work[:, 7168:8192].rearrange("p (g t) -> p g t", t=T)
        yT = {"A": uT, "B": qbT, "C": qcT}
        hT = work[:, 6144:8192].rearrange("p (k t) -> p k t", t=T)
        xgT = work[:, 0:1024].rearrange("p (k j) -> p k j", j=2 * J)
        silu = work[:, 1024:1024 + F]
        he = work[:, 1536:1536 + F]
        heT = work[:, 3072:3584].rearrange("p (f j) -> p f j", j=2 * J)
        sel = work[:, 4096:4352]
        gated = work[:, 4352:4608]
        scratch = work[:, 3072:4096]

        def merged_hi(k):
            return merged_hi_parts[k // 4][:, k % 4, :]


        gain = sb("gain", [P, D])
        v_gain = sb("v_gain", [P, AW])
        sub_gain = sb("sub_gain", [P, 1])
        lam_in = sb("lam_in", [P, 4, BQ])
        b_row = sb("b_row", [1, NG * P])
        rw = sb("rw", [P, KD, E])
        ffn_gain = sb("ffn_gain", [P, KD])
        rbias = sb("rbias", [P, E])
        wsT = sb("wsT", [P, NG, P])
        ident = sb("ident", [P, P])
        ones = sb("ones", [P, P])
        from_here = sb("from_here", [P, P])
        before = sb("before", [P, P])
        c_mask = sb("c_mask", [P, W3])
        iota_i = sb("iota_i", [P, T + J], I32)
        iota = sb("iota", [P, T + J])
        diff = sb("diff", [P, 2, W3])
        diffT = sb("diffT", [P, 2, W3])
        dist = diffT[:, 0, :]
        dist_i = diffT[:, 1, :].bitcast(I32)
        ws = o_b[:, 0, :, :]
        gate = sb("gate", [P, 2, T])
        gated_up = sb("gated_up", [P, 2, T])
        st = sb("st", [P, 128])
        rt = work[:, 4864:4864 + 20 * TT * E].rearrange("p (r n) -> p r n", n=TT * E)
        tab = sb("tab", [P, 16])
        gate_col = sb("gate_col", [P, 1])
        PAIR, ODD, NTH, UP_TO, W1_FIRST = range(5)
        plan_f = sb("plan_f", [P, 5, PASSES + 1])
        plan = sb("plan", [1, 5, PASSES + 1], I32)
        sums = sb("sums", [P, 3, 2 * PAIRS])

        bank = ctx.enter_context(nc.psum_tensor("bank", [P, 8, 512], F32))
        PJ, UP, SC, TR, OV = 0, 2, 4, 6, 7

        slot_full = [sem(f"slot_full{s}") for s in range(RING)]
        w2_left = [sem(f"w2_left{e}") for e in range(2)]
        w3_top = [sem(f"w3_top{e}") for e in range(2)]
        ld_x = [sem(f"ld_x{a}") for a in range(TT)]
        ld_gain, ld_small, ld_ws, ld_ffn, ld_final, first_half = (
            sem(n) for n in ("ld_gain", "ld_small", "ld_ws", "ld_ffn", "ld_final", "first_half"))
        consts_pool, consts_dve = sem("consts_pool"), sem("consts_dve")
        ident_ready, rw_scaled = sem("ident_ready"), sem("rw_scaled")
        pool_step = sem("pool_step")
        ws_masked = sem("ws_masked")
        bias_scaled, bias_masked = sem("bias_scaled"), sem("bias_masked")
        act_stat, dve_stat = sem("act_stat"), sem("dve_stat")
        xn_ready = sem("xn_ready")
        turned = sem("turned")
        turn_taken_a, turn_taken_d = sem("turn_taken_a"), sem("turn_taken_d")
        ws_turned, wsT_ready = sem("ws_turned"), sem("wsT_ready")
        w_hi_ready, w_lo_ready = sem("w_hi_ready"), sem("w_lo_ready")
        u_hi_ready, u_lo_ready, y_split_done = sem("u_hi_ready"), sem("u_lo_ready"), sem("y_split_done")
        proj_done = sem("proj_done")
        pj_taken = [sem("pj_taken0"), sem("pj_taken1")]
        b_scored, b_max, b_exp, b_comb, b_diff, b_turned, b_turn_taken = (
            sem(n) for n in ("b_scored", "b_max", "b_exp", "b_comb", "b_diff", "b_turned", "b_turn_taken"))
        b_ov, b_ov_a, b_ov_d, b_normed, b_nturned, b_ready = (
            sem(n) for n in ("b_ov", "b_ov_a", "b_ov_d", "b_normed", "b_nturned", "b_ready"))
        c_scored, c_z, c_sp, c_summed, c_lo, c_prob, c_ov, c_ready = (
            sem(n) for n in ("c_scored", "c_z", "c_sp", "c_summed", "c_lo", "c_prob", "c_ov", "c_ready"))
        c_abs = sem("c_abs")
        a_gelu, a_vn, a_mixed, a_ready = (sem(n) for n in ("a_gelu", "a_vn", "a_mixed", "a_ready"))
        up_done, up_taken, merged, merged_split = (
            sem(n) for n in ("up_done", "up_taken", "merged", "merged_split"))
        out_done, h_ready, rows_ready = sem("out_done"), sem("h_ready"), sem("rows_ready")
        xn2_ready, turned2, turn2_a, turn2_d = (sem(n) for n in ("xn2_ready", "turned2", "turn2_a", "turn2_d"))
        nrs_ready, finished = sem("nrs_ready"), sem("finished")
        routed, aff_exp, masked, chosen_ready, pos_done, planned = (
            sem(n) for n in ("routed", "aff_exp", "masked", "chosen_ready", "pos_done", "planned"))
        stored = sem("stored")

        events = [sem(n) for n in ("sel", "gated", "gathered", "xg_a", "xg_d", "w1_done", "w3_done", "silu", "he",
                                   "he_turned", "heT", "gt_turned", "gt", "y_done", "ye_a", "ye_d")]
        (sel_ready, gated_ready, gathered, xg_a, xg_d, w1_done, w3_done, silu_ready, he_ready,
         he_turned, heT_ready, gt_turned, gt_ready, y_done, ye_a, ye_d) = events

        def full_at(i):
            return slot_full[i % MIX_RING], 16 * (i // MIX_RING + 1)

        def half_at(q):
            return full_at(split_order[q // 2]) if q else (first_half, 16)

        def half_read(q):
            n = q - 2 * len(PROJ)
            if q >= NH_IN:
                return out_done, TT * (q - NH_IN + 1)
            return proj_done, q + 1 if n < 0 else 2 * len(PROJ) + 2 * (n + 1)

        def w_half(q):
            return slot(split_order[q // 2], KD)[:, :, (q % 2) * HALF:(q % 2 + 1) * HALF]

        def read_at(i):
            if i in split_order:
                return w_lo_ready, 2 * split_order.index(i) + 2
            return u_lo_ready, 4 * ((i - len(PROJ)) // 3 + 1)

        def slot(i, k):
            return ring[:, i % MIX_RING, :].rearrange("p (k n) -> p k n", k=k)

        def u_quarter(r):
            return slot(up_chunk[BRANCHES[r // 4][0]], 4)[:, :, (r % 4) * HALF:(r % 4 + 1) * HALF]

        def before_experts(j):
            return len([i for i in range(NC) if i % MIX_RING == j]) if j < MIX_RING else 0

        SS, MS, RS, NRS = 0, 8, 16, 20
        LAMP, LAME, NLAM = 24, 26, 28
        NMAX, SUM, COEF = 32, 40, 48
        SSB, MSB, RSB = 56, 64, 72
        SSV, MSV, RSV = 80, 82, 84

        def col(c, n=1):
            return st[:, c:c + n]

        def out_view(q, a):
            return bank[:, 2 * q + a, 0:HALF]

        mix_scratch = diffT[:, :, :].rearrange("p m n -> p (m n)")[:, 0:AW]
        sub_gain_scaled = st[:, 90:91]

        def proj_dst(c, half):
            dst = {UA: uT, VA: va, QB: qbT, KB: kbT, VB: vb, QC: qcT, KC: kcT, VC: vc}[PROJ[c]]
            if PROJ[c] in (VA, VB, VC):
                return dst[:, :, half * HALF:(half + 1) * HALF]
            return dst[:, 2 * half:2 * half + 2, :]

        def bank_view(c, half):
            return bank[:, PJ + half, :].rearrange("p (h t) -> p h t", t=T)

        def all_passes(eng, expert_pass):
            eng.wait_ge(planned, 1)
            passes = eng.value_load(plan[0:1, UP_TO, PAIRS - 1:PAIRS], min_val=PAIRS, max_val=PASSES)
            with eng.Fori(0, passes) as n:
                expert_pass(n)

        def planned_value(eng, row, n, lo, hi):
            return eng.value_load(plan[0:1, row, bass.ds(n, 1)], min_val=lo, max_val=hi)

        block = ctx.enter_context(nc.Block())

        @block.sync
        def _(sp):
            for a in range(TT):
                sp.dma_start(h_sb[:, a, :], x[0, a * P:(a + 1) * P, :]).then_inc(ld_x[a], 16)
            sp.dma_start(gain[:, :], norm_mix_gain[0].partition_broadcast(P)).then_inc(ld_gain, 16)
            for event in events:
                sp.sem_inc(event, 1)
            def expert_chunk(j, matrix, idx):
                sp.dma_start(ring[:, j, :].rearrange("p (k n) -> p k n", n=matrix.shape[3]),
                             matrix[0, idx].rearrange("(k p) n -> p k n", p=P)).then_inc(slot_full[j], 16)

            def w3_chunk(e, idx, b):
                ks = slice(b * KD // 2, (b + 1) * KD // 2)
                dst = ring[:, W3_SLOTS[e], :].rearrange("p (k n) -> p k n", n=F)[:, ks, :]
                sp.dma_start(dst, moe_w3[0, idx].rearrange("(k p) n -> p k n", p=P)[:, ks, :])\
                    .then_inc(slot_full[W3_SLOTS[e]] if b else w3_top[e], 16)

            def w2_chunk(e, idx, b):
                cols = slice(b * 512, (b + 1) * 512)
                dst = ring[:, W2_SLOTS[e], :].rearrange("p (k n) -> p k n", n=D)[:, :, cols]
                sp.dma_start(dst, moe_w2[0, idx].rearrange("(k p) n -> p k n", p=P)[:, :, cols])\
                    .then_inc(slot_full[W2_SLOTS[e]] if b else w2_left[e], 16)

            for i in range(NC):
                if i >= MIX_RING:
                    sp.wait_ge(*read_at(i - MIX_RING))
                dst = slot(i, chunks[i].shape[1])
                if i == 0:
                    sp.dma_start(dst[:, :, 0:HALF], chunks[i][:, :, 0:HALF]).then_inc(first_half, 16)
                    sp.dma_start(dst[:, :, HALF:CW], chunks[i][:, :, HALF:CW]).then_inc(slot_full[0], 16)
                else:
                    sp.dma_start(dst, chunks[i]).then_inc(slot_full[i % MIX_RING], 16)

            def mixer_left(j):
                if j < MIX_RING:
                    sp.wait_ge(*read_at(max(i for i in range(NC) if i % MIX_RING == j)))
                else:
                    sp.wait_ge(*half_read(NH_IN - 1 if j == W2_SLOTS[0] else NH - 1))

            for e in range(2):
                mixer_left(W3_SLOTS[e])
                for b in range(2):
                    w3_chunk(e, e, b)
            mixer_left(W2_SLOTS[0])
            for b in range(2):
                w2_chunk(0, 0, b)
            for e in range(2):
                mixer_left(W1_SLOTS[1][e])
                expert_chunk(W1_SLOTS[1][e], moe_w1, 2 + e)
            for e in range(2):
                mixer_left(W1_SLOTS[0][e])
                expert_chunk(W1_SLOTS[0][e], moe_w1, e)
            mixer_left(W2_SLOTS[1])
            for b in range(2):
                w2_chunk(1, 1, b)

            def next_w1(p, odd, passes):
                sp.wait_ge(w1_done, passes + 1)
                for e in range(2):
                    expert_chunk(W1_SLOTS[odd][e], moe_w1, 2 * p + 4 + e)

            def next_w3_w2(p, passes):
                sp.wait_ge(w3_done, passes + 1)
                for b in range(2):
                    for e in range(2):
                        w3_chunk(e, 2 * p + 2 + e, b)
                for b in range(2):
                    sp.wait_ge(y_done, 2 * passes + b)
                    for e in range(2):
                        w2_chunk(e, 2 * p + 2 + e, b)

            sp.wait_ge(planned, 1)
            with sp.Fori(0, PAIRS // 2 - 1) as pp:
                for odd in range(2):
                    p = pp * 2 + odd
                    passes = planned_value(sp, UP_TO, p, 1, PASSES)
                    w1_first = planned_value(sp, W1_FIRST, p, 0, 3)
                    with sp.If(w1_first > 0):
                        next_w1(p, odd, passes)
                        next_w3_w2(p, passes)
                    with sp.Else():
                        next_w3_w2(p, passes)
                        next_w1(p, odd, passes)
            with sp.Fori(PAIRS - 2, PAIRS - 1) as p:
                passes = planned_value(sp, UP_TO, p, 1, PASSES)
                next_w3_w2(p, passes)
            for a in range(TT):
                sp.wait_ge(rows_ready, a + 1)
                sp.dma_start(out[0, a * P:(a + 1) * P, :], xn[:, a, :]).then_inc(stored, 16)
            sp.wait_ge(stored, 16 * TT)

        @block.gpsimd
        def _(pool):
            pool.memset(ident[:, :], 0.0).then_inc(pool_step, 1)
            pool.wait_ge(pool_step, 1)
            pool.affine_select(out=ident[:, :], in_=ident[:, :], compare_op=ALU.not_equal, fill=1.0, base=0,
                               pattern=[[-1, P]], channel_multiplier=1).then_inc(ident_ready, 1)
            pool.memset(ones[:, :], 1.0).then_inc(pool_step, 1)
            pool.memset(c_mask[:, :], 0.0).then_inc(pool_step, 1)
            pool.iota(dist_i[:, 0:P], pattern=[[-1, P]], base=0, channel_multiplier=1).then_inc(pool_step, 1)
            pool.iota(dist_i[:, P:W3], pattern=[[-1, 2 * P]], base=P, channel_multiplier=1).then_inc(pool_step, 1)
            pool.iota(iota_i[:, :], pattern=[[1, T + J]], base=0, channel_multiplier=0).then_inc(pool_step, 1)
            pool.wait_ge(pool_step, 6)
            pool.affine_select(out=from_here[:, :], in_=ones[:, :], compare_op=ALU.is_ge, fill=0.0, base=0,
                               pattern=[[-1, P]], channel_multiplier=1).then_inc(consts_pool, 1)
            pool.affine_select(out=before[:, :], in_=ones[:, :], compare_op=ALU.is_gt, fill=0.0, base=0,
                               pattern=[[1, P]], channel_multiplier=-1).then_inc(consts_pool, 1)
            for c in (0, 2):
                pool.affine_select(out=c_mask[:, c * P:(c + 1) * P], in_=c_mask[:, c * P:(c + 1) * P],
                                   compare_op=ALU.is_gt, fill=MASKED, base=0, pattern=[[1, P]],
                                   channel_multiplier=-1).then_inc(consts_pool, 1)

            def rows(ap):
                return ap.partition_broadcast(P)

            pool.dma_start(ws, gmlp_w_s[0].rearrange("g t s -> t g s")).then_inc(ld_ws, 16)
            small = [(lam_in[:, :, :], rows(diff_lambda[0])), (v_gain[:, :], rows(gmlp_v_gain[0])),
                     (sub_gain[:, :], diff_subln_gain[0].rearrange("(p a) -> p a", a=1)),
                     (b_row[:, :], gmlp_b_s[0:1].rearrange("a g t -> a (g t)")),
                     (rw[:, :, :], router_w.rearrange("(k p) e -> p k e", p=P)),
                     (rbias[:, :], rows(router_bias))]
            for dst, src in small:
                pool.dma_start(dst, src).then_inc(ld_small, 16)
            pool.dma_start(ffn_gain[:, :], norm_ffn_gain[0].rearrange("(k p) -> p k", p=P),
                           allow_slow_non_contiguous=True).then_inc(ld_small, 16)

            def masks():
                pool.wait_ge(ld_ws, 16)
                pool.affine_select(out=ws, in_=ws, compare_op=ALU.is_ge, fill=0.0, base=0,
                                   pattern=[[0, NG], [-1, P]], channel_multiplier=1).then_inc(ws_masked, 1)
                pool.wait_ge(bias_scaled, BH)
                pool.affine_select(out=b_bias[:, :, 0:P], in_=b_bias[:, :, 0:P], compare_op=ALU.is_ge, fill=MASKED,
                                   base=0, pattern=[[0, BH], [-1, P]], channel_multiplier=1)\
                    .then_inc(bias_masked, 1)
                pool.affine_select(out=b_bias[:, :, P:W3], in_=b_bias[:, :, P:W3], compare_op=ALU.is_ge, fill=MASKED,
                                   base=P, pattern=[[0, BH], [-1, 2 * P]], channel_multiplier=1)\
                    .then_inc(bias_masked, 1)

            for q in range(NH):
                if q == MASKS_AT:
                    masks()
                    pool.wait_ge(xn_ready, TT)
                    pool.dma_start(gain[:, :], norm_ffn_gain[0].partition_broadcast(P)).then_inc(ld_ffn, 16)
                    continue
                pool.wait_ge(*half_at(q))
                pool.wait_ge(w_hi_ready, q + 1)
                if q >= 2:
                    pool.wait_ge(*half_read(q - 2))
                pool.tensor_tensor(w_lo[q % 2][:, :, :], w_half(q), w_hi[q % 2][:, :, :].bitcast(F32),
                                   ALU.subtract).then_inc(w_lo_ready, 1)
                r = q - 2 * len(PROJ)
                if 0 <= r < 4 * len(BRANCHES):
                    pool.wait_ge(u_hi_ready, r + 1)
                    if r == 0:
                        pool.wait_ge(b_ov, BH)
                    elif r == 1:
                        pool.wait_ge(b_nturned, 2)
                    else:
                        pool.wait_ge(up_done, 2 * r - 2)
                    pool.tensor_tensor(u_lo[r % 2][:, :, :], u_quarter(r), u_hi[r % 2][:, :, :].bitcast(F32),
                                       ALU.subtract).then_inc(u_lo_ready, 1)
            pool.wait_ge(ld_small, 16 * 7)
            pool.tensor_tensor(rw[:, :, :], rw[:, :, :], ffn_gain[:, :].unsqueeze(2).to_broadcast([P, KD, E]),
                               ALU.mult).then_inc(rw_scaled, 1)
            pool.wait_ge(xn2_ready, TT)
            pool.dma_start(gain[:, :], final_gain.partition_broadcast(P)).then_inc(ld_final, 16)

        @block.scalar
        def _(act):
            def square_sum(src, dst, width):
                act.activation(scratch_of(width), src, ACT.Square, accum_out=dst).then_inc(act_stat, 1)

            def scratch_of(width):
                return scratch[:, 0:width]

            def sqrt(dst, src, need):
                act.wait_ge(dve_stat, need)
                act.activation(dst, src, ACT.Sqrt).then_inc(act_stat, 1)

            act.preload_act_table_set("sqrt_and_others")
            for a in range(TT):
                act.wait_ge(ld_x[a], 16)
                if a:
                    act.wait_ge(act_stat, a)
                square_sum(h_sb[:, a, :], col(SS + a), D)
            sqrt(col(RS, TT), col(MS, TT), 2)
            for g in range(4):
                act.wait_ge(turned, g + 1)
                act.activation(x_hi[:, 2 * g:2 * g + 2, :], bank[:, SC + g, :].rearrange("p (k t) -> p k t", t=T),
                               ACT.Copy).then_inc(turn_taken_a, 1)

            act.preload_act_table_set("natural_log_exp_and_others")

            def proj(c, half):
                if half or PROJ[c] in (UA, VA):
                    return
                act.wait_ge(proj_done, 2 * c + 1)
                act.activation(proj_dst(c, half), bank_view(c, half), ACT.Copy).then_inc(pj_taken[0], 1)

            def b_scores(h):
                q = h % 2
                act.wait_ge(b_max, h + 1)
                for m in range(2):
                    for blk, (lo, hi) in enumerate(((0, P), (P, W3))):
                        act.activation(prob[:, 2 * q + m, lo:hi], prob[:, 2 * q + m, lo:hi], ACT.Exp,
                                       bias=col(NMAX + 4 * q + 2 * blk + m),
                                       accum_out=col(SUM + 4 * q + 2 * blk + m)).then_inc(b_exp, 1)
                if h == 0:
                    act.wait_ge(dve_stat, 4)
                    act.activation(col(LAME, 2), col(LAMP, 2), ACT.Exp).then_inc(act_stat, 1)

            def b_turn(h):
                act.wait_ge(b_turned, h + 1)
                if h >= 2:
                    act.wait_ge(b_ov, h - 1)
                act.activation(diffT[:, h % 2, :], bank[:, TR, 0:W3], ACT.Copy).then_inc(b_turn_taken, 1)

            def b_values(h):
                act.wait_ge(b_ov_d, h + 1)
                for a in range(TT):
                    if h or a:
                        act.wait_ge(b_ov_a, TT * h + a)
                    act.activation(gate[:, 0, 0:P], o_b[:, a, h, :], ACT.Square,
                                   accum_out=col(SSB + BH * a + h)).then_inc(b_ov_a, 1)

            def b_norm(_):
                act.preload_act_table_set("sqrt_and_others")
                sqrt(col(RSB, TT * BH), col(MSB, TT * BH), 6)
                act.preload_act_table_set("natural_log_exp_and_others")

            def b_done(_):
                act.wait_ge(consts_dve, 4)
                act.wait_ge(b_nturned, 1)
                act.activation(yT["B"][:, 0:2, :], bank[:, TR, :].rearrange("p (h t) -> p h t", t=T), ACT.Copy,
                               scale=sub_gain_scaled).then_inc(b_ready, 1)

            def c_keep(h):
                act.wait_ge(c_z, h + 1)
                w = diff[:, h % 2, :]
                if h >= 2:
                    act.wait_ge(c_summed, h - 1)
                act.activation(w, prob[:, h % 4, :], ACT.Abs).then_inc(c_abs, 1)
                act.wait_ge(c_abs, 3 * h + 1)
                act.activation(w, w, ACT.Exp, scale=-1.0).then_inc(c_abs, 1)
                act.wait_ge(c_abs, 3 * h + 2)
                act.activation(w, w, ACT.Ln, bias=1.0).then_inc(c_abs, 1)

            def c_logits(h):
                act.wait_ge(c_lo, h + 1)
                act.activation(prob[:, h % 4, :], prob[:, h % 4, :], ACT.Exp).then_inc(c_prob, 1)

            def c_values(h):
                if h % 2:
                    act.wait_ge(c_ov, h + 1)
                    t = h // 2
                    act.activation(yT["C"][:, t, :], bank[:, OV, (t % 2) * T:(t % 2 + 1) * T],
                                   ACT.Copy).then_inc(c_ready, 1)

            def a_gelu_v(_):
                act.wait_ge(pj_taken[0], 7)
                act.wait_ge(pj_taken[1], 7)
                for a in range(TT):
                    act.activation(va[:, a, :], va[:, a, :], ACT.Gelu_apprx_tanh).then_inc(a_gelu, 1)
                act.wait_ge(a_gelu, TT)
                act.wait_ge(b_ov, BH)
                for a in range(TT):
                    if a:
                        act.wait_ge(act_stat, 6)
                    act.activation(mix_scratch, va[:, a, :], ACT.Square,
                                   accum_out=col(SSV + a)).then_inc(act_stat, 1)
                act.preload_act_table_set("natural_log_exp_and_others")

            def a_norm(_):
                sqrt(col(RSV, TT), col(MSV, TT), 8)

            def a_gelu_u(_):
                act.wait_ge(pj_taken[0], 8)
                act.wait_ge(pj_taken[1], 8)
                act.activation(uT[:, :, :], uT[:, :, :], ACT.Gelu_apprx_tanh).then_inc(a_gelu, 1)

            def gate_(b, d):
                n = KD * b + d
                act.wait_ge(proj_done, 16 + n + 1)
                if n >= 2:
                    act.wait_ge(up_taken, n - 1)
                act.activation(gate[:, n % 2, :], bank[:, PJ + n % 2, 0:T], ACT.Sigmoid)\
                   .then_inc(pj_taken[n % 2], 1)

            STEPS = {"proj": lambda i: proj(*i), "b_scores": b_scores, "b_turn": b_turn, "b_values": b_values,
                     "b_norm": b_norm, "b_done": b_done, "c_keep": c_keep, "c_logits": c_logits,
                     "c_values": c_values, "a_gelu_v": a_gelu_v, "a_norm": a_norm,
                     "a_gelu_u": a_gelu_u, "gate": lambda i: gate_(*i)}
            for step, i in TIMELINE:
                if step in STEPS:
                    STEPS[step](i)

            def turned_rows(a):
                act.wait_ge(turned2, 2 * a + 1)
                act.activation(hT[:, 0:4, a * P:(a + 1) * P], bank[:, SC + 2 * a, :].rearrange("p (k t) -> p k t", t=P),
                               ACT.Copy).then_inc(turn2_a, 1)

            act.preload_act_table_set("sqrt_and_others")
            act.wait_ge(merged, 2 * KD)
            for a in range(TT):
                act.wait_ge(h_ready, 7 + a)
                act.wait_ge(act_stat, 8 + a)
                square_sum(h_sb[:, a, :], col(SS + a), D)
                turned_rows(a)
            sqrt(col(RS, TT), col(MS, TT), 10)
            act.preload_act_table_set("natural_log_exp_and_others")
            act.wait_ge(routed, 1)
            act.wait_ge(nrs_ready, 1)
            for a in range(TT):
                act.activation(rt[:, 0, a * E:(a + 1) * E], bank[:, SC, a * E:(a + 1) * E], ACT.Exp,
                               scale=col(NRS + a)).then_inc(aff_exp, 1)

            def gathered_rows(n):
                act.wait_ge(gathered, 2 * n + 2)
                act.activation(xgT[:, 0:4, :], bank[:, 4, :].rearrange("p (k j) -> p k j", j=2 * J), ACT.Copy)\
                   .then_inc(xg_a, 1)

            def expert_pass(n):
                act.wait_ge(w1_done, n + 2)
                act.wait_ge(he_ready, n + 1)
                act.activation(silu, bank[:, 6, :], ACT.Silu).then_inc(silu_ready, 1)
                act.wait_ge(gt_turned, n + 2)
                act.activation(selT[:, :], bank[:, 4, 0:T], ACT.Copy)
                act.activation(gate_col[:, :], bank[:, 4, T:T + 1], ACT.Copy).then_inc(gt_ready, 1)
                act.wait_ge(he_turned, n + 2)
                act.activation(heT[:, :, :], bank[:, 6, :].rearrange("p (f j) -> p f j", j=2 * J),
                               ACT.Copy).then_inc(heT_ready, 1)
                gathered_rows(n + 1)
                for b in range(2):
                    act.wait_ge(y_done, 2 * n + 2 + b)
                    act.activation(ye_hi[:, b * 512:(b + 1) * 512], bank[:, 7 - b, :], ACT.Copy).then_inc(ye_a, 1)

            act.preload_act_table_set("silu_and_others")
            gathered_rows(0)
            all_passes(act, expert_pass)
            act.preload_act_table_set("sqrt_and_others")
            act.wait_ge(finished, 1)
            act.wait_ge(act_stat, 11)
            for a in range(TT):
                if a:
                    act.wait_ge(act_stat, 11 + a)
                act.activation(scratch_of(D).rearrange("p (b n) -> p b n", b=2), bank[:, a:4:2, :], ACT.Square,
                               accum_out=col(SS + a)).then_inc(act_stat, 1)
            for a in range(TT):
                sqrt(col(RS + a), col(MS + a), 12 + 2 * a)

        @block.vector
        def _(dve):
            n_stat = [0]

            def stat(ins):
                n_stat[0] += 1
                ins.then_inc(dve_stat, 1)
                dve.wait_ge(dve_stat, n_stat[0])

            def mean_inverse(dst, src, width):
                stat(dve.tensor_scalar(dst, src, 1.0 / width, EPS, ALU.mult, ALU.add))
                stat(dve.reciprocal(dst, dst))

            def split(q):
                if q >= NH:
                    return
                dve.wait_ge(*half_at(q))
                if q >= 2:
                    dve.wait_ge(*half_read(q - 2))
                dve.tensor_copy(w_hi[q % 2][:, :, :], w_half(q)).then_inc(w_hi_ready, 1)
                if q == MASKS_AT:
                    dve.wait_ge(w_hi_ready, q + 1)
                    dve.wait_ge(w_lo_ready, q)
                    dve.tensor_tensor(w_lo[q % 2][:, :, :], w_half(q), w_hi[q % 2][:, :, :].bitcast(F32),
                                      ALU.subtract).then_inc(w_lo_ready, 1)

            dve.wait_ge(pool_step, 6)
            dve.tensor_copy(dist, dist_i).then_inc(consts_dve, 1)
            dve.tensor_copy(iota[:, :], iota_i[:, :]).then_inc(consts_dve, 1)
            dve.wait_ge(consts_dve, 2)
            for h in range(BH):
                dve.tensor_scalar(b_bias[:, h, :], dist, -SLOPES[h], None, ALU.mult).then_inc(bias_scaled, 1)
            dve.wait_ge(act_stat, 2)
            mean_inverse(col(MS, TT), col(SS, TT), D)
            dve.wait_ge(act_stat, 3)
            dve.wait_ge(ld_gain, 16)
            for a in range(TT):
                dve.scalar_tensor_tensor(out=xn[:, a, :], in0=h_sb[:, a, :], scalar=col(RS + a),
                                         in1=gain[:, :], op0=ALU.mult, op1=ALU.mult).then_inc(xn_ready, 1)
            split(0)
            for g in range(4):
                dve.wait_ge(turn_taken_a, g + 1)
                dve.tensor_tensor(x_lo[:, 2 * g:2 * g + 2, :],
                                  bank[:, SC + g, :].rearrange("p (k t) -> p k t", t=T),
                                  x_hi[:, 2 * g:2 * g + 2, :].bitcast(F32), ALU.subtract).then_inc(turn_taken_d, 1)
            split(1)

            def ws_turn(_):
                dve.wait_ge(ws_turned, 1)
                dve.tensor_copy(wsT[:, :, :], bank[:, TR, :].rearrange("p (g t) -> p g t", t=P)).then_inc(wsT_ready, 1)

            def proj(c, half):
                if half or PROJ[c] in (UA, VA):
                    dve.wait_ge(proj_done, 2 * c + half + 1)
                    dve.tensor_copy(proj_dst(c, half), bank_view(c, half)).then_inc(pj_taken[half], 1)
                split(2 * c + half + 2)

            def b_scores(h):
                q = h % 2
                if h == 0:
                    dve.wait_ge(bias_masked, 2)
                dve.wait_ge(b_scored, h + 1)
                p2 = prob[:, 2 * q:2 * q + 2, :]
                for m in range(2):
                    dve.scalar_tensor_tensor(out=prob[:, 2 * q + m, :], in0=bank[:, SC + m, 0:W3], scalar=B_SCALE,
                                             in1=b_bias[:, h, :], op0=ALU.mult, op1=ALU.add).then_inc(b_comb, 1)
                dve.wait_ge(b_comb, 7 * h + 2)
                for blk, (lo, hi) in enumerate(((0, P), (P, W3))):
                    dve.tensor_reduce(col(NMAX + 4 * q + 2 * blk, 2), p2[:, :, lo:hi], AX.X, ALU.max)\
                       .then_inc(b_comb, 1)
                dve.wait_ge(b_comb, 7 * h + 4)
                dve.tensor_scalar(col(NMAX + 4 * q, 4), col(NMAX + 4 * q, 4), -1.0, None, ALU.mult)\
                   .then_inc(b_max, 1)

            def b_combine(h):
                q = h % 2
                if h == 0:
                    dve.wait_ge(ld_small, 16 * 7)
                    lam4 = lam_in[:, :, :].rearrange("p (a b) q -> p a b q", b=2)
                    stat(dve.tensor_tensor(gated_up[:, 0, 0:2 * BQ].rearrange("p (a q) -> p a q", q=BQ),
                                           lam4[:, :, 0, :], lam4[:, :, 1, :], ALU.mult))
                    stat(dve.tensor_reduce(col(LAMP, 2), gated_up[:, 0, 0:2 * BQ].rearrange("p (a q) -> p a q", q=BQ),
                                           AX.X, ALU.add))
                    dve.wait_ge(act_stat, 4)
                    dve.scalar_tensor_tensor(out=col(NLAM), in0=col(LAME + 1), scalar=-LAMBDA_INIT, in1=col(LAME),
                                             op0=ALU.add, op1=ALU.subtract).then_inc(consts_dve, 1)
                    dve.tensor_scalar(sub_gain_scaled, sub_gain[:, :], 1.0 - LAMBDA_INIT, None, ALU.mult)\
                       .then_inc(consts_dve, 1)
                    dve.wait_ge(consts_dve, 4)
                dve.wait_ge(b_exp, 4 * (h + 1))
                dve.reciprocal(col(COEF + 4 * q, 4), col(SUM + 4 * q, 4)).then_inc(b_comb, 1)
                dve.wait_ge(b_comb, 7 * h + 5)
                lam_cols = st[:, COEF + 4 * q + 1:COEF + 4 * q + 4:2]
                dve.tensor_scalar(lam_cols, lam_cols, col(NLAM), None, ALU.mult).then_inc(b_comb, 1)
                dve.wait_ge(b_comb, 7 * h + 6)
                if h >= 2:
                    dve.wait_ge(b_turned, h - 1)
                for blk, (lo, hi) in enumerate(((0, P), (P, W3))):
                    ins = dve.tensor_scalar(prob[:, 2 * q + 1, lo:hi], prob[:, 2 * q + 1, lo:hi],
                                            col(COEF + 4 * q + 2 * blk + 1), None, ALU.mult)
                ins.then_inc(b_comb, 1)
                dve.wait_ge(b_comb, 7 * h + 7)
                for blk, (lo, hi) in enumerate(((0, P), (P, W3))):
                    ins = dve.scalar_tensor_tensor(out=diff[:, q, lo:hi], in0=prob[:, 2 * q, lo:hi],
                                                   scalar=col(COEF + 4 * q + 2 * blk), in1=prob[:, 2 * q + 1, lo:hi],
                                                   op0=ALU.mult, op1=ALU.add)
                ins.then_inc(b_diff, 1)

            def b_values(h):
                dve.wait_ge(b_ov, h + 1)
                dve.tensor_copy(o_b[:, :, h, :], bank[:, OV, (h % 2) * T:(h % 2 + 1) * T]
                                .rearrange("p (a n) -> p a n", a=TT)).then_inc(b_ov_d, 1)

            def b_norm(_):
                dve.wait_ge(b_ov_a, TT * BH)
                mean_inverse(col(MSB, TT * BH), col(SSB, TT * BH), P)
                dve.wait_ge(act_stat, 5)
                dve.wait_ge(b_ov_d, BH)
                o8 = o_b[:, :, :, :].rearrange("p a h n -> p (a h) n")
                dve.tensor_tensor(o8, o8, col(RSB, TT * BH).unsqueeze(2).to_broadcast([P, TT * BH, P]), ALU.mult)\
                   .then_inc(b_normed, 1)

            def b_done(_):
                dve.wait_ge(b_nturned, 2)
                dve.tensor_scalar(yT["B"][:, 2:4, :], bank[:, PJ, :].rearrange("p (h t) -> p h t", t=T),
                                  sub_gain_scaled, None, ALU.mult).then_inc(b_ready, 1)

            def c_scores(h):
                dve.wait_ge(c_scored, h + 1)
                if h == 0:
                    dve.wait_ge(consts_pool, 4)
                if h >= 4:
                    dve.wait_ge(c_ov, h - 3)
                dve.scalar_tensor_tensor(out=prob[:, h % 4, :], in0=bank[:, SC + h % 2, 0:W3], scalar=C_SCALE,
                                         in1=c_mask[:, :], op0=ALU.mult, op1=ALU.add).then_inc(c_z, 1)

            def c_keep(h):
                dve.wait_ge(c_abs, 3 * h + 3)
                w = diff[:, h % 2, :]
                dve.scalar_tensor_tensor(out=w, in0=prob[:, h % 4, :], scalar=0.0, in1=w,
                                         op0=ALU.max, op1=ALU.add).then_inc(c_sp, 1)

            def c_logits(h):
                dve.wait_ge(c_summed, h + 1)
                dve.tensor_tensor(prob[:, h % 4, :], prob[:, h % 4, :], bank[:, UP + h % 2, 0:W3],
                                  ALU.subtract).then_inc(c_lo, 1)

            def a_norm(_):
                dve.wait_ge(act_stat, 7)
                mean_inverse(col(MSV, TT), col(SSV, TT), AW)
                dve.wait_ge(act_stat, 8)
                for a in range(TT):
                    dve.scalar_tensor_tensor(out=va[:, a, :], in0=va[:, a, :], scalar=col(RSV + a),
                                             in1=v_gain[:, :], op0=ALU.mult, op1=ALU.mult).then_inc(a_vn, 1)

            def a_mix(_):
                dve.wait_ge(a_gelu, TT + 1)
                for a in range(TT):
                    dve.wait_ge(a_mixed, a + 1)
                    dve.tensor_tensor(uT[:, :, a * P:(a + 1) * P], uT[:, :, a * P:(a + 1) * P],
                                      bank[:, SC + a, :].rearrange("p (g t) -> p g t", t=P), ALU.mult)\
                       .then_inc(a_ready, 1)

            def u_split(r):
                if r >= 4 * len(BRANCHES):
                    return
                dve.wait_ge(*full_at(up_chunk[BRANCHES[r // 4][0]]))
                if r == 0:
                    dve.wait_ge(b_scored, BH)
                elif r == 1:
                    dve.wait_ge(b_max, BH)
                else:
                    dve.wait_ge(up_done, 2 * r - 2)
                    dve.wait_ge(u_lo_ready, r - 1)
                dve.tensor_copy(u_hi[r % 2][:, :, :], u_quarter(r)).then_inc(u_hi_ready, 1)

            def y_split(b):
                name = BRANCHES[b][0]
                if name == "B":
                    dve.wait_ge(b_ready, 2)
                    dve.wait_ge(c_scored, CH)
                elif name == "C":
                    dve.wait_ge(c_ready, CH // 2)
                else:
                    dve.wait_ge(a_ready, TT)
                dve.tensor_copy(y_hi[name][:, :, :], yT[name][:, :, :]).then_inc(y_split_done, 1)
                dve.wait_ge(y_split_done, 2 * b + 1)
                dve.tensor_tensor(y_lo[name][:, :, :], yT[name][:, :, :], y_hi[name][:, :, :].bitcast(F32),
                                  ALU.subtract).then_inc(y_split_done, 1)
                if b == 0:
                    u_split(0)
                    u_split(1)

            def gate_(b, d):
                n = KD * b + d
                if d % 2:
                    split(2 * len(PROJ) + 4 * b + d // 2 + 2)
                dve.wait_ge(pj_taken[n % 2], 8 + n // 2 + 1)
                dve.wait_ge(up_done, n + 1)
                if b == 0:
                    dve.tensor_tensor(mergedT[:, d, :], gate[:, n % 2, :], bank[:, UP + n % 2, 0:T], ALU.mult)\
                       .then_inc(up_taken, 1)
                else:
                    dve.tensor_tensor(gated_up[:, n % 2, :], gate[:, n % 2, :], bank[:, UP + n % 2, 0:T], ALU.mult)\
                       .then_inc(up_taken, 1)
                    dve.wait_ge(up_taken, n + 1)
                    if b == 2:
                        dve.wait_ge(merged, d + 1)
                    dve.tensor_tensor(mergedT[:, d, :], mergedT[:, d, :], gated_up[:, n % 2, :], ALU.add)\
                       .then_inc(merged, 1)
                if d % 2:
                    u_split(4 * b + d // 2 + 2)
                if b == 2:
                    dve.wait_ge(merged, KD + d + 1)
                    dve.tensor_copy(merged_hi(d), mergedT[:, d, :]).then_inc(merged_split, 1)
                    dve.wait_ge(merged_split, 2 * d + 1)
                    dve.tensor_tensor(merged_lo[:, d, :], mergedT[:, d, :], merged_hi(d).bitcast(F32),
                                      ALU.subtract).then_inc(merged_split, 1)

            STEPS = {"proj": lambda i: proj(*i), "ws_turn": ws_turn, "b_scores": b_scores,
                     "b_combine": b_combine, "b_values": b_values,
                     "b_norm": b_norm, "b_done": b_done, "c_scores": c_scores, "c_keep": c_keep,
                     "c_logits": c_logits, "a_norm": a_norm, "a_mix": a_mix, "y_split": y_split,
                     "gate": lambda i: gate_(*i)}
            for step, i in TIMELINE:
                if step in STEPS:
                    STEPS[step](i)

            def turned_rows(a):
                dve.wait_ge(turned2, 2 * a + 2)
                dve.tensor_copy(hT[:, 4:8, a * P:(a + 1) * P],
                                bank[:, SC + 2 * a + 1, :].rearrange("p (k t) -> p k t", t=P)).then_inc(turn2_d, 1)

            for q in range(4):
                for a in range(TT):
                    dve.wait_ge(out_done, TT * q + a + 1)
                    dve.tensor_tensor(h_sb[:, a, q * HALF:(q + 1) * HALF], h_sb[:, a, q * HALF:(q + 1) * HALF],
                                      out_view(q, a), ALU.add).then_inc(h_ready, 1)
                split(NH_IN + q + 2)
            turned_rows(0)
            dve.wait_ge(act_stat, 10)
            mean_inverse(col(MS, TT), col(SS, TT), D)
            turned_rows(1)
            dve.wait_ge(act_stat, 11)
            dve.tensor_scalar(col(NRS, TT), col(RS, TT), -1.0, None, ALU.mult).then_inc(nrs_ready, 1)
            dve.wait_ge(ld_ffn, 16)
            for a in range(TT):
                dve.scalar_tensor_tensor(out=xn[:, a, :], in0=h_sb[:, a, :], scalar=col(RS + a),
                                         in1=gain[:, :], op0=ALU.mult, op1=ALU.mult).then_inc(xn2_ready, 1)

            n_step = [0]

            def step(ins):
                n_step[0] += 1
                ins.then_inc(masked, 1)
                dve.wait_ge(masked, n_step[0])

            def r(i):
                return rt[:, i, :]

            def by_expert(ap):
                return ap.rearrange("p (a e) -> p a e", e=E)

            def by_group(ap):
                return ap.rearrange("p (g e) -> p g e", e=EG)

            def small(i, n):
                return rt[:, i, 0:n]

            def tt(o, a, b, op):
                step(dve.tensor_tensor(o, a, b, op))

            def ts(o, a, s1, s2, op0, op1=ALU.bypass):
                step(dve.tensor_scalar(o, a, s1, s2, op0, op1))

            NGT = TT * NGR
            bias2 = rbias[:, :].unsqueeze(1).to_broadcast([P, TT, E])
            dve.memset(plan_f[:, :, :], 0.0)
            dve.memset(sums[:, :, :], 0.0)
            ts(tab[:, 0:E], iota[:, 0:E], -1.0, float(E), ALU.mult, ALU.add)
            dve.wait_ge(aff_exp, TT)
            ts(r(0), r(0), 1.0, None, ALU.add)
            step(dve.reciprocal(r(1), r(0)))
            tt(by_expert(r(2)), by_expert(r(1)), bias2, ALU.add)
            s4 = by_group(r(2)).rearrange("p g (h e) -> p g h e", e=2)
            pair2 = "p (g h) -> p g h"
            most, least = (rt[:, i, 0:2 * NGT].rearrange(pair2, h=2) for i in (3, 5))
            dve.tensor_tensor(most, s4[:, :, :, 0], s4[:, :, :, 1], ALU.max)
            tt(least, s4[:, :, :, 0], s4[:, :, :, 1], ALU.min)
            dve.tensor_tensor(small(7, NGT), most[:, :, 0], most[:, :, 1], ALU.max)
            dve.tensor_tensor(small(8, NGT), most[:, :, 0], most[:, :, 1], ALU.min)
            tt(small(9, NGT), least[:, :, 0], least[:, :, 1], ALU.max)
            tt(small(8, NGT), small(8, NGT), small(9, NGT), ALU.max)
            tt(small(9, NGT), small(7, NGT), small(8, NGT), ALU.add)

            def first_of_max(oh, v, n, w, m):
                def view(ap):
                    return ap.rearrange("p (a e) -> p a e", e=n)

                def wide(ap):
                    return ap.unsqueeze(2).to_broadcast([P, TT, n])
                step(dve.tensor_reduce(m, view(v), AX.X, ALU.max))
                tt(view(w), view(v), wide(m), ALU.is_equal)
                tt(view(w), view(w), tab[:, 0:n].unsqueeze(1).to_broadcast([P, TT, n]), ALU.mult)
                step(dve.tensor_reduce(m, view(w), AX.X, ALU.max))
                tt(view(oh), view(w), wide(m), ALU.is_equal)

            first_of_max(small(10, NGT), small(9, NGT), NGR, small(11, NGT), small(12, TT))
            ts(small(11, NGT), small(10, NGT), -MASKED, MASKED, ALU.mult, ALU.add)
            tt(by_group(r(2)), by_group(r(2)), small(11, NGT).unsqueeze(2).to_broadcast([P, NGT, EG]), ALU.add)
            first_of_max(r(13), r(2), E, r(14), small(12, TT))
            step(dve.scalar_tensor_tensor(out=r(2), in0=r(13), scalar=2 * MASKED, in1=r(2),
                                          op0=ALU.mult, op1=ALU.add))
            first_of_max(r(15), r(2), E, r(14), small(12, TT))
            tt(r(13), r(13), r(15), ALU.add)
            dve.tensor_tensor(r(14), r(13), r(1), ALU.mult).then_inc(chosen_ready, 1)
            dve.wait_ge(chosen_ready, 1)
            step(dve.tensor_reduce(small(12, TT), by_expert(r(14)), AX.X, ALU.add))
            step(dve.reciprocal(small(16, TT), small(12, TT)))
            pair_order = "p (a q e) -> p a q e"
            dst17 = rt[:, 17, :].rearrange("p (q a e) -> p a q e", a=TT, e=2)
            dst18 = rt[:, 18, :].rearrange("p (q a e) -> p a q e", a=TT, e=2)
            for a in range(TT):
                ts(dst17[:, a], r(14).rearrange(pair_order, a=TT, e=2)[:, a], rt[:, 16, a:a + 1], None, ALU.mult)
            dve.wait_ge(pos_done, 1)
            tt(r(19), bank[:, SC, 0:TT * E], r(13), ALU.mult)
            for a in range(TT):
                step(dve.scalar_tensor_tensor(out=dst18[:, a], in0=r(19).rearrange(pair_order, a=TT, e=2)[:, a],
                                              scalar=-1.0, in1=r(13).rearrange(pair_order, a=TT, e=2)[:, a],
                                              op0=ALU.add, op1=ALU.add))

            def pick(row, pair):
                cols = slice(0, 4) if pair is None else bass.ds(pair * 4, 4)
                return rt[:, row, cols].unsqueeze(2).to_broadcast([P, 4, J])

            sel4 = sel.rearrange("p (a j) -> p a j", j=J)
            gated4 = gated.rearrange("p (a j) -> p a j", j=J)

            def select(pair, nth):
                cols = iota[:, 0:J] if nth is None else iota[:, bass.ds(nth * J, J)]
                dve.tensor_tensor(sel4, cols.unsqueeze(1).to_broadcast([P, 4, J]), pick(18, pair), ALU.is_equal)\
                   .then_inc(sel_ready, 1)

            def gate_rows(pair, m):
                dve.wait_ge(sel_ready, m + 2)
                dve.tensor_tensor(gated4, sel4, pick(17, pair), ALU.mult).then_inc(gated_ready, 1)

            def gathered_rows(n):
                dve.wait_ge(gathered, 2 * n + 3)
                dve.tensor_copy(xgT[:, 4:8, :], bank[:, 5, :].rearrange("p (k j) -> p k j", j=2 * J))\
                   .then_inc(xg_d, 1)

            most = tab[:, 0:PAIRS]
            step(dve.tensor_reduce(most, bank[:, SC + 1, 0:E].rearrange("p (q e) -> p q e", e=2), AX.X, ALU.max))
            select(None, None)
            gate_rows(None, 0)
            NP = PASSES + 1
            full = work[:, 5504:5504 + 3 * PAIRS].rearrange("p (q c) -> p q c", c=3)
            over = work[:, 5536:5536 + NP * PAIRS].rearrange("p (n q) -> p n q", q=PAIRS)
            weighed = work[:, 5536 + NP * PAIRS:5536 + 2 * NP * PAIRS].rearrange("p (n q) -> p n q", q=PAIRS)
            tt(full, most.unsqueeze(2).to_broadcast([P, PAIRS, 3]),
               iota[:, J:T:J].unsqueeze(1).to_broadcast([P, PAIRS, 3]), ALU.is_gt)
            extra = sums[:, 0, PAIRS:2 * PAIRS]
            step(dve.tensor_reduce(extra, full, AX.X, ALU.add))
            for i, shift in enumerate((1, 2, 4)):
                src = sums[:, i, :]
                dst = sums[:, i + 1, PAIRS:] if i < 2 else plan_f[:, UP_TO, 0:PAIRS]
                tt(dst, src[:, PAIRS:], src[:, PAIRS - shift:2 * PAIRS - shift], ALU.add)
            up_to = plan_f[:, UP_TO, 0:PAIRS]
            dve.tensor_copy(plan_f[:, W1_FIRST, 1:PAIRS], extra[:, 1:PAIRS]).then_inc(masked, 1)
            dve.memset(plan_f[:, W1_FIRST, 0:1], 1.0).then_inc(masked, 1)
            n_step[0] += 2
            tt(up_to, up_to, iota[:, 1:1 + PAIRS], ALU.add)
            tt(over, iota[:, 0:NP].unsqueeze(2).to_broadcast([P, NP, PAIRS]),
               up_to.unsqueeze(1).to_broadcast([P, NP, PAIRS]), ALU.is_ge)
            pair_row, odd_row, nth_row = (plan_f[:, i, :] for i in (PAIR, ODD, NTH))
            dve.tensor_reduce(pair_row, over, AX.X, ALU.add).then_inc(masked, 1)
            n_step[0] += 1
            dve.tensor_reduce(odd_row, over[:, :, 1::2], AX.X, ALU.add).then_inc(masked, 1)
            n_step[0] += 1
            tt(weighed, over, extra.unsqueeze(1).to_broadcast([P, NP, PAIRS]), ALU.mult)
            step(dve.tensor_reduce(nth_row, weighed, AX.X, ALU.add))
            tt(nth_row, nth_row, pair_row, ALU.add)
            dve.tensor_tensor(nth_row, iota[:, 0:NP], nth_row, ALU.subtract).then_inc(masked, 1)
            n_step[0] += 1
            dve.scalar_tensor_tensor(out=odd_row, in0=odd_row, scalar=-2.0, in1=pair_row,
                                     op0=ALU.mult, op1=ALU.add).then_inc(masked, 1)
            n_step[0] += 1
            ts(pair_row, pair_row, float(PAIRS - 1), None, ALU.min)
            dve.tensor_copy(plan[0:1, :, :], plan_f[0:1, :, :]).then_inc(planned, 1)
            gathered_rows(0)

            def expert_pass(n):
                pair = planned_value(dve, PAIR, n + 1, 0, PAIRS - 1)
                nth = planned_value(dve, NTH, n + 1, 0, T // J)
                dve.wait_ge(gt_turned, n + 2)
                dve.wait_ge(gated_ready, n + 2)
                select(pair, nth)
                gate_rows(pair, n + 1)
                dve.wait_ge(silu_ready, n + 2)
                dve.wait_ge(gt_ready, n + 2)
                dve.wait_ge(w3_done, n + 2)
                dve.scalar_tensor_tensor(out=he, in0=bank[:, 7, :], scalar=gate_col[:, :], in1=silu,
                                         op0=ALU.mult, op1=ALU.mult).then_inc(he_ready, 1)
                for b in range(2):
                    dve.wait_ge(ye_a, 2 * n + 2 + b)
                    cols = slice(b * 512, (b + 1) * 512)
                    dve.tensor_tensor(ye_lo[:, cols], bank[:, 7 - b, :], ye_hi[:, cols].bitcast(F32),
                                      ALU.subtract).then_inc(ye_d, 1)
                gathered_rows(n + 1)

            all_passes(dve, expert_pass)

            for a in range(TT):
                dve.wait_ge(act_stat, 12 + a)
                mean_inverse(col(MS + a), col(SS + a), D)
            dve.wait_ge(ld_final, 16)
            for a in range(TT):
                dve.wait_ge(act_stat, 14 + a)
                dve.scalar_tensor_tensor(out=xn[:, a, :].rearrange("p (b n) -> p b n", b=2), in0=bank[:, a:4:2, :],
                                         scalar=col(RS + a), in1=gain[:, :].rearrange("p (b n) -> p b n", b=2),
                                         op0=ALU.mult, op1=ALU.mult).then_inc(rows_ready, 1)

        @block.tensor
        def _(pe):
            pe.wait_ge(ident_ready, 1)
            for a in range(TT):
                pe.wait_ge(xn_ready, a + 1)
                for k in range(KD):
                    ins = pe.transpose(bank[:, SC + k // 2, (k % 2) * T + a * P:(k % 2) * T + (a + 1) * P],
                                       xn[:, a, k * P:(k + 1) * P], ident[:, :])
                    if a and k % 2:
                        ins.then_inc(turned, 1)
            pe.wait_ge(turn_taken_a, 4)

            def ws_turn(_):
                pe.wait_ge(ws_masked, 1)
                pe.wait_ge(turn_taken_d, 4)
                for g in range(NG):
                    ins = pe.transpose(bank[:, TR, g * P:(g + 1) * P], ws[:, g, :], ident[:, :])
                ins.then_inc(ws_turned, 1)

            def products(dst, q, tiles, stationary_x):
                b = q % 2
                parts = ((w_hi[b], x_hi), (w_hi[b], x_lo), (w_lo[b], x_hi))
                for part, (w, xp) in enumerate(parts):
                    if q == 0 and part == 1:
                        pe.wait_ge(turn_taken_d, 4)
                    if part == 2:
                        pe.wait_ge(w_lo_ready, q + 1)
                    for i, m in enumerate(tiles):
                        for k in range(KD):
                            lhsT, rhs = ((xp[:, k, m * P:(m + 1) * P], w[:, k, :]) if stationary_x else
                                         (w[:, k, m * P:(m + 1) * P], xp[:, k, :]))
                            ins = pe.matmul(dst[:, i * T:(i + 1) * T], lhsT, rhs, start=(part + i + k == 0),
                                            stop=(part == 2 and k == KD - 1), skip_group_check=True)
                return ins

            def proj(c, half):
                q = 2 * c + half
                pe.wait_ge(w_hi_ready, q + 1)
                if c:
                    pe.wait_ge(pj_taken[half], c)
                if (c, half) == (7, 0):
                    pe.wait_ge(b_ready, 2)
                products(bank[:, PJ + half, :], q, (0, 1), PROJ[c] in (VA, VB, VC)).then_inc(proj_done, 1)

            def b_scores(h):
                if h == 0:
                    pe.wait_ge(pj_taken[0], 2)
                    pe.wait_ge(pj_taken[1], 2)
                else:
                    pe.wait_ge(b_max, h)
                for block in range(TT):
                    for m in range(2):
                        rows = slice(m * BQ, (m + 1) * BQ)
                        if block == 0:
                            pe.matmul(bank[:, SC + m, 0:P], qbT[rows, h, 0:P], kbT[rows, h, 0:P], start=True, stop=True)
                        else:
                            ins = pe.matmul(bank[:, SC + m, P:W3], qbT[rows, h, P:T], kbT[rows, h, :],
                                            start=True, stop=True)
                ins.then_inc(b_scored, 1)

            def b_turn(h):
                pe.wait_ge(b_diff, h + 1)
                if h == 0:
                    pe.wait_ge(wsT_ready, 1)
                if h >= 1:
                    pe.wait_ge(b_turn_taken, h)
                for i in range(3):
                    ins = pe.transpose(bank[:, TR, i * P:(i + 1) * P], diff[:, h % 2, i * P:(i + 1) * P], ident[:, :])
                ins.then_inc(b_turned, 1)

            def b_values(h):
                pe.wait_ge(b_turn_taken, h + 1)
                if h == 0:
                    pe.wait_ge(pj_taken[0], 3)
                    pe.wait_ge(pj_taken[1], 3)
                if h >= 1:
                    pe.wait_ge(b_ov_d, h)
                o, e = (h % 2) * T, slice(h * P, (h + 1) * P)
                pe.matmul(bank[:, OV, o:o + P], diffT[:, h % 2, 0:P], vb[:, 0, e], start=True, stop=True)
                pe.matmul(bank[:, OV, o + P:o + T], diffT[:, h % 2, P:2 * P], vb[:, 0, e], start=True, stop=False)
                pe.matmul(bank[:, OV, o + P:o + T], diffT[:, h % 2, 2 * P:W3], vb[:, 1, e], start=False, stop=True)\
                  .then_inc(b_ov, 1)

            def b_done(_):
                pe.wait_ge(b_normed, 1)
                pe.wait_ge(b_turn_taken, BH)
                pe.wait_ge(pj_taken[0], 7)
                for b, first in ((TR, 0), (PJ, 2)):
                    for i in range(4):
                        h, a = first + i // 2, i % 2
                        ins = pe.transpose(bank[:, b, i * P:(i + 1) * P], o_b[:, a, h, :], ident[:, :])
                    ins.then_inc(b_nturned, 1)

            def c_scores(h):
                if h == 0:
                    pe.wait_ge(pj_taken[0], 5)
                    pe.wait_ge(pj_taken[1], 5)
                    pe.wait_ge(b_max, BH)
                if h % 2:
                    return
                if h >= 2:
                    pe.wait_ge(c_z, h)
                t = h // 2
                for block in range(TT):
                    for m in range(2):
                        rows = slice(m * CD, (m + 1) * CD)
                        if block == 0:
                            pe.matmul(bank[:, SC + m, 0:T], kcT[rows, t, 0:P], qcT[rows, t, :], start=True, stop=True)
                        else:
                            pe.matmul(bank[:, SC + m, T:W3], kcT[rows, t, P:T], qcT[rows, t, P:T],
                                      start=True, stop=True).then_inc(c_scored, 1)

            def c_sums(h):
                pe.wait_ge(c_sp, h + 1)
                if h == 0:
                    pe.wait_ge(consts_pool, 4)
                if h >= 2:
                    pe.wait_ge(c_lo, h - 1)
                w, b = diff[:, h % 2, :], bank[:, UP + h % 2, :]
                pe.matmul(b[:, 0:W3], from_here[:, :], w, start=True, stop=False, skip_group_check=True)
                pe.matmul(b[:, P:T], ones[:, :], w[:, T:W3], start=False, stop=True, skip_group_check=True)\
                  .then_inc(c_summed, 1)

            def c_values(h):
                pe.wait_ge(c_prob, h + 1)
                if h == 0:
                    pe.wait_ge(pj_taken[0], 6)
                    pe.wait_ge(pj_taken[1], 6)
                if h >= 2 and h % 2 == 0:
                    pe.wait_ge(c_ready, h // 2)
                rows, t = slice((h % 2) * CD, (h % 2 + 1) * CD), h // 2
                o = (t % 2) * T
                a, v = prob[:, h % 4, :], slice(h * CD, (h + 1) * CD)
                pe.matmul(bank[rows, OV, o:o + T], vc[:, 0, v], a[:, 0:T], start=True, stop=False,
                          skip_group_check=True)
                pe.matmul(bank[rows, OV, o + P:o + T], vc[:, 1, v], a[:, T:W3], start=False, stop=True,
                          skip_group_check=True).then_inc(c_ov, 1)

            def a_mix(_):
                pe.wait_ge(a_vn, TT)
                pe.wait_ge(c_z, CH)
                for a in range(TT):
                    for g in range(NG):
                        dst = bank[:, SC + a, g * P:(g + 1) * P]
                        pe.matmul(dst, va[:, a, g * P:(g + 1) * P], wsT[:, g, :], start=True, stop=False)
                        ins = pe.matmul(dst, ones[0:1, :], b_row[0:1, g * P:(g + 1) * P], start=False, stop=True)
                    ins.then_inc(a_mixed, 1)

            def gate_(b, d):
                name = BRANCHES[b][0]
                n = KD * b + d
                q = 2 * len(PROJ) + 4 * b + d // 2
                pe.wait_ge(w_hi_ready, q + 1)
                pe.wait_ge(pj_taken[n % 2], 8 + n // 2)
                products(bank[:, PJ + n % 2, 0:T], q, (d % 2,), False).then_inc(proj_done, 1)
                if d == 0:
                    pe.wait_ge(y_split_done, 2 * b + 2)
                r = 4 * b + d // 2
                pe.wait_ge(u_hi_ready, r + 1)
                pe.wait_ge(u_lo_ready, r + 1)
                if n < 2:
                    pe.wait_ge(c_lo, CH - 1 + n)
                else:
                    pe.wait_ge(up_taken, n - 1)
                parts = ((u_hi[r % 2], y_hi[name]), (u_hi[r % 2], y_lo[name]), (u_lo[r % 2], y_hi[name]))
                for part, (w, y) in enumerate(parts):
                    for k in range(4):
                        ins = pe.matmul(bank[:, UP + n % 2, 0:T], w[:, k, (d % 2) * P:(d % 2 + 1) * P], y[:, k, :],
                                        start=(part + k == 0), stop=(part == 2 and k == 3))
                ins.then_inc(up_done, 1)

            STEPS = {"proj": lambda i: proj(*i), "ws_turn": ws_turn, "b_scores": b_scores, "b_turn": b_turn,
                     "b_values": b_values, "b_done": b_done, "c_scores": c_scores, "c_sums": c_sums, "c_values": c_values,
                     "a_mix": a_mix, "gate": lambda i: gate_(*i)}
            for step, i in TIMELINE:
                if step in STEPS:
                    STEPS[step](i)

            def turn_rows(a):
                pe.wait_ge(h_ready, 7 + a)
                for b in range(2):
                    for i in range(4):
                        k = 4 * b + i
                        ins = pe.transpose(bank[:, SC + 2 * a + b, i * P:(i + 1) * P],
                                           h_sb[:, a, k * P:(k + 1) * P], ident[:, :])
                    ins.then_inc(turned2, 1)

            pe.wait_ge(pj_taken[0], 8 + 3 * KD // 2)
            pe.wait_ge(pj_taken[1], 8 + 3 * KD // 2)
            pe.wait_ge(a_ready, TT)
            for q in range(4):
                if q == 1:
                    pe.wait_ge(up_taken, 3 * KD)
                w = q % 2
                pe.wait_ge(w_hi_ready, NH_IN + q + 1)
                pe.wait_ge(w_lo_ready, NH_IN + q + 1)
                for a in range(TT):
                    rows = slice(a * P, (a + 1) * P)
                    for k in range(KD):
                        if q == 0 and a == 0:
                            pe.wait_ge(merged_split, 2 * k + 2)
                        hi, lo = merged_hi(k)[:, rows], merged_lo[:, k, rows]
                        for part, (mp, wp) in enumerate(((hi, w_hi[w]), (lo, w_hi[w]), (hi, w_lo[w]))):
                            ins = pe.matmul(out_view(q, a), mp, wp[:, k, :],
                                            start=(k + part == 0), stop=(k == KD - 1 and part == 2))
                    ins.then_inc(out_done, 1)
            turn_rows(0)
            turn_rows(1)
            pe.wait_ge(rw_scaled, 1)
            for a in range(TT):
                pe.wait_ge(turn2_a, a + 1)
                pe.wait_ge(turn2_d, a + 1)
                for k in range(KD):
                    ins = pe.matmul(bank[:, SC, a * E:(a + 1) * E], hT[:, k, a * P:(a + 1) * P], rw[:, k, :],
                                    start=(k == 0), stop=(k == KD - 1))
            ins.then_inc(routed, 1)

            def sums_start(banks):
                for b in banks:
                    pe.matmul(bank[:, b, :], ident[:, :], h_sb[:, b % 2, b // 2 * CW:(b // 2 + 1) * CW],
                              start=True, stop=True)

            sums_start(range(3))
            pe.wait_ge(chosen_ready, 1)
            chosen = rt[:, 13, :]
            pe.matmul(bank[:, SC, 0:2 * E], before[:, :], chosen, start=True, stop=False, skip_group_check=True)
            pe.matmul(bank[:, SC, E:2 * E], ones[:, :], chosen[:, 0:E], start=False, stop=True, skip_group_check=True)
            pe.matmul(bank[:, SC + 1, 0:E], ones[:, :], chosen[:, 0:E], start=True, stop=False)
            pe.matmul(bank[:, SC + 1, 0:E], ones[:, :], chosen[:, E:2 * E], start=False, stop=True)\
              .then_inc(pos_done, 1)
            sums_start(range(3, 4))

            def gather(b, ks):
                for k in ks:
                    for a in range(TT):
                        ins = pe.matmul(bank[:, 4 + b, k * P:(k + 1) * P],
                                        xn[:, a, (4 * b + k) * P:(4 * b + k + 1) * P],
                                        sel[:, a * 2 * J:(a + 1) * 2 * J], start=(a == 0), stop=(a == TT - 1))
                if ks[-1] == 3:
                    ins.then_inc(gathered, 1)

            def two_experts(dst, lhsT, rhs, tiles, second_half=()):
                for k in range(tiles):
                    if k == 4:
                        for wait in second_half:
                            pe.wait_ge(*wait)
                    for e in range(2):
                        last = pe.matmul(bank[e * J:(e + 1) * J, dst, :], lhsT[:, k, e * J:(e + 1) * J],
                                         rhs[e][:, k, :], start=(k == 0), stop=(k == tiles - 1))
                return last

            def landed(slots, loads):
                for j in slots:
                    pe.wait_ge(slot_full[j], loads + 16 * before_experts(j))

            def matrices(slots, k):
                return [ring[:, j, :].rearrange("p (k n) -> p k n", k=k) for j in slots]

            def expert_pass(n):
                pair = planned_value(pe, PAIR, n, 0, PAIRS - 1)
                odd = planned_value(pe, ODD, n, 0, 1)
                pe.wait_ge(xg_a, n + 2)
                pe.wait_ge(ye_d, 2 * n + 1)
                with pe.If(odd > 0):
                    landed(W1_SLOTS[1], pair * 8 + 8)
                    two_experts(6, xgT, matrices(W1_SLOTS[1], KD), KD, [(xg_d, n + 2)]).then_inc(w1_done, 1)
                with pe.Else():
                    landed(W1_SLOTS[0], pair * 8 + 16)
                    two_experts(6, xgT, matrices(W1_SLOTS[0], KD), KD, [(xg_d, n + 2)]).then_inc(w1_done, 1)
                pe.wait_ge(gated_ready, n + 2)
                for a in range(TT):
                    pe.transpose(bank[:, 4, a * P:(a + 1) * P], sel[:, a * 2 * J:(a + 1) * 2 * J], ident[:, :])
                for a in range(TT):
                    ins = pe.matmul(bank[:, 4, T:T + 1], gated[:, a * 2 * J:(a + 1) * 2 * J], ones[:, 0:1],
                                    start=(a == 0), stop=(a == TT - 1))
                ins.then_inc(gt_turned, 1)
                for top in w3_top:
                    pe.wait_ge(top, pair * 16 + 16)
                two_experts(7, xgT, matrices(W3_SLOTS, KD), KD,
                            [(slot_full[j], pair * 16 + 16 + 16 * before_experts(j)) for j in W3_SLOTS])\
                    .then_inc(w3_done, 1)
                pe.wait_ge(gt_ready, n + 2)
                pe.wait_ge(sel_ready, n + 3)
                gather(0, (0, 1))
                pe.wait_ge(he_ready, n + 2)
                for f in range(KF):
                    ins = pe.transpose(bank[:, 6, f * P:(f + 1) * P], he[:, f * P:(f + 1) * P], ident[:, :])
                ins.then_inc(he_turned, 1)
                gather(0, (2, 3))
                pe.wait_ge(heT_ready, n + 2)
                for left in w2_left:
                    pe.wait_ge(left, pair * 16 + 16)
                w2 = matrices(W2_SLOTS, KF)
                for b in range(2):
                    if b:
                        landed(W2_SLOTS, pair * 16 + 16)
                    two_experts(7 - b, heT, [w[:, :, b * 512:(b + 1) * 512] for w in w2], KF).then_inc(y_done, 1)
                for b in range(2):
                    for ready, y in ((ye_a, ye_hi), (ye_d, ye_lo)):
                        if b and y is ye_lo:
                            gather(1, range(4))
                        pe.wait_ge(ready, 2 * n + 2 + b)
                        for a in range(TT):
                            pe.matmul(bank[:, 2 * b + a, :], selT[:, a * P:(a + 1) * P],
                                      y[:, b * 512:(b + 1) * 512], start=False, stop=False,
                                      skip_group_check=True)

            pe.wait_ge(sel_ready, 2)
            gather(0, range(4))
            gather(1, range(4))
            all_passes(pe, expert_pass)
            pe.matmul(bank[:, 4, 0:P], ident[:, :], ident[:, :], start=True, stop=True).then_inc(finished, 1)


_INS = ["x", "norm_mix_gain", "w_in", "gmlp_w_s", "gmlp_b_s", "gmlp_v_gain", "diff_lambda", "diff_subln_gain",
        "w_up_a", "w_up_b", "w_up_c", "w_out", "norm_ffn_gain", "router_w", "router_bias",
        "moe_w1", "moe_w3", "moe_w2", "final_gain"]


def kernel(**inputs):
    import numpy as np
    import concourse.bacc as bacc
    from concourse.bass_utils import run_bass_kernel_spmd as run

    nc = bacc.Bacc("TRN2", target_bir_lowering=False, num_devices=1)
    arrays, args = {}, []
    for name in _INS:
        a = np.ascontiguousarray(inputs[name])
        arrays["in_" + name] = a
        args.append(nc.dram_tensor("in_" + name, a.shape, mybir.dt.from_np(a.dtype), kind="ExternalInput").ap())
    args.append(nc.dram_tensor("out_0", inputs["x"].shape, F32, kind="ExternalOutput").ap())
    trunk(nc, *args)
    r = run(nc, [arrays], core_ids=[0])
    return r.results[0]["out_0"]
```
